# Optimizing a Trainium2 kernel written in Bass

```python
import math
import jax, jax.numpy as jnp
from jax import lax
import numpy as np

D_MODEL = 1024
BATCH = 1
SEQ = 512
DEPTH = 2

D_MIX = D_MODEL
HEAD_DIM = 64
D_SC = D_MIX // 4
D_ATT = D_MIX // 2
D_CC = D_MIX // 4
N_Q_HEADS = D_ATT // HEAD_DIM
N_KV_HEADS = 2
GQA_GROUP = N_Q_HEADS // N_KV_HEADS
SC_WIDTH = 3
CC_WIDTH = 31
WINDOW = 128
BLOCK = 128
ROPE_THETA = 10000.0
D_FF = 2816
LN_EPS = 1e-5
ALPHA = (2.0 * DEPTH) ** 0.25
BETA = (8.0 * DEPTH) ** -0.25
IN_SIZES = (D_SC, D_SC, D_SC, N_Q_HEADS * HEAD_DIM, N_KV_HEADS * HEAD_DIM, N_KV_HEADS * HEAD_DIM, D_CC, D_CC)
D_IN = sum(IN_SIZES)
IN_OFFSETS = tuple(int(v) for v in np.cumsum(IN_SIZES)[:-1])


def layer_norm(x, g, b):
    xf = x.astype(jnp.float32)
    mu = jnp.mean(xf, axis=-1, keepdims=True)
    var = jnp.mean(jnp.square(xf - mu), axis=-1, keepdims=True)
    y = (xf - mu) * lax.rsqrt(var + LN_EPS)
    return (y * g.astype(jnp.float32) + b.astype(jnp.float32)).astype(x.dtype)

def swiglu(x, w_gu, w_down):
    g, u = jnp.split(x @ w_gu, 2, axis=-1)
    return (jax.nn.silu(g) * u) @ w_down

def depthwise_conv(x, w):
    k = w.shape[0]
    pad = (k - 1) // 2
    return lax.conv_general_dilated(
        x, w[:, None, :].astype(x.dtype), window_strides=(1,), padding=[(pad, pad)],
        dimension_numbers=("NWC", "WIO", "NWC"), feature_group_count=x.shape[-1])

def rope(x, positions):
    half = HEAD_DIM // 2
    inv_freq = ROPE_THETA ** (-jnp.arange(half, dtype=jnp.float32) / half)
    ang = positions.astype(jnp.float32)[:, None] * inv_freq[None, :]
    cos = jnp.cos(ang)[None, :, None, :]
    sin = jnp.sin(ang)[None, :, None, :]
    xf = x.astype(jnp.float32)
    x1, x2 = xf[..., :half], xf[..., half:]
    return jnp.concatenate([x1 * cos - x2 * sin, x2 * cos + x1 * sin], axis=-1).astype(x.dtype)

def banded_window_attention(q, k, v, sink):
    b, s = q.shape[0], q.shape[1]
    nb = s // BLOCK
    qb = q.reshape(b, nb, BLOCK, N_KV_HEADS, GQA_GROUP, HEAD_DIM)

    def band(t):
        tp = jnp.pad(t, ((0, 0), (BLOCK, BLOCK), (0, 0), (0, 0)))
        parts = [tp[:, o * BLOCK:o * BLOCK + s].reshape(b, nb, BLOCK, N_KV_HEADS, HEAD_DIM) for o in range(3)]
        return jnp.concatenate(parts, axis=2)

    kb, vb = band(k), band(v)
    scores = jnp.einsum("bnqkgd,bnskd->bnkgqs", qb, kb).astype(jnp.float32) * (HEAD_DIM ** -0.5)
    qpos = jnp.arange(s).reshape(nb, BLOCK)
    kpos = jnp.arange(nb)[:, None] * BLOCK - BLOCK + jnp.arange(3 * BLOCK)[None, :]
    valid = (jnp.abs(qpos[:, :, None] - kpos[:, None, :]) <= WINDOW) \
        & (kpos >= 0)[:, None, :] & (kpos < s)[:, None, :]
    scores = jnp.where(valid[None, :, None, None], scores, -1e30)
    sink_f = sink.astype(jnp.float32).reshape(N_KV_HEADS, GQA_GROUP)[None, None, :, :, None]
    m = jnp.maximum(jnp.max(scores, axis=-1), sink_f)
    p = jnp.exp(scores - m[..., None])
    denom = jnp.sum(p, axis=-1) + jnp.exp(sink_f - m)
    o = jnp.einsum("bnkgqs,bnskd->bnqkgd", p.astype(v.dtype), vb).astype(jnp.float32)
    o = o / jnp.transpose(denom, (0, 1, 4, 2, 3))[..., None]
    return o.reshape(b, s, D_ATT).astype(q.dtype)

def hybrid_mixer(x, w_in, sc_conv_w, attn_sink, cc_conv_w, cc_conv_b, cc_ln_g, cc_ln_b, w_out):
    b, s, _ = x.shape
    positions = jnp.arange(s)
    z = x @ w_in
    sc_b, sc_c, sc_h, q, k, v, cc_a, cc_gate = jnp.split(z, IN_OFFSETS, axis=-1)
    y_sc = sc_b * depthwise_conv(sc_c * sc_h, sc_conv_w)
    q = rope(q.reshape(b, s, N_Q_HEADS, HEAD_DIM), positions)
    k = rope(k.reshape(b, s, N_KV_HEADS, HEAD_DIM), positions)
    v = v.reshape(b, s, N_KV_HEADS, HEAD_DIM)
    y_att = banded_window_attention(q, k, v, attn_sink)
    u = cc_a * jax.nn.sigmoid(cc_gate)
    u = depthwise_conv(u, cc_conv_w) + cc_conv_b
    y_cc = jax.nn.silu(layer_norm(u, cc_ln_g, cc_ln_b))
    return jnp.concatenate([y_sc, y_att, y_cc], axis=-1) @ w_out

def first_inputs(seed: int = 0) -> dict:
    key = jax.random.key(seed)
    ks = jax.random.split(key, 24)
    f32 = jnp.float32

    def nrm(k, shape, scale):
        return jax.random.normal(k, shape, f32) * scale

    def gain(k, n):
        return 1.0 + 0.02 * jax.random.normal(k, (DEPTH, n), f32)

    return {
        "x": jax.random.normal(ks[0], (BATCH, SEQ, D_MODEL), f32),
        "ffn1_w_gu": nrm(ks[1], (DEPTH, D_MODEL, 2 * D_FF), D_MODEL ** -0.5),
        "ffn1_w_down": nrm(ks[2], (DEPTH, D_FF, D_MODEL), BETA * D_FF ** -0.5),
        "ln1_g": gain(ks[3], D_MODEL),
        "ln1_b": nrm(ks[4], (DEPTH, D_MODEL), 0.02),
        "w_in": nrm(ks[5], (DEPTH, D_MODEL, D_IN), D_MODEL ** -0.5),
        "sc_conv_w": nrm(ks[6], (DEPTH, SC_WIDTH, D_SC), SC_WIDTH ** -0.5),
        "attn_sink": nrm(ks[7], (DEPTH, N_Q_HEADS), 0.5),
        "cc_conv_w": nrm(ks[8], (DEPTH, CC_WIDTH, D_CC), CC_WIDTH ** -0.5),
        "cc_conv_b": nrm(ks[9], (DEPTH, D_CC), 0.02),
        "cc_ln_g": gain(ks[10], D_CC),
        "cc_ln_b": nrm(ks[11], (DEPTH, D_CC), 0.02),
        "w_out": nrm(ks[12], (DEPTH, D_MIX, D_MODEL), BETA * D_MIX ** -0.5),
        "ln2_g": gain(ks[13], D_MODEL),
        "ln2_b": nrm(ks[14], (DEPTH, D_MODEL), 0.02),
        "ffn2_w_gu": nrm(ks[15], (DEPTH, D_MODEL, 2 * D_FF), D_MODEL ** -0.5),
        "ffn2_w_down": nrm(ks[16], (DEPTH, D_FF, D_MODEL), BETA * D_FF ** -0.5),
        "ln3_g": gain(ks[17], D_MODEL),
        "ln3_b": nrm(ks[18], (DEPTH, D_MODEL), 0.02),
    }

def first_block(x, ffn1_w_gu, ffn1_w_down, ln1_g, ln1_b, w_in, sc_conv_w, attn_sink, cc_conv_w,
              cc_conv_b, cc_ln_g, cc_ln_b, w_out, ln2_g, ln2_b, ffn2_w_gu, ffn2_w_down, ln3_g, ln3_b):
    for l in range(DEPTH):
        x = layer_norm(ALPHA * x + 0.5 * swiglu(x, ffn1_w_gu[l], ffn1_w_down[l]), ln1_g[l], ln1_b[l])
        x = layer_norm(ALPHA * x + hybrid_mixer(x, w_in[l], sc_conv_w[l], attn_sink[l], cc_conv_w[l],
                                                 cc_conv_b[l], cc_ln_g[l], cc_ln_b[l], w_out[l]),
                       ln2_g[l], ln2_b[l])
        x = layer_norm(ALPHA * x + 0.5 * swiglu(x, ffn2_w_gu[l], ffn2_w_down[l]), ln3_g[l], ln3_b[l])
    return x


MEM_LEN = 256
EPS = 1e-6
MIX_WIDTH = D_MODEL
ML_HEADS = 4
ML_WIDTH = MIX_WIDTH // 2
ML_HD = ML_WIDTH // ML_HEADS
ML_CHUNK = 64
RG_WIDTH = MIX_WIDTH - ML_WIDTH
RG_BLOCKS = 4
RG_BW = RG_WIDTH // RG_BLOCKS
RG_CONV = 4
RG_C = 8.0
IN_COLS = 4 * ML_WIDTH + 2 * ML_HEADS + 2 * RG_WIDTH
SW_HEADS = 16
SW_KV_HEADS = 4
SW_HD = D_MODEL // SW_HEADS
SW_GROUP = SW_HEADS // SW_KV_HEADS
SW_WINDOW = 128
SW_BLOCK = 128
QKV_COLS = (SW_HEADS + 2 * SW_KV_HEADS) * SW_HD
X_HEADS = 4
X_HD = D_MODEL // X_HEADS
D_FF_2 = 4 * D_MODEL
N_EVEN = (DEPTH + 1) // 2
N_ODD = DEPTH // 2


def rms_norm(x, g):
    xf = x.astype(jnp.float32)
    y = xf * lax.rsqrt(jnp.mean(xf * xf, axis=-1, keepdims=True) + EPS)
    return (y * g.astype(jnp.float32)).astype(x.dtype)

def rotary(t, positions):
    d = t.shape[-1]
    half = d // 2
    inv = jnp.power(ROPE_THETA, -jnp.arange(half, dtype=jnp.float32) * 2.0 / d)
    ang = positions.astype(jnp.float32)[..., None] * inv
    cos = jnp.cos(ang)[:, :, None, :]
    sin = jnp.sin(ang)[:, :, None, :]
    t1 = t[..., :half].astype(jnp.float32)
    t2 = t[..., half:].astype(jnp.float32)
    return jnp.concatenate([t1 * cos - t2 * sin, t2 * cos + t1 * sin], axis=-1).astype(t.dtype)

def mlstm_chunkwise(q, k, v, i_pre, f_pre):
    B, S, H, dh = q.shape
    nc = S // ML_CHUNK
    f32 = jnp.float32

    def to_chunks(t):
        t = t.astype(f32).reshape((B, nc, ML_CHUNK) + t.shape[2:])
        return jnp.moveaxis(t, (1, 3), (0, 2))

    qc = to_chunks(q)
    kc = to_chunks(k) * (dh ** -0.5)
    vc = to_chunks(v)
    logi = to_chunks(i_pre)
    logf = to_chunks(jax.nn.log_sigmoid(f_pre.astype(f32)))
    causal = jnp.tril(jnp.ones((ML_CHUNK, ML_CHUNK), dtype=bool))

    def step(carry, inp):
        C, n, m = carry
        qb, kb, vb, li, lf = inp
        b = jnp.cumsum(lf, axis=-1)
        dmat = b[..., :, None] - b[..., None, :] + li[..., None, :]
        dmat = jnp.where(causal, dmat, -jnp.inf)
        m_t = jnp.maximum(b + m[..., None], jnp.max(dmat, axis=-1))
        decay_prev = jnp.exp(b + m[..., None] - m_t)
        s = jnp.einsum('bhtd,bhsd->bhts', qb, kb) * jnp.exp(dmat - m_t[..., None])
        num = jnp.einsum('bhts,bhsd->bhtd', s, vb) + decay_prev[..., None] * jnp.einsum('bhtd,bhde->bhte', qb, C)
        den = jnp.sum(s, axis=-1) + decay_prev * jnp.einsum('bhtd,bhd->bht', qb, n)
        h = num / jnp.maximum(jnp.abs(den), jnp.exp(-m_t))[..., None]
        b_last = b[..., -1]
        g = b_last[..., None] - b + li
        m_new = jnp.maximum(b_last + m, jnp.max(g, axis=-1))
        w_prev = jnp.exp(b_last + m - m_new)
        w_s = jnp.exp(g - m_new[..., None])
        C_new = w_prev[..., None, None] * C + jnp.einsum('bhs,bhsd,bhse->bhde', w_s, kb, vb)
        n_new = w_prev[..., None] * n + jnp.einsum('bhs,bhsd->bhd', w_s, kb)
        return (C_new, n_new, m_new), h

    init = (jnp.zeros((B, H, dh, dh), f32), jnp.zeros((B, H, dh), f32), jnp.zeros((B, H), f32))
    _, hs = lax.scan(step, init, (qc, kc, vc, logi, logf))
    hs = jnp.moveaxis(hs, (0, 2), (1, 3))
    return hs.reshape(B, S, H * dh)

def rg_lru_branch(rx, conv_w, conv_b, rg_wa, rg_ba, rg_wx, rg_bx, rg_lambda):
    B, S, _ = rx.shape
    xc = lax.conv_general_dilated(rx, conv_w[:, None, :], window_strides=(1,),
                                  padding=[(RG_CONV - 1, 0)],
                                  dimension_numbers=('NWC', 'WIO', 'NWC'),
                                  feature_group_count=RG_WIDTH) + conv_b
    xb = xc.reshape(B, S, RG_BLOCKS, RG_BW)
    r = jax.nn.sigmoid((jnp.einsum('bsnc,ncd->bsnd', xb, rg_wa).reshape(B, S, RG_WIDTH) + rg_ba).astype(jnp.float32))
    i = jax.nn.sigmoid((jnp.einsum('bsnc,ncd->bsnd', xb, rg_wx).reshape(B, S, RG_WIDTH) + rg_bx).astype(jnp.float32))
    log_a = -RG_C * r * jax.nn.softplus(-rg_lambda.astype(jnp.float32))
    a = jnp.exp(log_a)
    u = jnp.sqrt(-jnp.expm1(2.0 * log_a)) * (i * xc.astype(jnp.float32))

    def combine(e1, e2):
        a1, b1 = e1
        a2, b2 = e2
        return a1 * a2, a2 * b1 + b2

    _, h = lax.associative_scan(combine, (a, u), axis=1)
    return h

def mlstm_rglru_mixer(u, w_in, b_if, conv_w, conv_b, rg_wa, rg_ba, rg_wx, rg_bx, rg_lambda, w_out):
    B, S, _ = u.shape
    z = u @ w_in
    q, k, v, o, gif, rx, ry = jnp.split(z, [ML_WIDTH, 2 * ML_WIDTH, 3 * ML_WIDTH, 4 * ML_WIDTH,
                                            4 * ML_WIDTH + 2 * ML_HEADS,
                                            4 * ML_WIDTH + 2 * ML_HEADS + RG_WIDTH], axis=-1)
    gif = gif + b_if
    i_pre, f_pre = gif[..., :ML_HEADS], gif[..., ML_HEADS:]
    hm = mlstm_chunkwise(q.reshape(B, S, ML_HEADS, ML_HD), k.reshape(B, S, ML_HEADS, ML_HD),
                         v.reshape(B, S, ML_HEADS, ML_HD), i_pre, f_pre)
    y_a = jax.nn.sigmoid(o) * hm.astype(u.dtype)
    h_rg = rg_lru_branch(rx, conv_w, conv_b, rg_wa, rg_ba, rg_wx, rg_bx, rg_lambda)
    y_b = jax.nn.gelu(ry) * h_rg.astype(u.dtype)
    return jnp.concatenate([y_a, y_b], axis=-1) @ w_out

def sliding_window_sink_attention(u, positions, w_qkv, sinks, w_o):
    B, S, _ = u.shape
    qkv = u @ w_qkv
    q, k, v = jnp.split(qkv, [SW_HEADS * SW_HD, (SW_HEADS + SW_KV_HEADS) * SW_HD], axis=-1)
    q = rotary(q.reshape(B, S, SW_HEADS, SW_HD), positions).reshape(B, S, SW_KV_HEADS, SW_GROUP, SW_HD)
    k = rotary(k.reshape(B, S, SW_KV_HEADS, SW_HD), positions)
    v = v.reshape(B, S, SW_KV_HEADS, SW_HD)
    pad = ((0, 0), (SW_BLOCK, 0), (0, 0), (0, 0))
    kp = jnp.pad(k, pad)
    vp = jnp.pad(v, pad)
    nb = S // SW_BLOCK
    r = jnp.arange(SW_BLOCK)[:, None]
    c = jnp.arange(2 * SW_BLOCK)[None, :]
    diff = r + SW_BLOCK - c
    band = (diff >= 0) & (diff < SW_WINDOW)
    sink = sinks.astype(jnp.float32).reshape(SW_KV_HEADS, SW_GROUP)[None, :, :, None]
    scale = SW_HD ** -0.5

    def block(j):
        start = j * SW_BLOCK
        qb = lax.dynamic_slice_in_dim(q, start, SW_BLOCK, axis=1)
        kb = lax.dynamic_slice_in_dim(kp, start, 2 * SW_BLOCK, axis=1)
        vb = lax.dynamic_slice_in_dim(vp, start, 2 * SW_BLOCK, axis=1)
        s = jnp.einsum('blkgd,bckd->bkglc', qb, kb).astype(jnp.float32) * scale
        valid = band & (start + c - SW_BLOCK >= 0)
        s = jnp.where(valid, s, -jnp.inf)
        m = jnp.maximum(jnp.max(s, axis=-1), sink)
        p = jnp.exp(s - m[..., None])
        den = jnp.sum(p, axis=-1) + jnp.exp(sink - m)
        ob = jnp.einsum('bkglc,bckd->blkgd', p, vb.astype(jnp.float32))
        ob = ob / jnp.moveaxis(den, -1, 1)[..., None]
        return ob.astype(u.dtype)

    out = lax.map(block, jnp.arange(nb))
    out = jnp.moveaxis(out, 0, 1).reshape(B, S, SW_HEADS * SW_HD)
    return out @ w_o

def memory_cross_attention(u, mem, g_mem, w_q, w_kv, w_o):
    B, S, _ = u.shape
    M = mem.shape[1]
    q = (u @ w_q).reshape(B, S, X_HEADS, X_HD)
    kv = (rms_norm(mem, g_mem) @ w_kv).reshape(B, M, 2, X_HEADS, X_HD)
    k, v = kv[:, :, 0], kv[:, :, 1]
    s = jnp.einsum('bshd,bmhd->bhsm', q, k).astype(jnp.float32) * (X_HD ** -0.5)
    p = jax.nn.softmax(s, axis=-1)
    o = jnp.einsum('bhsm,bmhd->bshd', p.astype(v.dtype), v).reshape(B, S, D_MODEL)
    return o @ w_o

def squared_relu_mlp(u, w1, w2):
    return jnp.square(jax.nn.relu(u @ w1)) @ w2

def second_inputs(seed: int = 0) -> dict:
    key = jax.random.key(seed)
    ks = iter(jax.random.split(key, 40))

    def nrm(shape, scale):
        return jax.random.normal(next(ks), shape, jnp.float32) * scale

    def gains(n):
        return 1.0 + nrm((n, D_MODEL), 0.02)

    x = nrm((BATCH, SEQ, D_MODEL), 1.0)
    mem = nrm((BATCH, MEM_LEN, D_MODEL), 1.0)
    positions = jnp.broadcast_to(jnp.arange(SEQ, dtype=jnp.int32)[None, :], (BATCH, SEQ))
    ev_w_in = nrm((N_EVEN, D_MODEL, IN_COLS), D_MODEL ** -0.5)
    ev_b_if = jnp.concatenate([nrm((N_EVEN, ML_HEADS), 0.1),
                               jnp.linspace(3.0, 6.0, ML_HEADS)[None, :] + nrm((N_EVEN, ML_HEADS), 0.01)], axis=-1)
    ev_conv_w = nrm((N_EVEN, RG_CONV, RG_WIDTH), RG_CONV ** -0.5)
    ev_conv_b = nrm((N_EVEN, RG_WIDTH), 0.01)
    ev_rg_wa = nrm((N_EVEN, RG_BLOCKS, RG_BW, RG_BW), RG_BW ** -0.5)
    ev_rg_ba = nrm((N_EVEN, RG_WIDTH), 0.01)
    ev_rg_wx = nrm((N_EVEN, RG_BLOCKS, RG_BW, RG_BW), RG_BW ** -0.5)
    ev_rg_bx = nrm((N_EVEN, RG_WIDTH), 0.01)
    a_c = jax.random.uniform(next(ks), (N_EVEN, RG_WIDTH), jnp.float32, 0.9, 0.999)
    a_base = a_c ** (1.0 / RG_C)
    ev_rg_lambda = jnp.log(a_base) - jnp.log1p(-a_base)
    ev_w_out = nrm((N_EVEN, MIX_WIDTH, D_MODEL), MIX_WIDTH ** -0.5)
    od_w_qkv = nrm((N_ODD, D_MODEL, QKV_COLS), D_MODEL ** -0.5)
    od_sinks = nrm((N_ODD, SW_HEADS), 1.0)
    od_w_o = nrm((N_ODD, SW_HEADS * SW_HD, D_MODEL), (SW_HEADS * SW_HD) ** -0.5)
    return {
        'x': x, 'mem': mem, 'positions': positions,
        'ev_w_in': ev_w_in, 'ev_b_if': ev_b_if, 'ev_conv_w': ev_conv_w, 'ev_conv_b': ev_conv_b,
        'ev_rg_wa': ev_rg_wa, 'ev_rg_ba': ev_rg_ba, 'ev_rg_wx': ev_rg_wx, 'ev_rg_bx': ev_rg_bx,
        'ev_rg_lambda': ev_rg_lambda, 'ev_w_out': ev_w_out,
        'od_w_qkv': od_w_qkv, 'od_sinks': od_sinks, 'od_w_o': od_w_o,
        'g_mix_pre': gains(DEPTH), 'g_mix_post': gains(DEPTH),
        'g_x_pre': gains(DEPTH), 'g_x_post': gains(DEPTH), 'g_mem': gains(DEPTH),
        'w_xq': nrm((DEPTH, D_MODEL, D_MODEL), D_MODEL ** -0.5),
        'w_xkv': nrm((DEPTH, D_MODEL, 2 * D_MODEL), D_MODEL ** -0.5),
        'w_xo': nrm((DEPTH, D_MODEL, D_MODEL), D_MODEL ** -0.5),
        'g_ff_pre': gains(DEPTH), 'g_ff_post': gains(DEPTH),
        'w_ff1': nrm((DEPTH, D_MODEL, D_FF_2), D_MODEL ** -0.5),
        'w_ff2': nrm((DEPTH, D_FF_2, D_MODEL), D_FF_2 ** -0.5),
    }

def second_block(x, mem, positions, ev_w_in, ev_b_if, ev_conv_w, ev_conv_b, ev_rg_wa, ev_rg_ba,
              ev_rg_wx, ev_rg_bx, ev_rg_lambda, ev_w_out, od_w_qkv, od_sinks, od_w_o,
              g_mix_pre, g_mix_post, g_x_pre, g_x_post, g_mem, w_xq, w_xkv, w_xo,
              g_ff_pre, g_ff_post, w_ff1, w_ff2):
    h = x
    for l in range(DEPTH):
        u = rms_norm(h, g_mix_pre[l])
        if l % 2 == 0:
            e = l // 2
            u = mlstm_rglru_mixer(u, ev_w_in[e], ev_b_if[e], ev_conv_w[e], ev_conv_b[e],
                                  ev_rg_wa[e], ev_rg_ba[e], ev_rg_wx[e], ev_rg_bx[e],
                                  ev_rg_lambda[e], ev_w_out[e])
        else:
            o = l // 2
            u = sliding_window_sink_attention(u, positions, od_w_qkv[o], od_sinks[o], od_w_o[o])
        h = h + rms_norm(u, g_mix_post[l])
        u = memory_cross_attention(rms_norm(h, g_x_pre[l]), mem, g_mem[l], w_xq[l], w_xkv[l], w_xo[l])
        h = h + rms_norm(u, g_x_post[l])
        u = squared_relu_mlp(rms_norm(h, g_ff_pre[l]), w_ff1[l], w_ff2[l])
        h = h + rms_norm(u, g_ff_post[l])
    return h


def setup_inputs(seed=0):
    out = dict(first_inputs(seed))
    for name, value in second_inputs(seed + 1).items():
        if name != "x":
            out[name + "_2"] = value
    return out


def reference(
    x, ffn1_w_gu, ffn1_w_down, ln1_g, ln1_b, w_in, sc_conv_w, attn_sink, cc_conv_w, cc_conv_b,
    cc_ln_g, cc_ln_b, w_out, ln2_g, ln2_b, ffn2_w_gu, ffn2_w_down, ln3_g, ln3_b, mem_2,
    positions_2, ev_w_in_2, ev_b_if_2, ev_conv_w_2, ev_conv_b_2, ev_rg_wa_2, ev_rg_ba_2,
    ev_rg_wx_2, ev_rg_bx_2, ev_rg_lambda_2, ev_w_out_2, od_w_qkv_2, od_sinks_2, od_w_o_2,
    g_mix_pre_2, g_mix_post_2, g_x_pre_2, g_x_post_2, g_mem_2, w_xq_2, w_xkv_2, w_xo_2,
    g_ff_pre_2, g_ff_post_2, w_ff1_2, w_ff2_2,
):
    x = first_block(
        x, ffn1_w_gu, ffn1_w_down, ln1_g, ln1_b, w_in, sc_conv_w, attn_sink, cc_conv_w,
        cc_conv_b, cc_ln_g, cc_ln_b, w_out, ln2_g, ln2_b, ffn2_w_gu, ffn2_w_down, ln3_g, ln3_b,
    )
    return second_block(
        x, mem_2, positions_2, ev_w_in_2, ev_b_if_2, ev_conv_w_2, ev_conv_b_2, ev_rg_wa_2,
        ev_rg_ba_2, ev_rg_wx_2, ev_rg_bx_2, ev_rg_lambda_2, ev_w_out_2, od_w_qkv_2, od_sinks_2,
        od_w_o_2, g_mix_pre_2, g_mix_post_2, g_x_pre_2, g_x_post_2, g_mem_2, w_xq_2, w_xkv_2,
        w_xo_2, g_ff_pre_2, g_ff_post_2, w_ff1_2, w_ff2_2,
    )


_drawn_inputs = setup_inputs


def setup_inputs(seed=0):
    import zlib

    import numpy as np

    out = dict(_drawn_inputs(seed))
    spreads = {}
    factors = {'attn_sink': 8.0,
     'ev_conv_b_2': 2.675,
     'ev_rg_ba_2': 34.715,
     'ev_rg_bx_2': 8.0,
     'od_sinks_2': 2.948,
     'g_mix_post_2': 3.426,
     'g_x_pre_2': 4.019,
     'g_x_post_2': 9.208,
     'g_ff_pre_2': 14.373,
     'g_ff_post_2': 15.449}
    for name, (base, spread) in spreads.items():
        noise = np.random.default_rng([zlib.crc32(name.encode()), seed]).standard_normal(out[name].shape)
        drawn = base * np.exp(spread * noise) if base else spread * noise
        out[name] = __import__('jax').numpy.asarray(drawn.astype(out[name].dtype))
    for name, factor in factors.items():
        out[name] = (out[name] * factor).astype(out[name].dtype)
    return out
```

```python
import math
from contextlib import ExitStack

import numpy as np
import concourse.bass as bass
from concourse import mybir

F32 = mybir.dt.float32
F32R = mybir.dt.float32r
I32 = mybir.dt.int32
ALU = mybir.AluOpType
ACT = mybir.ActivationFunctionType
AX = mybir.AxisListType.X

P = 128
T = 512
D = 1024
KD = 8
NB = 4
ALPHA = float(4.0 ** 0.25)
LN_EPS = 1e-5
RMS_EPS = 1e-6
NEG = -1e30
FF1 = 2816
FF2 = 4096

RAW = 4
SPL = 3
NTMP = 12

C_ID = 0
C_ONE = 128
C_COS = 256
C_SIN = 768
C_M1 = 1280
C_M2 = 1664
C_CAUSAL = 1920
C_SEL = 2048
C_INV = 2560
C_EPS = 2561
C_SINK = 2564
C_W = 2608

VEC_SIZES = [("ln1_g", 16), ("ln1_b", 16), ("ln2_g", 16), ("ln2_b", 16), ("ln3_g", 16), ("ln3_b", 16),
             ("sc_conv_w", 12), ("cc_conv_w", 124), ("cc_conv_b", 4), ("cc_ln_g", 4), ("cc_ln_b", 4),
             ("g_mix_pre_2", 16), ("g_mix_post_2", 16), ("g_x_pre_2", 16), ("g_x_post_2", 16), ("g_mem_2", 16),
             ("g_ff_pre_2", 16), ("g_ff_post_2", 16), ("ev_conv_w_2", 16), ("ev_conv_b_2", 4),
             ("ev_rg_ba_2", 4), ("ev_rg_bx_2", 4), ("ev_rg_lambda_2", 4)]
V_OFF = {}
V_W = 0
for _n, _s in VEC_SIZES:
    V_OFF[_n] = V_W
    V_W += _s
V_BI = V_W
V_W += 2


class Ring:

    def __init__(self, items):
        self.q = [(i, ()) for i in items]

    def take(self):
        return self.q.pop(0)

    def give(self, item, *toks):
        self.q.append((item, toks))


def build(nc, d, units_in):
    units = []
    es = ExitStack()
    with es:
        def sb(name, shape, dt=F32):
            return es.enter_context(nc.sbuf_tensor(name, shape, dt))

        XR = sb("XR", [P, KD, T])
        XH = sb("XH", [P, KD, T], F32R)
        XL = sb("XL", [P, KD, T], F32R)
        Y = sb("Y", [P, KD, T])
        HHa = sb("HHa", [P, KD, T], F32R)
        HLa = sb("HLa", [P, KD, T], F32R)
        with nc.sbuf_tensor("HHb", [P, KD, T], F32R) as HHb, nc.sbuf_tensor("HLb", [P, KD, T], F32R) as HLb:
            pass
        M0 = sb("M0", [P, KD, T])
        M1 = sb("M1", [P, KD, T])
        raw = [sb(f"raw{i}", [P, KD, P]) for i in range(RAW)]
        wh = [sb(f"wh{i}", [P, KD, P], F32R) for i in range(SPL)]
        wl = [sb(f"wl{i}", [P, KD, P], F32R) for i in range(SPL)]
        tmps = [sb(f"tmp{i}", [P, T]) for i in range(NTMP)]
        CT = sb("CT", [P, C_W])
        VT = sb("VT", [P, V_W])
        sm = sb("sm", [P, 128])
        banks = [es.enter_context(nc.psum_tensor(f"ps{i}", [P, T], F32)) for i in range(8)]

        sems = {}

        def sem(name):
            if name not in sems:
                sems[name] = es.enter_context(nc.semaphore(name))
            return sems[name]

        for n in ("pe", "act", "dve", "pool", "ld", "ct", "mm", "out", "rga", "rgb", "pos"):
            sem(n)
        for i in range(RAW):
            sem(f"w{i}")

        Q = {e: [] for e in ("pe", "act", "dve", "pool", "sp")}
        cnt = {e: 0 for e in Q}

        def flat(ts):
            for t in ts:
                if not t:
                    continue
                if isinstance(t[0], str):
                    yield t
                else:
                    yield from flat(t)

        def op(e, fn, *after):
            cnt[e] += 1
            Q[e].append((fn, list(flat(after)), True))
            return (e, cnt[e])

        def quiet(e, fn, *after):
            Q[e].append((fn, list(flat(after)), False))

        def dve(fn, *a):
            return op("dve", fn, *a)

        def act(fn, *a):
            return op("act", fn, *a)

        def pool(fn, *a):
            return op("pool", fn, *a)

        dma_n = {}

        def dma(name, out, src, *after):
            dma_n[name] = dma_n.get(name, 0) + 16
            s = sem(name)
            quiet("sp", lambda e: e.dma_start(out, src).then_inc(s, 16), *after)
            return (name, dma_n[name])

        psum = Ring(banks)
        tmp = Ring(tmps)

        def copy(out, in_):
            return lambda e: e.activation(out, in_, ACT.Copy)

        def vcopy(out, in_):
            return lambda e: e.tensor_copy(out, in_)

        def func(out, in_, f, **kw):
            return lambda e: e.activation(out, in_, f, **kw)

        def tt(out, a, b, o):
            return lambda e: e.tensor_tensor(out, a, b, o)

        def ts(out, a, s1, s2, o0, o1=None):
            if o1 is None:
                return lambda e: e.tensor_scalar(out, a, s1, None, o0)
            return lambda e: e.tensor_scalar(out, a, s1, s2, o0, o1)

        def stt(out, a, s, b, o0, o1):
            return lambda e: e.scalar_tensor_tensor(out=out, in0=a, scalar=s, in1=b, op0=o0, op1=o1)

        def f32(ap):
            return ap.bitcast(F32)

        raw_free = [()] * RAW
        spl_free = [()] * SPL
        loaded, split_at, ptr = [], [], [0]

        def load_unit(i):
            name, l, k0, nk, c0 = units_in[i]
            s = i % RAW
            src = d[name][l][k0 * P:(k0 + nk) * P, c0:c0 + P].rearrange("(k p) c -> p k c", p=P)
            loaded.append(dma(f"w{s}", raw[s][:, 0:nk, :], src, raw_free[s]))

        def split_unit(i):
            nk = units_in[i][3]
            r, s = i % RAW, i % SPL
            hi = act(copy(wh[s][:, 0:nk, :], raw[r][:, 0:nk, :]), loaded[i], spl_free[s])
            lo = dve(tt(wl[s][:, 0:nk, :], raw[r][:, 0:nk, :], f32(wh[s][:, 0:nk, :]), ALU.subtract), hi)
            raw_free[r] = lo
            split_at.append(lo)

        def next_unit(w, c0, k0=0, nk=KD):
            i = ptr[0]
            ptr[0] += 1
            if units_in is None:
                units.append((*w, k0, nk, c0))
                return i % SPL, ("dve", 1)
            n = len(units_in)
            while len(split_at) < min(n, i + SPL):
                while len(loaded) < min(n, len(split_at) + RAW):
                    load_unit(len(loaded))
                split_unit(len(split_at))
            while len(loaded) < min(n, len(split_at) + RAW):
                load_unit(len(loaded))
            return i % SPL, split_at[i]

        def mm3(out, lh, ll, rh, rl, start, stop):
            def f(e):
                e.matmul(out, lh, rh, start=start, stop=False)
                e.matmul(out, lh, rl, start=False, stop=False)
                return e.matmul(out, ll, rh, start=False, stop=stop)
            return f

        def project(w, c0, xs, k0=0):
            nk = len(xs)
            s, ready = next_unit(w, c0, k0, nk)
            bank, free = psum.take()
            n = xs[0][0].shape[-1]
            for k, (h, l, tok) in enumerate(xs):
                f = mm3(bank[:, 0:n], wh[s][:, k, :], wl[s][:, k, :], h, l, k == 0, k == nk - 1)
                a = (ready, free, tok) if k == 0 else (tok,)
                if k < nk - 1:
                    quiet("pe", f, *a)
                else:
                    done = op("pe", f, *a)
            spl_free[s] = done
            return bank, done

        def split(hi, lo, src, *after):
            a = act(copy(hi, src), *after)
            return dve(tt(lo, src, f32(hi), ALU.subtract), a)

        t_ct = [dma("ct", CT[:, :], d["consts"]), dma("ct", VT[:, :], d["vecs"])][-1]
        t_x = dma("ld", XR[:, :, :], d["xT"].rearrange("(k p) t -> p k t", p=P))
        ident = CT[:, C_ID:C_ID + P]
        ones = CT[:, C_ONE:C_ONE + P]
        COS = CT[:, C_COS:C_COS + T]
        SIN = CT[:, C_SIN:C_SIN + T]
        M1m = CT[:, C_M1:C_M1 + 384]
        M2m = CT[:, C_M2:C_M2 + 256]
        CAU = CT[:, C_CAUSAL:C_CAUSAL + P]

        def eps(v):
            c = {LN_EPS: C_EPS, RMS_EPS: C_EPS + 1}[v]
            return CT[:, c:c + 1]

        def vec(name, i):
            return VT[:, V_OFF[name] + i:V_OFF[name] + i + 1]

        for e in ("pe", "act", "dve", "pool"):
            Q[e].append((None, [t_ct], False))

        xr_tok = [t_x] * KD
        x_free = [()] * KD
        xs = [None] * KD

        def split_x(k, src, *after):
            t = split(XH[:, k, :], XL[:, k, :], src, x_free[k], *after)
            xs[k] = (XH[:, k, :], XL[:, k, :], t)
            return t

        for k in range(KD):
            split_x(k, XR[:, k, :], t_x)

        hid = [(HHa[:, i, :], HLa[:, i, :]) for i in range(KD)] + [(HHb[:, i, :], HLb[:, i, :]) for i in range(KD)]
        hid_free = [()] * 16
        m_last = [()]

        def rstd_of(bank, tok, n, e):
            sd, f1 = tmp.take()
            w = bank.shape[-1]
            a = act(func(sd[:, 0:w], bank, ACT.Sqrt, bias=eps(e), scale=1.0 / n), tok, f1)
            rr, f2 = tmp.take()
            r = dve(lambda v: v.reciprocal(rr[:, 0:w], sd[:, 0:w]), a, f2)
            tmp.give(sd, r)
            return rr, r, a

        def colsum(srcs):
            bank, free = psum.take()
            n = len(srcs)
            for i, (ap, tok) in enumerate(srcs):
                w = ap.shape[-1]
                t = op("pe", lambda e, ap=ap, i=i, w=w: e.matmul(bank[:, 0:w], ones, ap, start=i == 0,
                                                                   stop=i == n - 1), tok, free if i == 0 else ())
            return bank, t

        def sumsq(srcs):
            bank, free = psum.take()
            n = len(srcs)
            reads = []
            for i, (ap, tok) in enumerate(srcs):
                q, f = tmp.take()
                w = ap.shape[-1]
                a = act(func(q[:, 0:w], ap, ACT.Square), tok, f)
                reads.append(a)
                t = op("pe", lambda e, q=q, i=i, w=w: e.matmul(bank[:, 0:w], ones, q[:, 0:w], start=i == 0,
                                                              stop=i == n - 1), a, free if i == 0 else ())
                tmp.give(q, t)
            return bank, t, reads

        def layer_norm(tiles, g, b, outs):
            n = len(tiles) * P
            bank, t = colsum(tiles)
            cen = []
            for ap, tok in tiles:
                c = dve(stt(ap, bank[:, :], -1.0 / n, ap, ALU.mult, ALU.add), t, tok)
                cen.append((ap, c))
            psum.give(bank, c)
            vb, t, _ = sumsq(cen)
            rr, r, a = rstd_of(vb[:, :], t, n, LN_EPS)
            psum.give(vb, a)
            for m, (ap, c) in enumerate(cen):
                s = dve(stt(ap, ap, g(m), rr[:, :], ALU.mult, ALU.mult), r, t)
                outs(m, ap, s)
            tmp.give(rr, s)

        def block_norm(l, which):
            g = lambda m: vec(f"{which}_g", l * KD + m)
            b = lambda m: vec(f"{which}_b", l * KD + m)

            def out(m, ap, s):
                xr_tok[m] = act(func(ap, ap, ACT.Identity, bias=b(m)), s)
                split_x(m, ap, xr_tok[m])
                xr_tok[m] = xs[m][2]

            layer_norm([(XR[:, m, :], xr_tok[m]) for m in range(KD)], g, b, out)

        def pre_norm(name, l):
            bank, t, _ = sumsq([(XR[:, m, :], xr_tok[m]) for m in range(KD)])
            rr, r, a = rstd_of(bank[:, :], t, D, RMS_EPS)
            psum.give(bank, a)
            for m in range(KD):
                q, f = tmp.take()
                s = dve(stt(q[:, :], XR[:, m, :], vec(name, l * KD + m), rr[:, :], ALU.mult, ALU.mult), r, f, xr_tok[m])
                t = split_x(m, q[:, :], s)
                tmp.give(q, t)
            tmp.give(rr, s)

        y_free = [()]

        def post_norm(name, l, ys):
            bank, t, _ = sumsq([(Y[:, m, :], ys[m]) for m in range(KD)])
            rr, r, a = rstd_of(bank[:, :], t, D, RMS_EPS)
            psum.give(bank, a)
            for m in range(KD):
                s = dve(stt(Y[:, m, :], Y[:, m, :], vec(name, l * KD + m), rr[:, :], ALU.mult, ALU.mult), r, t, ys[m])
                xr_tok[m] = dve(tt(XR[:, m, :], XR[:, m, :], Y[:, m, :], ALU.add), s, xr_tok[m])
            tmp.give(rr, s)
            y_free[0] = xr_tok[KD - 1]

        def ffn(w_up, w_down, nf, gated, take):
            chunks = [range(c, min(c + KD, nf)) for c in range(0, nf, KD)]
            ready = [None] * nf
            last_up = None

            def up(c):
                for j in chunks[c]:
                    s = (c % 2) * KD + j % KD
                    hi, lo = hid[s]
                    h, f2 = tmp.take()
                    q, f1 = tmp.take()
                    if gated:
                        gb, gt = project(w_up, j * P, xs)
                        a = act(func(q[:, :], gb[:, :], ACT.Silu), gt, f1)
                        psum.give(gb, a)
                        ub, ut = project(w_up, nf * P + j * P, xs)
                        v = dve(stt(h[:, :], q[:, :], 0.5, ub[:, :], ALU.mult, ALU.mult), a, ut, f2)
                    else:
                        ub, ut = project(w_up, j * P, xs)
                        a = act(func(q[:, :], ub[:, :], ACT.Relu), ut, f1)
                        v = dve(tt(h[:, :], q[:, :], ub[:, :], ALU.mult), a, f2)
                    psum.give(ub, v)
                    tmp.give(q, v)
                    ready[j] = split(hi, lo, h[:, :], v, hid_free[s])
                    tmp.give(h, ready[j])
                for k in range(KD):
                    x_free[k] = ut

            def down(c):
                src = [hid[(c % 2) * KD + j % KD] + (ready[j],) for j in chunks[c]]
                for m in range(KD):
                    bank, t = project(w_down, m * P, src, k0=chunks[c][0])
                    psum.give(bank, take(m, bank, t, c == 0))
                for j in chunks[c]:
                    hid_free[(c % 2) * KD + j % KD] = t

            for c in range(len(chunks)):
                up(c)
                if c:
                    down(c - 1)
            down(len(chunks) - 1)

        def add_residual(m, bank, t, first):
            if first:
                xr_tok[m] = dve(stt(XR[:, m, :], XR[:, m, :], ALPHA, bank[:, :], ALU.mult, ALU.add), t, xr_tok[m])
            else:
                xr_tok[m] = dve(tt(XR[:, m, :], XR[:, m, :], bank[:, :], ALU.add), t, xr_tok[m])
            return xr_tok[m]

        ys = [None] * KD

        def to_y(m, bank, t, first):
            if first:
                ys[m] = dve(vcopy(Y[:, m, :], bank[:, :]), t, y_free[0])
            else:
                ys[m] = dve(tt(Y[:, m, :], Y[:, m, :], bank[:, :], ALU.add), t, ys[m])
            return ys[m]

        def x_used(t):
            for k in range(KD):
                x_free[k] = t

        def rope(bank, tok, scale, outs, *free):
            a_, f1 = tmp.take()
            b_, f2 = tmp.take()
            c1 = dve(stt(a_[:, :], bank[:, :], scale, COS, ALU.mult, ALU.mult), tok, f1)
            for q in range(4):
                o = 32 * q
                i = 32 * (q ^ 1)
                c2 = dve(stt(b_[o:o + 32, :], bank[i:i + 32, :], scale, SIN[i:i + 32, :], ALU.mult, ALU.mult), tok, f2)
            psum.give(bank, c2)
            for ap, p0, n in outs:
                t = dve(tt(ap, a_[p0:p0 + n, :], b_[p0:p0 + n, :], ALU.add), c1, c2, *free)
            tmp.give(a_, t)
            tmp.give(b_, t)
            return t

        def value_rows(bank, tok, out, *free):
            q, f = tmp.take()
            a = act(copy(q[:, :], bank[:, :]), tok, f)
            psum.give(bank, a)
            vb, vf = psum.take()
            for b in range(NB):
                t = op("pe", lambda e, b=b: e.transpose(vb[:, b * P:(b + 1) * P], q[:, b * P:(b + 1) * P], ident),
                       a, vf)
            tmp.give(q, t)
            v = dve(vcopy(out, vb[:, :].rearrange("p (b c) -> p b c", b=NB)), t, *free)
            psum.give(vb, v)
            return v

        sm_ring = Ring([sm[:, 8 * i:8 * i + 8] for i in range(12)])

        def attention(heads, blocks, mask, sink, outs, done, fill=None):
            jobs = [(h, b) for h in range(len(heads)) for b in range(NB)]
            st = [None] * len(jobs)
            obank = {}

            def score(n):
                h, b = jobs[n]
                q, k, v, tile, p0, tok = heads[h]
                k0, nk, c0 = blocks(b)
                w = nk * P
                bank, f = psum.take()
                t = op("pe", lambda e: e.matmul(bank[:, 0:w], q[:, b * P:(b + 1) * P], k[:, k0 * P:k0 * P + w],
                                                start=True, stop=True), f, tok)
                s, sf = tmp.take()
                c, cf = sm_ring.take()
                r = dve(lambda e: e.tensor_tensor_reduce(s[:, 0:w], bank[:, 0:w], mask[:, c0:c0 + w], 1.0, -3e38,
                                                         ALU.add, ALU.max, c[:, 0:1]), t, sf, cf)
                psum.give(bank, r)
                m = dve(ts(c[:, 1:2], c[:, 0:1], sink(h), -1.0, ALU.max, ALU.mult), r)
                x = act(lambda e: e.activation(s[:, 0:w], s[:, 0:w], ACT.Exp, bias=c[:, 1:2], accum_out=c[:, 2:3]), m)
                z = act(func(c[:, 3:4], sink(h), ACT.Exp, bias=c[:, 1:2]), m)
                d1 = dve(tt(c[:, 4:5], c[:, 2:3], c[:, 3:4], ALU.add), x, z)
                d2 = dve(lambda e: e.reciprocal(c[:, 5:6], c[:, 4:5]), d1)
                nrm = dve(ts(s[:, 0:w], s[:, 0:w], c[:, 5:6], None, ALU.mult), d2)
                sm_ring.give(c, nrm)
                st[n] = (s, nrm)

            def turn(n):
                h, b = jobs[n]
                k0, nk, c0 = blocks(b)
                s, tok = st[n]
                bank, f = psum.take()
                for i in range(nk):
                    t = op("pe", lambda e, i=i: e.transpose(bank[:, i * P:(i + 1) * P], s[:, i * P:(i + 1) * P], ident),
                           tok, f)
                tmp.give(s, t)
                pt, pf = tmp.take()
                c = act(copy(pt[:, 0:nk * P], bank[:, 0:nk * P]), t, pf)
                psum.give(bank, c)
                st[n] = (pt, c)

            def value(n):
                h, b = jobs[n]
                q, k, v, tile, p0, tok = heads[h]
                k0, nk, c0 = blocks(b)
                pt, tok = st[n]
                if tile not in obank:
                    obank[tile] = psum.take()
                bank, f = obank[tile]
                for i in range(nk):
                    t = op("pe", lambda e, i=i: e.matmul(bank[p0:p0 + 64, b * P:(b + 1) * P], v(k0 + i),
                                                         pt[:, i * P:(i + 1) * P], start=i == 0, stop=i == nk - 1),
                           tok, f)
                tmp.give(pt, t)
                if b == NB - 1 and (h == len(heads) - 1 or heads[h + 1][3] != tile):
                    psum.give(bank, outs(tile, bank, t))
                done[0] = t

            for n in range(len(jobs) + 2):
                if n < len(jobs):
                    score(n)
                if 1 <= n <= len(jobs):
                    turn(n - 1)
                if n >= 2:
                    value(n - 2)
                if fill:
                    fill(n)

        def to_hidden(tile0):
            def outs(tile, bank, t):
                s = tile0 + tile
                hi, lo = hid[s]
                r = split(hi, lo, bank[:, :], t, hid_free[s])
                hs[s] = (hi, lo, r)
                return r
            return outs

        hs = [None] * KD

        def out_project(w, take):
            for m in range(KD):
                bank, t = project(w, m * P, hs)
                psum.give(bank, take(m, bank, t, True))
            for s in range(KD):
                hid_free[s] = t

        def m_enter():
            return [hid_free[s] for s in range(KD, 16)] + list(m_last)

        def m_leave(*toks):
            for s in range(KD, 16):
                hid_free[s] = toks
            m_last[0] = toks

        def conv(acc, src, taps, pad, bias, tok, *free):
            n, f = taps
            order = [pad] + [j for j in range(n) if j != pad]
            t = None
            for j in order:
                s = j - pad
                lo, hi = max(0, -s), min(T, T - s)
                o, i = acc[:, lo:hi], src[:, lo + s:hi + s]
                if t is None:
                    if bias is None:
                        t = dve(ts(o, i, f(j), None, ALU.mult), tok, *free)
                    else:
                        t = dve(ts(o, i, f(j), bias, ALU.mult, ALU.add), tok, *free)
                else:
                    t = dve(stt(o, i, f(j), o, ALU.mult, ALU.add), t)
                yield t

        def run_all(*gens):
            last = [None] * len(gens)
            live = list(range(len(gens)))
            while live:
                for g in list(live):
                    try:
                        last[g] = next(gens[g])
                    except StopIteration:
                        live.remove(g)
            return last

        def mixer1(l):
            w = ("w_in", l)
            menter = m_enter()
            yf = y_free[0]
            z = lambda i: project(w, i * P, xs)
            gens = []
            for i in range(2):
                gb, gt = z(14 + i)
                q, f = tmp.take()
                a = act(func(q[:, :], gb[:, :], ACT.Sigmoid), gt, f)
                psum.give(gb, a)
                ab, at = z(12 + i)
                u = dve(tt(Y[:, i, :], q[:, :], ab[:, :], ALU.mult), a, at, yf)
                psum.give(ab, u)
                tmp.give(q, u)
                gens.append(conv(Y[:, 2 + i, :], Y[:, i, :], (31, lambda j, i=i: vec("cc_conv_w", (l * 31 + j) * 2 + i)), 15,
                                 vec("cc_conv_b", l * 2 + i), u, yf))
            last = [None, None]

            def taps(n):
                for _ in range(n):
                    for i in range(2):
                        try:
                            last[i] = next(gens[i])
                        except StopIteration:
                            pass

            kb, kt = z(10)
            kd_t = rope(kb, kt, 1.0, [(M0[0:64, 4, :], 0, 64), (M0[64:128, 4, :], 0, 64),
                                      (M0[0:64, 5, :], 64, 64), (M0[64:128, 5, :], 64, 64)], menter)
            taps(4)
            vb, vt = z(11)
            vr = M0[:, 6, :].rearrange("p (b c) -> p b c", b=NB)
            v_t = value_rows(vb, vt, vr, menter)
            taps(4)
            heads = []
            q_t = []
            for i in range(4):
                qb, qt = z(6 + i)
                q_t.append(rope(qb, qt, 0.125, [(M0[:, i, :], 0, P)], menter))
                taps(4)
            for h in range(8):
                p0 = 64 * (h % 2)
                g = h // 4
                heads.append((M0[p0:p0 + 64, h // 2, :], M0[p0:p0 + 64, 4 + g, :],
                              lambda b, g=g: vr[:, b, 64 * g:64 * g + 64], h // 2, p0, (kd_t, v_t, q_t[h // 2])))
            for i in range(2):
                cb, ct = z(2 + i)
                q, f = tmp.take()
                a = act(copy(q[:, :], cb[:, :]), ct, f)
                psum.give(cb, a)
                hb, ht = z(4 + i)
                p = dve(tt(M1[:, i, :], q[:, :], hb[:, :], ALU.mult), a, ht, menter)
                psum.give(hb, p)
                tmp.give(q, p)
                c, = run_all(conv(M1[:, 2 + i, :], M1[:, i, :],
                                  (3, lambda j, i=i: vec("sc_conv_w", (l * 3 + j) * 2 + i)), 1, None, p))
                bb, bt = z(i)
                x_used(bt)
                q, f = tmp.take()
                y = dve(tt(q[:, :], M1[:, 2 + i, :], bb[:, :], ALU.mult), c, bt, f)
                psum.give(bb, y)
                r = split(*hid[i], q[:, :], y, hid_free[i])
                hs[i] = hid[i] + (r,)
                tmp.give(q, r)
                taps(4)
            taps(31)
            done = [None]

            def cc_norm():
                def out(m, ap, s):
                    q, f = tmp.take()
                    a = act(func(q[:, :], ap, ACT.Silu, bias=vec("cc_ln_b", l * 2 + m)), s, f)
                    r = split(*hid[6 + m], q[:, :], a, hid_free[6 + m])
                    hs[6 + m] = hid[6 + m] + (r,)
                    tmp.give(q, r)
                    y_free[0] = r

                layer_norm([(Y[:, 2 + i, :], last[i]) for i in range(2)], lambda m: vec("cc_ln_g", l * 2 + m), None, out)

            cc_norm()
            attention(heads, lambda b: (max(b - 1, 0), 3 - (b == 0) - (b == 3), P if b == 0 else 0), M1m,
                      lambda h: CT[:, C_SINK + l * 8 + h:C_SINK + l * 8 + h + 1], to_hidden(2), done)
            out_project(("w_out", l), add_residual)
            m_leave(done[0], r)

        def log1p(e_, out, n, w, tok):
            zt, f1 = tmp.take()
            z2, f2 = tmp.take()
            z, zz = zt[0:n, 0:w], z2[0:n, 0:w]
            t = dve(ts(z, e_, 2.0, None, ALU.add), tok, f1)
            t = dve(lambda v: v.reciprocal(z, z), t)
            t = dve(tt(z, z, e_, ALU.mult), t)
            t = dve(tt(zz, z, z, ALU.mult), t, f2)
            t = dve(ts(out, zz, 2.0 / 17, 2.0 / 15, ALU.mult, ALU.add), t)
            for k in (13, 11, 9, 7, 5, 3, 1):
                t = dve(tt(out, out, zz, ALU.mult), t)
                t = dve(ts(out, out, 2.0 / k, None, ALU.add), t)
            t = dve(tt(out, out, z, ALU.mult), t)
            tmp.give(zt, t)
            tmp.give(z2, t)
            return t

        def mixer2():
            w = ("ev_w_in_2", 0)
            menter = m_enter()
            yf = y_free[0]
            z = lambda c0: project(w, c0, xs)
            gb, gt = z(2048)
            G, f = tmp.take()
            t = dve(ts(G[0:8, :], gb[0:8, :], VT[0:8, V_BI:V_BI + 1], None, ALU.add), gt, f)
            psum.give(gb, t)
            fb, ff = psum.take()
            ft = op("pe", lambda e: e.matmul(fb[0:4, :], CT[0:8, C_ID + 4:C_ID + 8], G[0:8, :], start=True, stop=True),
                    t, ff)
            FP, f1 = tmp.take()
            t = dve(vcopy(FP[0:4, :], fb[0:4, :]), ft, f1)
            psum.give(fb, t)
            E_, f2 = tmp.take()
            t2 = dve(stt(E_[0:4, :], FP[0:4, :], -1.0, FP[0:4, :], ALU.mult, ALU.max), t, f2)
            t2 = act(func(E_[0:4, :], E_[0:4, :], ACT.Exp, scale=-1.0), t2)
            L_, f3 = tmp.take()
            t3 = log1p(E_[0:4, :], L_[0:4, :], 4, T, (t2, f3))
            t3 = dve(stt(L_[0:4, :], FP[0:4, :], 0.0, L_[0:4, :], ALU.min, ALU.subtract), t3)
            o1 = dve(lambda e: e.memset(E_[0:4, :], 1.0), t3)
            t3 = dve(lambda e: e.tensor_tensor_scan(FP[0:4, :], E_[0:4, :], L_[0:4, :], 0.0, ALU.mult, ALU.add), o1, t3)
            ta = dve(tt(G[0:4, :], G[0:4, :], FP[0:4, :], ALU.subtract), t3, ft)
            tM = dve(lambda e: e.tensor_tensor_scan(E_[0:4, :], G[0:4, :], G[0:4, :], 0.0, ALU.max, ALU.max), ta)
            t4 = dve(tt(L_[0:4, :], FP[0:4, :], E_[0:4, :], ALU.add), tM)
            tE = act(func(L_[0:4, :], L_[0:4, :], ACT.Exp, scale=-1.0), t4)
            tmp.give(FP, t4)
            cb, cf = psum.take()
            for b in range(NB):
                t = op("pe", lambda e, b=b: e.transpose(cb[:, 4 * b:4 * b + 4], G[0:4, b * P:(b + 1) * P],
                                                        CT[0:4, C_ID:C_ID + 4]), ta, cf)
            tmp.give(G, t)
            acol = sm[:, 96:112]
            tcol = dve(vcopy(acol, cb[:, 0:16]), t)
            psum.give(cb, tcol)

            rw, rf = tmp.take()
            rwa = dma("rga", rw[:, :].rearrange("p (n c) -> p n c", n=4), d["ev_rg_wa_2"][0].rearrange("n p c -> p n c"), rf)
            rx, rf = tmp.take()
            rwx = dma("rgb", rx[:, :].rearrange("p (n c) -> p n c", n=4), d["ev_rg_wx_2"][0].rearrange("n p c -> p n c"), rf)
            lam = VT[:, V_OFF["ev_rg_lambda_2"]:V_OFF["ev_rg_lambda_2"] + 4]
            s1, f = tmp.take()
            t = dve(stt(s1[:, 0:4], lam, -1.0, lam, ALU.mult, ALU.max), f)
            t = act(func(s1[:, 0:4], s1[:, 0:4], ACT.Exp, scale=-1.0), t)
            t = log1p(s1[:, 0:4], s1[:, 8:12], P, 4, t)
            t = dve(ts(s1[:, 16:20], lam, -1.0, 0.0, ALU.mult, ALU.max), t)
            t = dve(tt(s1[:, 8:12], s1[:, 8:12], s1[:, 16:20], ALU.add), t)
            tcs = dve(ts(sm[:, 112:116], s1[:, 8:12], 8.0, None, ALU.mult), t)
            tmp.give(s1, tcs)

            qkvo = []
            rec = []

            def lru(n):
                xb_, xt = z(2056 + n * P)
                x_t = act(copy(Y[:, n, :], xb_[:, :]), xt, yf)
                psum.give(xb_, x_t)
                xc, f = tmp.take()
                t, = run_all(conv(xc[:, :], Y[:, n, :], (4, lambda j: vec("ev_conv_w_2", j * 4 + n)), 3,
                                  vec("ev_conv_b_2", n), x_t, f))
                b1, f1 = psum.take()
                b2, f2 = psum.take()
                p1 = op("pe", lambda e: e.matmul(b1[:, :], rw[:, n * P:(n + 1) * P], xc[:, :], start=True, stop=True), t, f1, rwa)
                p2 = op("pe", lambda e: e.matmul(b2[:, :], rx[:, n * P:(n + 1) * P], xc[:, :], start=True, stop=True), t, f2, rwx)
                r_, f1 = tmp.take()
                i_, f2 = tmp.take()
                a1 = act(func(r_[:, :], b1[:, :], ACT.Sigmoid, bias=vec("ev_rg_ba_2", n)), p1, f1)
                a2 = act(func(i_[:, :], b2[:, :], ACT.Sigmoid, bias=vec("ev_rg_bx_2", n)), p2, f2)
                psum.give(b1, a1)
                psum.give(b2, a2)
                ix = dve(tt(i_[:, :], i_[:, :], xc[:, :], ALU.mult), a2)
                tmp.give(xc, ix)
                yy = dve(ts(r_[:, :], r_[:, :], sm[:, 112 + n:113 + n], None, ALU.mult), a1, tcs)
                th, f3 = tmp.take()
                at = act(func(th[:, :], r_[:, :], ACT.Tanh), yy, f3)
                ae = act(func(r_[:, :], r_[:, :], ACT.Exp, scale=-1.0), yy, at)
                dd, f4 = tmp.take()
                t = dve(ts(dd[:, :], th[:, :], 1.0, None, ALU.add), at, f4)
                t = dve(lambda e: e.reciprocal(dd[:, :], dd[:, :]), t)
                t = dve(stt(dd[:, :], dd[:, :], 2.0, th[:, :], ALU.mult, ALU.mult), t)
                tmp.give(th, t)
                t = act(func(dd[:, :], dd[:, :], ACT.Sqrt), t)
                t = dve(tt(i_[:, :], i_[:, :], dd[:, :], ALU.mult), t, ix)
                tmp.give(dd, t)
                t = dve(lambda e: e.tensor_tensor_scan(Y[:, n, :], r_[:, :], i_[:, :], 0.0, ALU.mult, ALU.add), t, ae)
                tmp.give(i_, t)
                tmp.give(r_, t)
                yb_, yt = z(2056 + 512 + n * P)
                g = act(func(Y[:, 4 + n, :], yb_[:, :], ACT.Gelu_apprx_tanh), yt, yf)
                psum.give(yb_, g)
                q, f = tmp.take()
                t = dve(tt(q[:, :], Y[:, n, :], Y[:, 4 + n, :], ALU.mult), t, g, f)
                r = split(*hid[4 + n], q[:, :], t, hid_free[4 + n])
                hs[4 + n] = hid[4 + n] + (r,)
                tmp.give(q, r)
                y_free[0] = t
                return p2, yt

            for h in range(4):
                qb, qt = z(h * P)
                tq = act(copy(M0[:, h, :], qb[:, :]), qt, menter)
                psum.give(qb, tq)
                kb, kt = z(512 + h * P)
                tk = dve(vcopy(M0[:, 4 + h, :], kb[:, :]), kt, menter)
                psum.give(kb, tk)
                vb, vt = z(1024 + h * P)
                tv = value_rows(vb, vt, M1[:, h, :].rearrange("p (b c) -> p b c", b=NB), menter)
                ob, ot = z(1536 + h * P)
                to = act(func(M1[:, 4 + h, :], ob[:, :], ACT.Sigmoid), ot, menter)
                psum.give(ob, to)
                rec.append(lru(h))
                qkvo.append((tq, tk, tv, to))
            x_used(rec[-1][1])
            tmp.give(rw, rec[-1][0])
            tmp.give(rx, rec[-1][0])

            SCL = float(128) ** -0.5
            def head(h):
                tq, tk, tv, to = qkvo[h]
                sel = CT[0:4, C_SEL + h * P:C_SEL + (h + 1) * P]
                mb, mf = psum.take()
                tm = op("pe", lambda e: e.matmul(mb[:, :], sel, E_[0:4, :], start=True, stop=True), tM, mf)
                eb, ef = psum.take()
                te = op("pe", lambda e: e.matmul(eb[:, :], sel, L_[0:4, :], start=True, stop=True), tE, ef)
                nb_, nf = psum.take()
                db_, df = psum.take()
                g2 = None
                for s in range(NB):
                    t0 = s * P
                    w_ = T - t0
                    sbk, sf = psum.take()
                    ts_ = op("pe", lambda e, s=s, t0=t0, w_=w_, sbk=sbk: e.matmul(
                        sbk[:, 0:w_], M0[:, 4 + h, t0:t0 + P], M0[:, h, t0:T], start=True, stop=True), tq, tk, sf)
                    ex, xf = tmp.take()
                    ac = acol[:, 4 * s + h:4 * s + h + 1]
                    g0 = dve(stt(ex[:, 0:P], mb[:, t0:t0 + P], -1.0, CAU, ALU.mult, ALU.add), tm, xf, g2)
                    g1 = act(func(ex[:, 0:P], ex[:, 0:P], ACT.Exp, bias=ac), g0, tcol)
                    if w_ > P:
                        g2 = act(func(ex[:, P:w_], mb[:, t0 + P:T], ACT.Exp, bias=ac, scale=-1.0), g0, tcol)
                    else:
                        g2 = g1
                    v = dve(stt(ex[:, 0:w_], sbk[:, 0:w_], SCL, ex[:, 0:w_], ALU.mult, ALU.mult), g1, g2, ts_)
                    psum.give(sbk, v)
                    vr = M1[:, h, t0:t0 + P]
                    tn = op("pe", lambda e, s=s, t0=t0, w_=w_, ex=ex, vr=vr: e.matmul(
                        nb_[:, t0:T], vr, ex[:, 0:w_], start=s == 0, stop=s == NB - 1), v, tv, nf)
                    td = op("pe", lambda e, s=s, t0=t0, w_=w_, ex=ex: e.matmul(
                        db_[:, t0:T], ones, ex[:, 0:w_], start=s == 0, stop=s == NB - 1), v, df)
                    tmp.give(ex, td)
                psum.give(mb, g1, g2)
                dn, f = tmp.take()
                a = act(func(dn[:, :], db_[:, :], ACT.Abs), td, f)
                psum.give(db_, a)
                v = dve(tt(dn[:, :], dn[:, :], eb[:, :], ALU.max), a, te)
                psum.give(eb, v)
                v = dve(lambda e, dn=dn: e.reciprocal(dn[:, :], dn[:, :]), v)
                v = dve(tt(dn[:, :], dn[:, :], nb_[:, :], ALU.mult), v, tn)
                psum.give(nb_, v)
                v = dve(tt(dn[:, :], dn[:, :], M1[:, 4 + h, :], ALU.mult), v, to)
                r = split(*hid[h], dn[:, :], v, hid_free[h])
                hs[h] = hid[h] + (r,)
                tmp.give(dn, r)
                return tm, te, td, r

            for h in range(4):
                tm, te, td, r = head(h)
            tmp.give(E_, tm)
            tmp.give(L_, te)
            m_leave(td, r)
            out_project(("ev_w_out_2", 0), to_y)

        def rope_tables(after):
            pi_, f = tmp.take()
            tp = dma("pos", pi_[:, :].bitcast(I32), d["pos"], f)
            an, f1 = tmp.take()
            k_, f2 = tmp.take()
            t = dve(vcopy(an[:, :], pi_[:, :].bitcast(I32)), tp, f1)
            t = dve(ts(an[:, :], an[:, :], CT[:, C_INV:C_INV + 1], None, ALU.mult), t, f2)
            c1, c2, c3 = two_pi_parts()
            big = 12582912.0
            for m in (4096.0, 1.0):
                t = dve(ts(k_[:, :], an[:, :], 1.0 / (2 * math.pi * m), big, ALU.mult, ALU.add), t)
                t = dve(ts(k_[:, :], k_[:, :], big, None, ALU.subtract), t)
                for c in (c1, c2, c3):
                    t = dve(stt(an[:, :], k_[:, :], -c * m, an[:, :], ALU.mult, ALU.add), t)
            lim = 3.1415925
            t = dve(ts(an[:, :], an[:, :], lim, -lim, ALU.min, ALU.max), t)
            t1 = dve(stt(k_[:, :], an[:, :], -1.0, an[:, :], ALU.mult, ALU.max), t)
            t1 = dve(ts(k_[:, :], k_[:, :], -1.0, 0.5 * math.pi, ALU.mult, ALU.add), t1)
            a1 = act(func(SIN, an[:, :], ACT.Sin), t, after)
            a2 = act(func(COS, k_[:, :], ACT.Sin), t1, after)
            for q in (1, 3):
                t = dve(ts(SIN[32 * q:32 * q + 32, :], SIN[32 * q:32 * q + 32, :], -1.0, None, ALU.mult), a1)
            tmp.give(pi_, t1)
            tmp.give(an, a1)
            tmp.give(k_, a2)
            return t, a2

        def two_pi_parts():
            v = 2 * math.pi
            out = []
            for _ in range(2):
                e = math.floor(math.log2(v))
                c = math.floor(v / 2.0 ** (e - 9)) * 2.0 ** (e - 9)
                out.append(c)
                v -= c
            return out + [v]

        rope_last = [()]

        def swa():
            w = ("od_w_qkv_2", 0)
            menter = m_enter()
            tab = rope_tables(rope_last[0])
            Q["dve"].append((None, list(flat(tab)), False))
            z = lambda i: project(w, i * P, xs)
            kts, vts = [], []
            for i in range(2):
                kb, kt = z(8 + i)
                kts.append(rope(kb, kt, 1.0, [(M1[0:64, 2 * i, :], 0, 64), (M1[64:128, 2 * i, :], 0, 64),
                                              (M1[0:64, 2 * i + 1, :], 64, 64), (M1[64:128, 2 * i + 1, :], 64, 64)],
                                menter))
            for i in range(2):
                vb, vt = z(10 + i)
                vts.append(value_rows(vb, vt, M1[:, 4 + i, :].rearrange("p (b c) -> p b c", b=NB), menter))
            heads = []
            for i in range(8):
                qb, qt = z(i)
                x_used(qt)
                tq = rope(qb, qt, 0.125, [(M0[:, i, :], 0, P)], menter)
                for h in (2 * i, 2 * i + 1):
                    p0 = 64 * (h % 2)
                    g = h // 4
                    vr = M1[:, 4 + g // 2, :].rearrange("p (b c) -> p b c", b=NB)
                    heads.append((M0[p0:p0 + 64, i, :], M1[p0:p0 + 64, g, :],
                                  lambda b, g=g, vr=vr: vr[:, b, 64 * (g % 2):64 * (g % 2) + 64], i, p0,
                                  (kts[g // 2], vts[g // 2], tq)))
            done = [None]
            attention(heads, lambda b: (max(b - 1, 0), 2 - (b == 0), P if b == 0 else 0), M2m,
                      lambda h: CT[:, C_SINK + 16 + h:C_SINK + 17 + h], to_hidden(0), done)
            m_leave(done[0])
            out_project(("od_w_o_2", 0), to_y)

        def memory(l):
            menter = m_enter()
            yf = y_free[0]
            mem = Y[:, 0:4, :].rearrange("p a (b t) -> p (a b) t", b=2)
            tl = dma("mm", mem, d["memT"].rearrange("(k p) t -> p k t", p=P), yf)
            bank, t, _ = sumsq([(mem[:, k, :], tl) for k in range(KD)])
            rr, r, a = rstd_of(bank[:, 0:256], t, D, RMS_EPS)
            psum.give(bank, a)
            mh = HHa[:, 0:4, :].rearrange("p a (b t) -> p (a b) t", b=2)
            ml = HLa[:, 0:4, :].rearrange("p a (b t) -> p (a b) t", b=2)
            ms = []
            for k in range(KD):
                s = dve(stt(mem[:, k, :], mem[:, k, :], vec("g_mem_2", l * KD + k), rr[:, 0:256], ALU.mult, ALU.mult), r, t)
                ms.append((mh[:, k, :], ml[:, k, :],
                           split(mh[:, k, :], ml[:, k, :], mem[:, k, :], s, [hid_free[i] for i in range(4)])))
            tmp.give(rr, s)
            w = ("w_xkv_2", l)
            KT = M1[:, 0:4, :].rearrange("p a (b t) -> p (a b) t", b=2)
            VR = M1[:, 4:8, :].rearrange("p (m a) t -> p m (a t)", m=2)
            kt, vt = [], []
            for m in range(KD):
                bank, t = project(w, m * P, ms)
                kt.append(act(copy(KT[:, m, :], bank[:, 0:256]), t, menter))
                psum.give(bank, kt[-1])
            for m in range(KD):
                s, ready = next_unit(w, D + m * P)
                bank, free = psum.take()
                for b in range(2):
                    for k, (h, lo, tok) in enumerate(ms):
                        t = op("pe", mm3(bank[:, b * P:(b + 1) * P], h[:, b * P:(b + 1) * P], lo[:, b * P:(b + 1) * P],
                                         wh[s][:, k, :], wl[s][:, k, :], k == 0, k == KD - 1), ready, free, tok)
                spl_free[s] = t
                vt.append(act(copy(VR[:, :, m * P:(m + 1) * P], bank[:, 0:256].rearrange("p (b c) -> p b c", b=2)), t, menter))
                psum.give(bank, vt[-1])
            for i in range(4):
                hid_free[i] = t
            y_free[0] = ms[-1][2]
            return KT, VR, kt, vt

        def cross(l, KT, VR, kt, vt):
            menter = m_enter()
            tq = []
            for m in range(KD):
                bank, t = project(("w_xq_2", l), m * P, xs)
                tq.append(act(copy(M0[:, m, :], bank[:, :]), t, menter))
                psum.give(bank, tq[-1])
            x_used(t)
            st = {}
            pt_free = [y_free[0], y_free[0]]
            pts = {}
            SC = 1.0 / 16

            def score(h, b):
                bank, f = psum.take()
                for i in range(2):
                    t = op("pe", lambda e, i=i: e.matmul(bank[:, 0:256], M0[:, 2 * h + i, b * P:(b + 1) * P],
                                                         KT[:, 2 * h + i, :], start=i == 0, stop=i == 1),
                           f, tq[2 * h + i], kt[2 * h + i])
                s, sf = tmp.take()
                c, cf = sm_ring.take()
                r = dve(lambda e: e.tensor_reduce(c[:, 0:1], bank[:, 0:256], AX, ALU.max), t, cf)
                r = dve(ts(c[:, 1:2], c[:, 0:1], -SC, None, ALU.mult), r)
                x = act(lambda e: e.activation(s[:, 0:256], bank[:, 0:256], ACT.Exp, bias=c[:, 1:2], scale=SC,
                                               accum_out=c[:, 2:3]), r, sf)
                psum.give(bank, x)
                r = dve(lambda e: e.reciprocal(c[:, 3:4], c[:, 2:3]), x)
                r = dve(ts(s[:, 0:256], s[:, 0:256], c[:, 3:4], None, ALU.mult), r)
                sm_ring.give(c, r)
                st[h, b] = (s, r)

            def turn(h, b):
                s, tok = st.pop((h, b))
                bank, f = psum.take()
                for i in range(2):
                    t = op("pe", lambda e, i=i: e.transpose(bank[:, i * P:(i + 1) * P], s[:, i * P:(i + 1) * P], ident),
                           tok, f)
                tmp.give(s, t)
                o = 4 * (h % 2)
                c = act(copy(Y[:, o:o + 2, b * P:(b + 1) * P], bank[:, 0:256].rearrange("p (i q) -> p i q", i=2)), t,
                        pt_free[h % 2])
                psum.give(bank, c)
                pts[h] = c

            def value(h):
                o = 4 * (h % 2)
                for j in range(2):
                    bank, f = psum.take()
                    for i in range(2):
                        t = op("pe", lambda e, i=i, j=j, bank=bank: e.matmul(bank[:, :], VR[:, i, (2 * h + j) * P:(2 * h + j + 1) * P],
                                                             Y[:, o + i, :], start=i == 0, stop=i == 1),
                               f, pts[h], vt[2 * h + j])
                    s = 2 * h + j
                    hi, lo = hid[s]
                    r = split(hi, lo, bank[:, :], t, hid_free[s])
                    hs[s] = (hi, lo, r)
                    psum.give(bank, r)
                pt_free[h % 2] = t
                return t

            jobs = [(h, b) for h in range(4) for b in range(NB)]
            for n in range(len(jobs) + 1):
                if n < len(jobs):
                    score(*jobs[n])
                if n >= 1:
                    turn(*jobs[n - 1])
                if n >= NB and n % NB == 1 and n > NB:
                    value(n // NB - 1)
            t = value(3)
            y_free[0] = t
            m_leave(t)
            out_project(("w_xo_2", l), to_y)

        def first_ffn(l, n, ln):
            ffn((f"ffn{n}_w_gu", l), (f"ffn{n}_w_down", l), FF1 // P, True, add_residual)
            block_norm(l, ln)

        def first_mixer(l):
            mixer1(l)
            block_norm(l, "ln2")

        def second_mixer(l):
            if l == 0:
                rope_last[0] = ("dve", cnt["dve"])
            pre_norm("g_mix_pre_2", l)
            if l == 0:
                mixer2()
            else:
                swa()
            post_norm("g_mix_post_2", l, ys)

        def second_cross(l):
            kv = memory(l)
            pre_norm("g_x_pre_2", l)
            cross(l, *kv)
            post_norm("g_x_post_2", l, ys)

        def second_ffn(l):
            pre_norm("g_ff_pre_2", l)
            ffn(("w_ff1_2", l), ("w_ff2_2", l), FF2 // P, False, to_y)
            post_norm("g_ff_post_2", l, ys)

        steps = []
        for l in range(2):
            steps += [lambda l=l: first_ffn(l, 1, "ln1"), lambda l=l: first_mixer(l), lambda l=l: first_ffn(l, 2, "ln3")]
        for l in range(2):
            steps += [lambda l=l: second_mixer(l), lambda l=l: second_cross(l), lambda l=l: second_ffn(l)]
        for step in steps:
            step()
        oT = d["outT"].rearrange("(k p) t -> p k t", p=P)
        for m in range(KD):
            last = dma("out", oT[:, m, :], XR[:, m, :], xr_tok[m])
        Q["sp"].append((None, [last], False))

        if units_in is None:
            return units

        def emit(name, eng):
            seen = {}
            for fn, waits, inc in Q[name]:
                need = {}
                for s, v in waits:
                    need[s] = max(need.get(s, 0), v)
                for s, v in need.items():
                    if seen.get(s, 0) < v:
                        eng.wait_ge(sems[s], v)
                        seen[s] = v
                if fn is None:
                    continue
                ins = fn(eng)
                if inc:
                    ins.then_inc(sems[name], 1)

        block = es.enter_context(nc.Block())

        @block.sync
        def _(eng):
            emit("sp", eng)

        @block.scalar
        def _(eng):
            emit("act", eng)

        @block.vector
        def _(eng):
            emit("dve", eng)

        @block.gpsimd
        def _(eng):
            emit("pool", eng)

        @block.tensor
        def _(eng):
            emit("pe", eng)


def constants():
    c = np.zeros((P, C_W), np.float32)
    p = np.arange(P)
    c[:, C_ID:C_ID + P] = np.eye(P)
    c[:, C_ONE:C_ONE + P] = 1.0
    half = 32
    inv = np.power(np.float32(10000.0), -np.arange(half, dtype=np.float32) / np.float32(half)).astype(np.float32)
    ang = (np.arange(T, dtype=np.float32)[None, :] * inv[p % 32][:, None]).astype(np.float32).astype(np.float64)
    sign = np.where((p // 32) % 2 == 0, 1.0, -1.0)[:, None]
    c[:, C_COS:C_COS + T] = np.cos(ang)
    c[:, C_SIN:C_SIN + T] = np.sin(ang) * sign
    r, k = p[:, None], np.arange(P)[None, :]
    c[:, C_M1:C_M1 + P] = np.where(k >= r, 0.0, NEG)
    c[:, C_M1 + 2 * P:C_M1 + 3 * P] = np.where(k <= r, 0.0, NEG)
    c[:, C_M2:C_M2 + P] = np.where(k > r, 0.0, NEG)
    c[:, C_M2 + P:C_M2 + 2 * P] = np.where(k <= r, 0.0, NEG)
    c[:, C_CAUSAL:C_CAUSAL + P] = np.where(k >= r, 0.0, NEG)
    for h in range(4):
        c[h, C_SEL + h * P:C_SEL + (h + 1) * P] = 1.0
    c[:, C_INV] = inv[p % 32]
    c[:, C_EPS] = LN_EPS
    c[:, C_EPS + 1] = RMS_EPS
    return c


_WEIGHTS = ["ffn1_w_gu", "ffn1_w_down", "w_in", "w_out", "ffn2_w_gu", "ffn2_w_down", "ev_w_in_2", "ev_rg_wa_2",
            "ev_rg_wx_2", "ev_w_out_2", "od_w_qkv_2", "od_w_o_2", "w_xq_2", "w_xkv_2", "w_xo_2", "w_ff1_2", "w_ff2_2",
            ]


def kernel(**inputs):
    import concourse.bacc as _bacc
    from concourse.bass_utils import run_bass_kernel_spmd as _run

    a = {n: np.ascontiguousarray(v) for n, v in inputs.items()}
    arrays = {n: a[n] for n in _WEIGHTS}
    arrays["xT"] = np.ascontiguousarray(a["x"][0].T)
    arrays["memT"] = np.ascontiguousarray(a["mem_2"][0].T)
    vecs = np.zeros((V_W, P), np.float32)
    for n, s in VEC_SIZES:
        vecs[V_OFF[n]:V_OFF[n] + s] = a[n].reshape(s, P)
    vecs[V_BI, 0:8] = a["ev_b_if_2"][0]
    arrays["vecs"] = np.ascontiguousarray(vecs.T)
    c = constants()
    c[:, C_SINK:C_SINK + 16] = a["attn_sink"].reshape(1, 16)
    c[:, C_SINK + 16:C_SINK + 32] = a["od_sinks_2"].reshape(1, 16)
    arrays["consts"] = c
    arrays["pos"] = np.ascontiguousarray(np.broadcast_to(a["positions_2"].reshape(1, T), (P, T)))

    def make():
        nc = _bacc.Bacc("TRN2", target_bir_lowering=False, num_devices=1)
        d = {}
        for n, v in arrays.items():
            d[n] = nc.dram_tensor(f"in_{n}", v.shape, mybir.dt.from_np(v.dtype), kind="ExternalInput").ap()
        d["outT"] = nc.dram_tensor("outT", (D, T), F32, kind="ExternalOutput").ap()
        return nc, d

    order = build(*make(), None)
    nc, d = make()
    build(nc, d, order)
    r = _run(nc, [{f"in_{n}": v for n, v in arrays.items()}], core_ids=[0])
    return np.ascontiguousarray(r.results[0]["outT"].T)[None]
```

```python
import math
from contextlib import ExitStack

import numpy as np
import concourse.bass as bass
from concourse import mybir

F32 = mybir.dt.float32
F32R = mybir.dt.float32r
I32 = mybir.dt.int32
ALU = mybir.AluOpType
ACT = mybir.ActivationFunctionType
AX = mybir.AxisListType.X

P = 128
T = 512
D = 1024
KD = 8
NB = 4
ALPHA = float(4.0 ** 0.25)
LN_EPS = 1e-5
RMS_EPS = 1e-6
NEG = -1e30
FF1 = 2816
FF2 = 4096

RAW = 3
SPL = 4
LEAD = 3
NTMP = 11

C_ID = 0
C_ONE = 128
C_COS = 256
C_SIN = 768
C_M1 = 1280
C_M2 = 1664
C_SEL = 1920
C_INV = 2432
C_EPS = 2433
C_SINK = 2436
C_W = 2468

VEC_SIZES = [("ln1_g", 16), ("ln1_b", 16), ("ln2_g", 16), ("ln2_b", 16), ("ln3_g", 16), ("ln3_b", 16),
             ("sc_conv_w", 12), ("cc_conv_w", 124), ("cc_conv_b", 4), ("cc_ln_g", 4), ("cc_ln_b", 4),
             ("g_mix_pre_2", 16), ("g_mix_post_2", 16), ("g_x_pre_2", 16), ("g_x_post_2", 16), ("g_mem_2", 16),
             ("g_ff_pre_2", 16), ("g_ff_post_2", 16), ("ev_conv_w_2", 16), ("ev_conv_b_2", 4),
             ("ev_rg_ba_2", 4), ("ev_rg_bx_2", 4), ("ev_rg_lambda_2", 4)]
V_OFF = {}
V_W = 0
for _n, _s in VEC_SIZES:
    V_OFF[_n] = V_W
    V_W += _s
V_BI = V_W
V_W += 2


class Ring:

    def __init__(self, items):
        self.q = [(i, ()) for i in items]

    def take(self):
        return self.q.pop(0)

    def give(self, item, *toks):
        self.q.append((item, toks))


def build(nc, d, units_in):
    units = []
    es = ExitStack()
    with es:
        def sb(name, shape, dt=F32):
            return es.enter_context(nc.sbuf_tensor(name, shape, dt))

        XR = sb("XR", [P, KD, T])
        XH = sb("XH", [P, KD, T], F32R)
        XL = sb("XL", [P, KD, T], F32R)
        Y = sb("Y", [P, KD, T])
        HHa = sb("HHa", [P, KD, T], F32R)
        HLa = sb("HLa", [P, KD, T], F32R)
        with nc.sbuf_tensor("HHb", [P, KD, T], F32R) as HHb, nc.sbuf_tensor("HLb", [P, KD, T], F32R) as HLb:
            pass
        M0 = sb("M0", [P, KD, T])
        M1 = sb("M1", [P, KD, T])
        raw = [sb(f"raw{i}", [P, KD, P]) for i in range(RAW)]
        wh = [sb(f"wh{i}", [P, KD, P], F32R) for i in range(SPL)]
        wl = [sb(f"wl{i}", [P, KD, P], F32R) for i in range(SPL)]
        tmps = [sb(f"tmp{i}", [P, T]) for i in range(NTMP)]
        CT = sb("CT", [P, C_W])
        VT = sb("VT", [P, V_W])
        sm = sb("sm", [P, 128])
        sts = [sb(f"st{i}", [P, 24]) for i in range(2)]
        banks = [es.enter_context(nc.psum_tensor(f"ps{i}", [P, T], F32)) for i in range(8)]

        sems = {}

        def sem(name):
            if name not in sems:
                sems[name] = es.enter_context(nc.semaphore(name))
            return sems[name]

        for n in ("pe", "act", "dve", "pool", "ld", "ct", "mm", "out", "rga", "rgb", "pos"):
            sem(n)
        for i in range(RAW):
            sem(f"w{i}")

        Q = {e: [] for e in ("pe", "act", "dve", "pool", "sp")}
        cnt = {e: 0 for e in Q}

        def flat(ts):
            for t in ts:
                if not t:
                    continue
                if isinstance(t[0], str):
                    yield t
                else:
                    yield from flat(t)

        def op(e, fn, *after):
            cnt[e] += 1
            Q[e].append((fn, list(flat(after)), True))
            return (e, cnt[e])

        def quiet(e, fn, *after):
            Q[e].append((fn, list(flat(after)), False))

        def dve(fn, *a):
            return op("dve", fn, *a)

        def act(fn, *a):
            return op("act", fn, *a)

        def pool(fn, *a):
            return op("pool", fn, *a)

        dma_n = {}

        def dma(name, out, src, *after):
            dma_n[name] = dma_n.get(name, 0) + 16
            s = sem(name)
            quiet("sp", lambda e: e.dma_start(out, src).then_inc(s, 16), *after)
            return (name, dma_n[name])

        psum = Ring(banks)
        tmp = Ring(tmps)
        st_ring = Ring(sts)

        def copy(out, in_):
            return lambda e: e.activation(out, in_, ACT.Copy)

        def vcopy(out, in_):
            return lambda e: e.tensor_copy(out, in_)

        def func(out, in_, f, **kw):
            return lambda e: e.activation(out, in_, f, **kw)

        def tt(out, a, b, o):
            return lambda e: e.tensor_tensor(out, a, b, o)

        def ts(out, a, s1, s2, o0, o1=None):
            if o1 is None:
                return lambda e: e.tensor_scalar(out, a, s1, None, o0)
            return lambda e: e.tensor_scalar(out, a, s1, s2, o0, o1)

        def stt(out, a, s, b, o0, o1):
            return lambda e: e.scalar_tensor_tensor(out=out, in0=a, scalar=s, in1=b, op0=o0, op1=o1)

        def f32(ap):
            return ap.bitcast(F32)

        raw_free = [()] * RAW
        spl_free = [()] * SPL
        loaded, split_at, ptr = [], [], [0]

        def load_unit(i):
            name, l, k0, nk, c0 = units_in[i]
            s = i % RAW
            src = d[name][l][k0 * P:(k0 + nk) * P, c0:c0 + P].rearrange("(k p) c -> p k c", p=P)
            loaded.append(dma(f"w{s}", raw[s][:, 0:nk, :], src, raw_free[s]))

        def split_unit(i):
            nk = units_in[i][3]
            r, s = i % RAW, i % SPL
            hi = act(copy(wh[s][:, 0:nk, :], raw[r][:, 0:nk, :]), loaded[i], spl_free[s])
            lo = dve(tt(wl[s][:, 0:nk, :], raw[r][:, 0:nk, :], f32(wh[s][:, 0:nk, :]), ALU.subtract), hi)
            raw_free[r] = lo
            split_at.append(lo)

        def next_unit(w, c0, k0=0, nk=KD, base=None):
            i = ptr[0]
            base = i if base is None else base
            ptr[0] += 1
            if units_in is None:
                units.append((*w, k0, nk, c0))
                return i % SPL, ("dve", 1)
            n = len(units_in)
            while len(split_at) < min(n, base + SPL):
                while len(loaded) < min(n, len(split_at) + RAW):
                    load_unit(len(loaded))
                split_unit(len(split_at))
            while len(loaded) < min(n, len(split_at) + RAW):
                load_unit(len(loaded))
            return i % SPL, split_at[i]

        def mm3(out, lh, ll, rh, rl, start, stop):
            def f(e):
                e.matmul(out, lh, rh, start=start, stop=False)
                e.matmul(out, lh, rl, start=False, stop=False)
                return e.matmul(out, ll, rh, start=False, stop=stop)
            return f

        def project_group(cols, xs, k0=0):
            nk = len(xs)
            base = ptr[0]
            n = xs[0][0].shape[-1]
            us = [next_unit(w, c0, k0, nk, base) + psum.take() for w, c0 in cols]
            out = []
            for k, (h, l, tok) in enumerate(xs):
                for s, ready, bank, free in us:
                    f = mm3(bank[:, 0:n], wh[s][:, k, :], wl[s][:, k, :], h, l, k == 0, k == nk - 1)
                    a = (ready, free, tok) if k == 0 else (tok,)
                    if k < nk - 1:
                        quiet("pe", f, *a)
                    else:
                        done = op("pe", f, *a)
                        spl_free[s] = done
                        out.append((bank, done))
            return out

        def project(w, c0, xs, k0=0):
            return project_group([(w, c0)], xs, k0)[0]

        def stream(cols, xs):
            todo = list(cols)
            got = []

            def start():
                lead = todo[:LEAD]
                got.extend(project_group(lead, xs))

            def nxt():
                if not got:
                    got.extend(project_group(todo[:1], xs))
                todo.pop(0)
                return got.pop(0)

            nxt.start = start
            return nxt

        def split(hi, lo, src, *after):
            a = act(copy(hi, src), *after)
            return dve(tt(lo, src, f32(hi), ALU.subtract), a)

        xT = d["xT"].rearrange("(k p) t -> p k t", p=P)
        t_x = [dma(f"x{k}", XR[:, k, :], xT[:, k, :]) for k in range(KD)]
        ident = CT[:, C_ID:C_ID + P]
        ones = CT[:, C_ONE:C_ONE + P]
        COS = CT[:, C_COS:C_COS + T]
        SIN = CT[:, C_SIN:C_SIN + T]
        M1m = CT[:, C_M1:C_M1 + 384]
        M2m = CT[:, C_M2:C_M2 + 256]
        CAU = CT[:, C_M1:C_M1 + P]

        def eps(v):
            c = {LN_EPS: C_EPS, RMS_EPS: C_EPS + 1}[v]
            return CT[:, c:c + 1]

        def vec(name, i):
            return VT[:, V_OFF[name] + i:V_OFF[name] + i + 1]

        xr_tok = list(t_x)
        x_free = [()] * KD
        xs = [None] * KD

        def split_x(k, src, *after):
            t = split(XH[:, k, :], XL[:, k, :], src, x_free[k], *after)
            xs[k] = (XH[:, k, :], XL[:, k, :], t)
            return t

        for k in range(KD):
            split_x(k, XR[:, k, :], t_x[k])
        if units_in is not None:
            for i in range(RAW):
                load_unit(i)
        t_ct = [dma("ct", CT[:, :], d["consts"]), dma("ct", VT[:, :], d["vecs"])][-1]

        hid = [(HHa[:, i, :], HLa[:, i, :]) for i in range(KD)] + [(HHb[:, i, :], HLb[:, i, :]) for i in range(KD)]
        hid_free = [()] * 16
        m_last = [()]

        class Stats:

            def __init__(self, mean):
                self.mean, self.n, self.t1, self.t2 = mean, 0, None, None
                self.s2, self.f2 = tmp.take()
                if mean:
                    self.s1, self.f1 = tmp.take()

            def add(self, ap, tok, eng="dve"):
                self.n += 1
                if self.n == 1:
                    self.t2 = act(func(self.s2[:, :], ap, ACT.Square), tok, self.f2)
                    self.first = (ap, tok)
                    return
                q, f = tmp.take()
                a = act(func(q[:, :], ap, ACT.Square), tok, f)
                if self.mean:
                    if self.n == 2:
                        self.t1 = pool(tt(self.s1[:, :], self.first[0], ap, ALU.add), self.first[1], tok, self.f1)
                    else:
                        self.t1 = pool(tt(self.s1[:, :], self.s1[:, :], ap, ALU.add), self.t1, tok)
                self.t2 = op(eng, tt(self.s2[:, :], self.s2[:, :], q[:, :], ALU.add), a, self.t2)
                tmp.give(q, self.t2)

            def finish(self, n, e, blocks=NB):
                tb, bf = psum.take()
                for b in range(blocks):
                    t = op("pe", lambda v, b=b: v.matmul(tb[:, b:b + 1], self.s2[:, b * P:(b + 1) * P], ones[:, 0:1],
                                                         start=True, stop=True), self.t2, bf)
                tmp.give(self.s2, t)
                if self.mean:
                    for b in range(blocks):
                        t = op("pe", lambda v, b=b: v.matmul(tb[:, 4 + b:5 + b], self.s1[:, b * P:(b + 1) * P],
                                                             ones[:, 0:1], start=True, stop=True), self.t1)
                    tmp.give(self.s1, t)
                c, cf = st_ring.take()
                w = blocks
                if self.mean:
                    m = dve(ts(c[:, 8:8 + w], tb[:, 4:4 + w], 1.0 / n, None, ALU.mult), t, cf)
                    v = dve(stt(c[:, 12:12 + w], c[:, 8:8 + w], -1.0, c[:, 8:8 + w], ALU.mult, ALU.mult), m)
                    v = dve(stt(c[:, 16:16 + w], tb[:, 0:w], 1.0 / n, c[:, 12:12 + w], ALU.mult, ALU.add), v)
                    psum.give(tb, v)
                    v = dve(ts(c[:, 16:16 + w], c[:, 16:16 + w], 0.0, None, ALU.max), v)
                    a = act(func(c[:, 0:w], c[:, 16:16 + w], ACT.Sqrt, bias=eps(e)), v)
                else:
                    a = act(func(c[:, 0:w], tb[:, 0:w], ACT.Sqrt, bias=eps(e), scale=1.0 / n), t, cf)
                    psum.give(tb, a)
                r = dve(lambda v: v.reciprocal(c[:, 4:4 + w], c[:, 0:w]), a)
                parts = [(4, r)]
                if self.mean:
                    parts.append((20, dve(tt(c[:, 20:20 + w], c[:, 8:8 + w], c[:, 4:4 + w], ALU.mult), r)))
                out = []
                for o, tok in parts:
                    g, gf = tmp.take()
                    bank, bf = psum.take()
                    for b in range(blocks):
                        t = dve(ts(g[:, b * P:(b + 1) * P], ones, c[:, o + b:o + b + 1], None, ALU.mult), tok, gf)
                        p = op("pe", lambda v, b=b, g=g, bank=bank: v.matmul(
                            bank[:, b * P:(b + 1) * P], g[:, b * P:(b + 1) * P], ident, start=True, stop=True), t, bf)
                    tmp.give(g, p)
                    out.append((bank, p))
                st_ring.give(c, t)
                return out

        def center():
            s, f = tmp.take()
            t = dve(tt(s[:, :], XR[:, 0, :], XR[:, 1, :], ALU.add), xr_tok[0], xr_tok[1], f)
            for m in range(2, KD):
                t = dve(tt(s[:, :], s[:, :], XR[:, m, :], ALU.add), t, xr_tok[m])

            def rest():
                bank, bf = psum.take()
                p = op("pe", lambda e: e.matmul(bank[:, :], ones, s[:, :], start=True, stop=True), t, bf)
                tmp.give(s, p)
                for m in range(KD):
                    xr_tok[m] = dve(stt(XR[:, m, :], bank[:, :], -1.0 / D, XR[:, m, :], ALU.mult, ALU.add), p, xr_tok[m])
                psum.give(bank, xr_tok[m])
            return rest

        stats = [None]

        def block_norm(l, which):
            (rb, rt), (mb, mt) = stats[0].finish(D, LN_EPS)
            pend = None
            for m in range(KD + 1):
                if m < KD:
                    q, f = tmp.take()
                    t = dve(tt(q[:, :], XR[:, m, :], rb[:, :], ALU.mult), rt, f, xr_tok[m])
                    t = dve(tt(q[:, :], q[:, :], mb[:, :], ALU.subtract), t, mt)
                    x = act(func(XR[:, m, :], q[:, :], ACT.Identity, bias=vec(f"{which}_b", l * KD + m),
                                 scale=vec(f"{which}_g", l * KD + m)), t)
                    tmp.give(q, x)
                    h = act(copy(XH[:, m, :], XR[:, m, :]), x, x_free[m])
                if pend is not None:
                    k, hk = pend
                    xr_tok[k] = dve(tt(XL[:, k, :], XR[:, k, :], f32(XH[:, k, :]), ALU.subtract), hk, x_free[k])
                    xs[k] = (XH[:, k, :], XL[:, k, :], xr_tok[k])
                pend = (m, h)
            psum.give(rb, t)
            psum.give(mb, t)

        def scaled_split(m, name, l):
            g = vec(name, l * KD + m)
            h = act(func(XH[:, m, :], XR[:, m, :], ACT.Copy, scale=g), xr_tok[m], x_free[m])

            def lo():
                stats[0].add(XR[:, m, :], xr_tok[m], "pool")
                t = dve(stt(XL[:, m, :], XR[:, m, :], g, f32(XH[:, m, :]), ALU.mult, ALU.subtract), h, x_free[m])
                xs[m] = (XH[:, m, :], XL[:, m, :], t)
            return lo

        def first_split(name, l):
            stats[0] = Stats(False)
            for m in range(KD):
                scaled_split(m, name, l)()

        y_free = [()]

        def post_norm(name, l, ystats, nxt, fill=None):
            (rb, rt), = ystats.finish(D, RMS_EPS)
            if nxt:
                stats[0] = Stats(False)
            pend = None
            for m in range(KD + 1):
                if m < KD:
                    s = dve(stt(Y[:, m, :], Y[:, m, :], vec(name, l * KD + m), rb[:, :], ALU.mult, ALU.mult), rt, ys[m])
                    xr_tok[m] = dve(tt(XR[:, m, :], XR[:, m, :], Y[:, m, :], ALU.add), s, xr_tok[m])
                    lo = scaled_split(m, *nxt) if nxt else None
                if pend:
                    pend()
                pend = lo
                if fill and m < KD:
                    fill(m)
            psum.give(rb, s)
            y_free[0] = xr_tok[KD - 1]

        def pre_scale():
            (rb, rt), = stats[0].finish(D, RMS_EPS)
            rr, f = tmp.take()
            t = act(copy(rr[:, :], rb[:, :]), rt, f)
            psum.give(rb, t)
            return rr, t

        t_met = [None]

        def ffn(w_up, w_down, nf, gated, take):
            chunks = [range(c, min(c + KD, nf)) for c in range(0, nf, KD)]
            ready = [None] * nf
            cols = []
            for j in range(nf):
                cols.append((w_up, j * P))
                if gated:
                    cols.append((w_up, nf * P + j * P))
            nxt = stream(cols, xs)
            nxt.start()
            if t_met[0] is None:
                for e in ("pe", "act", "dve", "pool"):
                    Q[e].append((None, [t_ct], False))
                t_met[0] = True
            rr, rt = (None, None) if gated else pre_scale()
            side = []
            rr_used = [None]

            def up(c):
                for j in chunks[c]:
                    s = (c % 2) * KD + j % KD
                    hi, lo = hid[s]
                    h, f2 = tmp.take()
                    q, f1 = tmp.take()
                    if gated:
                        gb, gt = nxt()
                        a = act(func(q[:, :], gb[:, :], ACT.Silu), gt, f1)
                        psum.give(gb, a)
                        ub, ut = nxt()
                        v = dve(stt(h[:, :], q[:, :], 0.5, ub[:, :], ALU.mult, ALU.mult), a, ut, f2)
                        psum.give(ub, v)
                    else:
                        ub, ut = nxt()
                        v = dve(stt(q[:, :], ub[:, :], 0.0, rr[:, :], ALU.max, ALU.mult), ut, f1, rt)
                        rr_used[0] = v
                        psum.give(ub, v)
                        v = act(func(h[:, :], q[:, :], ACT.Square), v, f2)
                    tmp.give(q, v)
                    ready[j] = split(hi, lo, h[:, :], v, hid_free[s])
                    tmp.give(h, ready[j])
                    if gated and j == 2:
                        side.append(center())
                    if gated and j == 5:
                        side[0]()
                for k in range(KD):
                    x_free[k] = ut

            def down(c):
                src = [hid[(c % 2) * KD + j % KD] + (ready[j],) for j in chunks[c]]
                for m in range(KD):
                    bank, t = project(w_down, m * P, src, k0=chunks[c][0])
                    psum.give(bank, take(m, bank, t, c == 0, c == len(chunks) - 1))
                for j in chunks[c]:
                    hid_free[(c % 2) * KD + j % KD] = t

            for c in range(len(chunks)):
                up(c)
                if c:
                    down(c - 1)
            if not gated:
                tmp.give(rr, rr_used[0])
            down(len(chunks) - 1)

        def add_residual(m, bank, t, first, last):
            if first:
                xr_tok[m] = dve(stt(XR[:, m, :], XR[:, m, :], ALPHA, bank[:, :], ALU.mult, ALU.add), t, xr_tok[m])
            else:
                xr_tok[m] = dve(tt(XR[:, m, :], XR[:, m, :], bank[:, :], ALU.add), t, xr_tok[m])
            done = xr_tok[m]
            if last:
                if m == 0:
                    stats[0] = Stats(True)
                stats[0].add(XR[:, m, :], xr_tok[m])
            return done

        ys = [None] * KD
        ystats = [None]

        def to_y(m, bank, t, first, last):
            if first:
                ys[m] = dve(vcopy(Y[:, m, :], bank[:, :]), t, y_free[0])
            else:
                ys[m] = dve(tt(Y[:, m, :], Y[:, m, :], bank[:, :], ALU.add), t, ys[m])
            if last:
                if m == 0:
                    ystats[0] = Stats(False)
                ystats[0].add(Y[:, m, :], ys[m])
            return ys[m]

        def x_used(t):
            for k in range(KD):
                x_free[k] = t

        def rope(bank, tok, scale, outs, *free):
            a_, f1 = tmp.take()
            b_, f2 = tmp.take()
            c1 = dve(stt(a_[:, :], bank[:, :], scale, COS, ALU.mult, ALU.mult), tok, f1)
            for q in range(4):
                o = 32 * q
                i = 32 * (q ^ 1)
                c2 = dve(stt(b_[o:o + 32, :], bank[i:i + 32, :], scale, SIN[i:i + 32, :], ALU.mult, ALU.mult), tok, f2)
            psum.give(bank, c2)
            for ap, p0, n in outs:
                t = dve(tt(ap, a_[p0:p0 + n, :], b_[p0:p0 + n, :], ALU.add), c1, c2, *free)
            tmp.give(a_, t)
            tmp.give(b_, t)
            return t

        def value_rows(bank, tok, out, rr, *free):
            q, f = tmp.take()
            if rr:
                a = dve(tt(q[:, :], bank[:, :], rr[0][:, :], ALU.mult), tok, f, rr[1])
            else:
                a = act(copy(q[:, :], bank[:, :]), tok, f)
            psum.give(bank, a)
            vb, vf = psum.take()
            for b in range(NB):
                t = op("pe", lambda e, b=b: e.transpose(vb[:, b * P:(b + 1) * P], q[:, b * P:(b + 1) * P], ident),
                       a, vf)
            tmp.give(q, t)
            v = dve(vcopy(out, vb[:, :].rearrange("p (b c) -> p b c", b=NB)), t, *free)
            psum.give(vb, v)
            return v

        sm_ring = Ring([sm[:, 8 * i:8 * i + 8] for i in range(12)])

        def attention(heads, blocks, mask, sink, outs, done, fill=None):
            jobs = [(h, b) for h in range(len(heads)) for b in range(NB)]
            st = [None] * len(jobs)
            obank = {}

            def score(n):
                h, b = jobs[n]
                q, k, v, tile, p0, tok = heads[h]
                k0, nk, c0 = blocks(b)
                w = nk * P
                bank, f = psum.take()
                t = op("pe", lambda e: e.matmul(bank[:, 0:w], q[:, b * P:(b + 1) * P], k[:, k0 * P:k0 * P + w],
                                                start=True, stop=True), f, tok)
                s, sf = tmp.take()
                c, cf = sm_ring.take()
                r = dve(lambda e: e.tensor_tensor_reduce(s[:, 0:w], bank[:, 0:w], mask[:, c0:c0 + w], 1.0, -3e38,
                                                         ALU.add, ALU.max, c[:, 0:1]), t, sf, cf)
                psum.give(bank, r)
                m = dve(ts(c[:, 1:2], c[:, 0:1], sink(h), -1.0, ALU.max, ALU.mult), r)
                x = act(lambda e: e.activation(s[:, 0:w], s[:, 0:w], ACT.Exp, bias=c[:, 1:2], accum_out=c[:, 2:3]), m)
                z = act(func(c[:, 3:4], sink(h), ACT.Exp, bias=c[:, 1:2]), m)
                d1 = dve(tt(c[:, 4:5], c[:, 2:3], c[:, 3:4], ALU.add), x, z)
                d2 = dve(lambda e: e.reciprocal(c[:, 5:6], c[:, 4:5]), d1)
                nrm = dve(ts(s[:, 0:w], s[:, 0:w], c[:, 5:6], None, ALU.mult), d2)
                sm_ring.give(c, nrm)
                st[n] = (s, nrm)

            def turn(n):
                h, b = jobs[n]
                k0, nk, c0 = blocks(b)
                s, tok = st[n]
                bank, f = psum.take()
                for i in range(nk):
                    t = op("pe", lambda e, i=i: e.transpose(bank[:, i * P:(i + 1) * P], s[:, i * P:(i + 1) * P], ident),
                           tok, f)
                tmp.give(s, t)
                pt, pf = tmp.take()
                c = act(copy(pt[:, 0:nk * P], bank[:, 0:nk * P]), t, pf)
                psum.give(bank, c)
                st[n] = (pt, c)

            def value(n):
                h, b = jobs[n]
                q, k, v, tile, p0, tok = heads[h]
                k0, nk, c0 = blocks(b)
                pt, tok = st[n]
                if tile not in obank:
                    obank[tile] = psum.take()
                bank, f = obank[tile]
                for i in range(nk):
                    t = op("pe", lambda e, i=i: e.matmul(bank[p0:p0 + 64, b * P:(b + 1) * P], v(k0 + i),
                                                         pt[:, i * P:(i + 1) * P], start=i == 0, stop=i == nk - 1),
                           tok, f)
                tmp.give(pt, t)
                if b == NB - 1 and (h == len(heads) - 1 or heads[h + 1][3] != tile):
                    psum.give(bank, outs(tile, bank, t))
                done[0] = t

            for n in range(len(jobs) + 2):
                if n < len(jobs):
                    score(n)
                if 1 <= n <= len(jobs):
                    turn(n - 1)
                if n >= 2:
                    value(n - 2)
                if fill:
                    fill(n)

        def to_hidden(tile0):
            def outs(tile, bank, t):
                s = tile0 + tile
                hi, lo = hid[s]
                r = split(hi, lo, bank[:, :], t, hid_free[s])
                hs[s] = (hi, lo, r)
                return r
            return outs

        hs = [None] * KD

        def out_project(w, take, fill=None):
            for m in range(KD):
                if fill:
                    fill(m)
                bank, t = project(w, m * P, hs)
                psum.give(bank, take(m, bank, t, True, True))
            for s in range(KD):
                hid_free[s] = t

        def m_enter():
            return [hid_free[s] for s in range(KD, 16)] + list(m_last)

        def m_leave(*toks):
            for s in range(KD, 16):
                hid_free[s] = toks
            m_last[0] = toks

        def conv(acc, src, taps, pad, bias, tok, *free):
            n, f = taps
            order = [pad] + [j for j in range(n) if j != pad]
            t = None
            for j in order:
                s = j - pad
                lo, hi = max(0, -s), min(T, T - s)
                o, i = acc[:, lo:hi], src[:, lo + s:hi + s]
                if t is None:
                    if bias is None:
                        t = dve(ts(o, i, f(j), None, ALU.mult), tok, *free)
                    else:
                        t = dve(ts(o, i, f(j), bias, ALU.mult, ALU.add), tok, *free)
                else:
                    t = dve(stt(o, i, f(j), o, ALU.mult, ALU.add), t)
                yield t

        def run_all(*gens):
            last = [None] * len(gens)
            live = list(range(len(gens)))
            while live:
                for g in list(live):
                    try:
                        last[g] = next(gens[g])
                    except StopIteration:
                        live.remove(g)
            return last

        def mixer1(l):
            w = ("w_in", l)
            menter = m_enter()
            yf = y_free[0]
            nxt = stream([(w, i * P) for i in (14, 12, 15, 13, 10, 11, 6, 7, 8, 9, 2, 4, 0, 3, 5, 1)], xs)
            nxt.start()
            z = lambda i: nxt()
            gens = []
            for i in range(2):
                gb, gt = z(14 + i)
                q, f = tmp.take()
                a = act(func(q[:, :], gb[:, :], ACT.Sigmoid), gt, f)
                psum.give(gb, a)
                ab, at = z(12 + i)
                u = dve(tt(Y[:, i, :], q[:, :], ab[:, :], ALU.mult), a, at, yf)
                psum.give(ab, u)
                tmp.give(q, u)
                gens.append(conv(Y[:, 2 + i, :], Y[:, i, :], (31, lambda j, i=i: vec("cc_conv_w", (l * 31 + j) * 2 + i)), 15,
                                 vec("cc_conv_b", l * 2 + i), u, yf))
            last = [None, None]

            def taps(n):
                for _ in range(n):
                    for i in range(2):
                        try:
                            last[i] = next(gens[i])
                        except StopIteration:
                            pass

            kb, kt = z(10)
            kd_t = rope(kb, kt, 1.0, [(M0[0:64, 4, :], 0, 64), (M0[64:128, 4, :], 0, 64),
                                      (M0[0:64, 5, :], 64, 64), (M0[64:128, 5, :], 64, 64)], menter)
            taps(4)
            vb, vt = z(11)
            vr = M0[:, 6, :].rearrange("p (b c) -> p b c", b=NB)
            v_t = value_rows(vb, vt, vr, None, menter)
            rest = center()
            taps(4)
            heads = []
            q_t = []
            for i in range(4):
                qb, qt = z(6 + i)
                q_t.append(rope(qb, qt, 0.125, [(M0[:, i, :], 0, P)], menter))
                if i == 1:
                    rest()
                taps(4)
            for h in range(8):
                p0 = 64 * (h % 2)
                g = h // 4
                heads.append((M0[p0:p0 + 64, h // 2, :], M0[p0:p0 + 64, 4 + g, :],
                              lambda b, g=g: vr[:, b, 64 * g:64 * g + 64], h // 2, p0, (kd_t, v_t, q_t[h // 2])))
            for i in range(2):
                cb, ct = z(2 + i)
                q, f = tmp.take()
                a = act(copy(q[:, :], cb[:, :]), ct, f)
                psum.give(cb, a)
                hb, ht = z(4 + i)
                p = dve(tt(M1[:, i, :], q[:, :], hb[:, :], ALU.mult), a, ht, menter)
                psum.give(hb, p)
                tmp.give(q, p)
                c, = run_all(conv(M1[:, 2 + i, :], M1[:, i, :],
                                  (3, lambda j, i=i: vec("sc_conv_w", (l * 3 + j) * 2 + i)), 1, None, p))
                bb, bt = z(i)
                x_used(bt)
                q, f = tmp.take()
                y = dve(tt(q[:, :], M1[:, 2 + i, :], bb[:, :], ALU.mult), c, bt, f)
                psum.give(bb, y)
                r = split(*hid[i], q[:, :], y, hid_free[i])
                hs[i] = hid[i] + (r,)
                tmp.give(q, r)
                taps(4)
            taps(31)
            done = [None]

            def cc_norm():
                def out(m, ap, s):
                    q, f = tmp.take()
                    a = act(func(q[:, :], ap, ACT.Silu, bias=vec("cc_ln_b", l * 2 + m), scale=vec("cc_ln_g", l * 2 + m)), s, f)
                    r = split(*hid[6 + m], q[:, :], a, hid_free[6 + m])
                    hs[6 + m] = hid[6 + m] + (r,)
                    tmp.give(q, r)
                    y_free[0] = r

                st = Stats(True)
                for i in range(2):
                    st.add(Y[:, 2 + i, :], last[i])
                (rb, rt), (mb, mt) = st.finish(2 * P, LN_EPS)
                for i in range(2):
                    ap = Y[:, 2 + i, :]
                    t = dve(tt(ap, ap, rb[:, :], ALU.mult), rt, last[i])
                    t = dve(tt(ap, ap, mb[:, :], ALU.subtract), t, mt)
                    out(i, ap, t)
                psum.give(rb, t)
                psum.give(mb, t)

            cc_norm()
            attention(heads, lambda b: (max(b - 1, 0), 3 - (b == 0) - (b == 3), P if b == 0 else 0), M1m,
                      lambda h: CT[:, C_SINK + l * 8 + h:C_SINK + l * 8 + h + 1], to_hidden(2), done)
            out_project(("w_out", l), add_residual)
            m_leave(done[0], r)

        def log1p(e_, out, n, w, tok):
            zt, f1 = tmp.take()
            z2, f2 = tmp.take()
            z, zz = zt[0:n, 0:w], z2[0:n, 0:w]
            t = dve(ts(z, e_, 2.0, None, ALU.add), tok, f1)
            t = dve(lambda v: v.reciprocal(z, z), t)
            t = dve(tt(z, z, e_, ALU.mult), t)
            t = dve(tt(zz, z, z, ALU.mult), t, f2)
            t = dve(ts(out, zz, 2.0 / 17, 2.0 / 15, ALU.mult, ALU.add), t)
            for k in (13, 11, 9, 7, 5, 3, 1):
                t = dve(tt(out, out, zz, ALU.mult), t)
                t = dve(ts(out, out, 2.0 / k, None, ALU.add), t)
            t = dve(tt(out, out, z, ALU.mult), t)
            tmp.give(zt, t)
            tmp.give(z2, t)
            return t

        def mixer2():
            w = ("ev_w_in_2", 0)
            menter = m_enter()
            yf = y_free[0]
            cols = [2048]
            for h in range(4):
                cols += [h * P, 512 + h * P, 1024 + h * P, 1536 + h * P, 2056 + h * P, 2568 + h * P]
            nxt = stream([(w, c) for c in cols], xs)
            nxt.start()
            rr, rrt = pre_scale()
            z = lambda c0: nxt()
            gb, gt = z(2048)
            G, f = tmp.take()
            t = dve(tt(G[0:8, :], gb[0:8, :], rr[0:8, :], ALU.mult), gt, f, rrt)
            psum.give(gb, t)
            t = dve(ts(G[0:8, :], G[0:8, :], VT[0:8, V_BI:V_BI + 1], None, ALU.add), t)
            fb, ff = psum.take()
            ft = op("pe", lambda e: e.matmul(fb[0:4, :], CT[0:8, C_ID + 4:C_ID + 8], G[0:8, :], start=True, stop=True),
                    t, ff)
            FP, f1 = tmp.take()
            t = dve(vcopy(FP[0:4, :], fb[0:4, :]), ft, f1)
            psum.give(fb, t)
            E_, f2 = tmp.take()
            t2 = dve(stt(E_[0:4, :], FP[0:4, :], -1.0, FP[0:4, :], ALU.mult, ALU.max), t, f2)
            t2 = act(func(E_[0:4, :], E_[0:4, :], ACT.Exp, scale=-1.0), t2)
            L_, f3 = tmp.take()
            t3 = log1p(E_[0:4, :], L_[0:4, :], 4, T, (t2, f3))
            t3 = dve(stt(L_[0:4, :], FP[0:4, :], 0.0, L_[0:4, :], ALU.min, ALU.subtract), t3)
            o1 = dve(lambda e: e.memset(E_[0:4, :], 1.0), t3)
            t3 = dve(lambda e: e.tensor_tensor_scan(FP[0:4, :], E_[0:4, :], L_[0:4, :], 0.0, ALU.mult, ALU.add), o1, t3)
            ta = dve(tt(G[0:4, :], G[0:4, :], FP[0:4, :], ALU.subtract), t3, ft)
            tM = dve(lambda e: e.tensor_tensor_scan(E_[0:4, :], G[0:4, :], G[0:4, :], 0.0, ALU.max, ALU.max), ta)
            t4 = dve(tt(L_[0:4, :], FP[0:4, :], E_[0:4, :], ALU.add), tM)
            tE = act(func(L_[0:4, :], L_[0:4, :], ACT.Exp, scale=-1.0), t4)
            tmp.give(FP, t4)
            cb, cf = psum.take()
            for b in range(NB):
                t = op("pe", lambda e, b=b: e.transpose(cb[:, 4 * b:4 * b + 4], G[0:4, b * P:(b + 1) * P],
                                                        CT[0:4, C_ID:C_ID + 4]), ta, cf)
            tmp.give(G, t)
            acol = sm[:, 96:112]
            tcol = dve(vcopy(acol, cb[:, 0:16]), t)
            psum.give(cb, tcol)

            rw, rf = tmp.take()
            rwa = dma("rga", rw[:, :].rearrange("p (n c) -> p n c", n=4), d["ev_rg_wa_2"][0].rearrange("n p c -> p n c"), rf)
            rx, rf = tmp.take()
            rwx = dma("rgb", rx[:, :].rearrange("p (n c) -> p n c", n=4), d["ev_rg_wx_2"][0].rearrange("n p c -> p n c"), rf)
            lam = VT[:, V_OFF["ev_rg_lambda_2"]:V_OFF["ev_rg_lambda_2"] + 4]
            s1, f = tmp.take()
            t = dve(stt(s1[:, 0:4], lam, -1.0, lam, ALU.mult, ALU.max), f)
            t = act(func(s1[:, 0:4], s1[:, 0:4], ACT.Exp, scale=-1.0), t)
            t = log1p(s1[:, 0:4], s1[:, 8:12], P, 4, t)
            t = dve(ts(s1[:, 16:20], lam, -1.0, 0.0, ALU.mult, ALU.max), t)
            t = dve(tt(s1[:, 8:12], s1[:, 8:12], s1[:, 16:20], ALU.add), t)
            tcs = dve(ts(sm[:, 112:116], s1[:, 8:12], 8.0, None, ALU.mult), t)
            tmp.give(s1, tcs)

            qkvo = []
            rec = []

            def lru(n):
                xb_, xt = z(2056 + n * P)
                x_t = dve(tt(Y[:, n, :], xb_[:, :], rr[:, :], ALU.mult), xt, yf, rrt)
                psum.give(xb_, x_t)
                xc, f = tmp.take()
                t, = run_all(conv(xc[:, :], Y[:, n, :], (4, lambda j: vec("ev_conv_w_2", j * 4 + n)), 3,
                                  vec("ev_conv_b_2", n), x_t, f))
                b1, f1 = psum.take()
                b2, f2 = psum.take()
                p1 = op("pe", lambda e: e.matmul(b1[:, :], rw[:, n * P:(n + 1) * P], xc[:, :], start=True, stop=True), t, f1, rwa)
                p2 = op("pe", lambda e: e.matmul(b2[:, :], rx[:, n * P:(n + 1) * P], xc[:, :], start=True, stop=True), t, f2, rwx)
                r_, f1 = tmp.take()
                i_, f2 = tmp.take()
                a1 = act(func(r_[:, :], b1[:, :], ACT.Sigmoid, bias=vec("ev_rg_ba_2", n)), p1, f1)
                a2 = act(func(i_[:, :], b2[:, :], ACT.Sigmoid, bias=vec("ev_rg_bx_2", n)), p2, f2)
                psum.give(b1, a1)
                psum.give(b2, a2)
                ix = dve(tt(i_[:, :], i_[:, :], xc[:, :], ALU.mult), a2)
                tmp.give(xc, ix)
                yy = dve(ts(r_[:, :], r_[:, :], sm[:, 112 + n:113 + n], None, ALU.mult), a1, tcs)
                th, f3 = tmp.take()
                at = act(func(th[:, :], r_[:, :], ACT.Tanh), yy, f3)
                ae = act(func(r_[:, :], r_[:, :], ACT.Exp, scale=-1.0), yy, at)
                dd, f4 = tmp.take()
                t = dve(ts(dd[:, :], th[:, :], 1.0, None, ALU.add), at, f4)
                t = dve(lambda e: e.reciprocal(dd[:, :], dd[:, :]), t)
                t = dve(stt(dd[:, :], dd[:, :], 2.0, th[:, :], ALU.mult, ALU.mult), t)
                tmp.give(th, t)
                t = act(func(dd[:, :], dd[:, :], ACT.Sqrt), t)
                t = dve(tt(i_[:, :], i_[:, :], dd[:, :], ALU.mult), t, ix)
                tmp.give(dd, t)
                t = dve(lambda e: e.tensor_tensor_scan(Y[:, n, :], r_[:, :], i_[:, :], 0.0, ALU.mult, ALU.add), t, ae)
                tmp.give(i_, t)
                tmp.give(r_, t)
                yb_, yt = z(2056 + 512 + n * P)
                g = dve(tt(Y[:, 4 + n, :], yb_[:, :], rr[:, :], ALU.mult), yt, yf, rrt)
                psum.give(yb_, g)
                g = act(func(Y[:, 4 + n, :], Y[:, 4 + n, :], ACT.Gelu_apprx_tanh), g)
                q, f = tmp.take()
                t = dve(tt(q[:, :], Y[:, n, :], Y[:, 4 + n, :], ALU.mult), t, g, f)
                r = split(*hid[4 + n], q[:, :], t, hid_free[4 + n])
                hs[4 + n] = hid[4 + n] + (r,)
                tmp.give(q, r)
                y_free[0] = t
                return p2, yt

            for h in range(4):
                qb, qt = z(h * P)
                tq = dve(tt(M0[:, h, :], qb[:, :], rr[:, :], ALU.mult), qt, menter, rrt)
                psum.give(qb, tq)
                kb, kt = z(512 + h * P)
                tk = dve(tt(M0[:, 4 + h, :], kb[:, :], rr[:, :], ALU.mult), kt, menter, rrt)
                psum.give(kb, tk)
                vb, vt = z(1024 + h * P)
                tv = value_rows(vb, vt, M1[:, h, :].rearrange("p (b c) -> p b c", b=NB), (rr, rrt), menter)
                ob, ot = z(1536 + h * P)
                to = dve(tt(M1[:, 4 + h, :], ob[:, :], rr[:, :], ALU.mult), ot, menter, rrt)
                psum.give(ob, to)
                to = act(func(M1[:, 4 + h, :], M1[:, 4 + h, :], ACT.Sigmoid), to)
                rec.append(lru(h))
                qkvo.append((tq, tk, tv, to))
            x_used(rec[-1][1])
            tmp.give(rr, y_free[0])
            tmp.give(rw, rec[-1][0])
            tmp.give(rx, rec[-1][0])

            SCL = float(128) ** -0.5
            def head(h):
                tq, tk, tv, to = qkvo[h]
                sel = CT[0:4, C_SEL + h * P:C_SEL + (h + 1) * P]
                mb, mf = psum.take()
                tm = op("pe", lambda e: e.matmul(mb[:, :], sel, E_[0:4, :], start=True, stop=True), tM, mf)
                eb, ef = psum.take()
                te = op("pe", lambda e: e.matmul(eb[:, :], sel, L_[0:4, :], start=True, stop=True), tE, ef)
                nb_, nf = psum.take()
                db_, df = psum.take()
                g2 = None
                for s in range(NB):
                    t0 = s * P
                    w_ = T - t0
                    sbk, sf = psum.take()
                    ts_ = op("pe", lambda e, s=s, t0=t0, w_=w_, sbk=sbk: e.matmul(
                        sbk[:, 0:w_], M0[:, 4 + h, t0:t0 + P], M0[:, h, t0:T], start=True, stop=True), tq, tk, sf)
                    ex, xf = tmp.take()
                    ac = acol[:, 4 * s + h:4 * s + h + 1]
                    g0 = dve(stt(ex[:, 0:P], mb[:, t0:t0 + P], -1.0, CAU, ALU.mult, ALU.add), tm, xf, g2)
                    g1 = act(func(ex[:, 0:P], ex[:, 0:P], ACT.Exp, bias=ac), g0, tcol)
                    if w_ > P:
                        g2 = act(func(ex[:, P:w_], mb[:, t0 + P:T], ACT.Exp, bias=ac, scale=-1.0), g0, tcol)
                    else:
                        g2 = g1
                    v = dve(stt(ex[:, 0:w_], sbk[:, 0:w_], SCL, ex[:, 0:w_], ALU.mult, ALU.mult), g1, g2, ts_)
                    psum.give(sbk, v)
                    vr = M1[:, h, t0:t0 + P]
                    tn = op("pe", lambda e, s=s, t0=t0, w_=w_, ex=ex, vr=vr: e.matmul(
                        nb_[:, t0:T], vr, ex[:, 0:w_], start=s == 0, stop=s == NB - 1), v, tv, nf)
                    td = op("pe", lambda e, s=s, t0=t0, w_=w_, ex=ex: e.matmul(
                        db_[:, t0:T], ones, ex[:, 0:w_], start=s == 0, stop=s == NB - 1), v, df)
                    tmp.give(ex, td)
                psum.give(mb, g1, g2)
                dn, f = tmp.take()
                a = act(func(dn[:, :], db_[:, :], ACT.Abs), td, f)
                psum.give(db_, a)
                v = dve(tt(dn[:, :], dn[:, :], eb[:, :], ALU.max), a, te)
                psum.give(eb, v)
                v = dve(lambda e, dn=dn: e.reciprocal(dn[:, :], dn[:, :]), v)
                v = dve(tt(dn[:, :], dn[:, :], nb_[:, :], ALU.mult), v, tn)
                psum.give(nb_, v)
                v = dve(tt(dn[:, :], dn[:, :], M1[:, 4 + h, :], ALU.mult), v, to)
                r = split(*hid[h], dn[:, :], v, hid_free[h])
                hs[h] = hid[h] + (r,)
                tmp.give(dn, r)
                return tm, te, td, r

            for h in range(4):
                tm, te, td, r = head(h)
            tmp.give(E_, tm)
            tmp.give(L_, te)
            m_leave(td, r)
            return ("ev_w_out_2", 0)

        def rope_tables(after):
            pi_, f = tmp.take()
            tp = dma("pos", pi_[:, :].bitcast(I32), d["pos"], f)
            an, f1 = tmp.take()
            k_, f2 = tmp.take()
            t = dve(vcopy(an[:, :], pi_[:, :].bitcast(I32)), tp, f1)
            t = dve(ts(an[:, :], an[:, :], CT[:, C_INV:C_INV + 1], None, ALU.mult), t, f2)
            c1, c2, c3 = two_pi_parts()
            big = 12582912.0
            for m in (4096.0, 1.0):
                t = dve(ts(k_[:, :], an[:, :], 1.0 / (2 * math.pi * m), big, ALU.mult, ALU.add), t)
                t = dve(ts(k_[:, :], k_[:, :], big, None, ALU.subtract), t)
                for c in (c1, c2, c3):
                    t = dve(stt(an[:, :], k_[:, :], -c * m, an[:, :], ALU.mult, ALU.add), t)
            lim = 3.1415925
            t = dve(ts(an[:, :], an[:, :], lim, -lim, ALU.min, ALU.max), t)
            t1 = dve(stt(k_[:, :], an[:, :], -1.0, an[:, :], ALU.mult, ALU.max), t)
            t1 = dve(ts(k_[:, :], k_[:, :], -1.0, 0.5 * math.pi, ALU.mult, ALU.add), t1)
            a1 = act(func(SIN, an[:, :], ACT.Sin), t, after)
            a2 = act(func(COS, k_[:, :], ACT.Sin), t1, after)
            for q in (1, 3):
                t = dve(ts(SIN[32 * q:32 * q + 32, :], SIN[32 * q:32 * q + 32, :], -1.0, None, ALU.mult), a1)
            tmp.give(pi_, t1)
            tmp.give(an, a1)
            tmp.give(k_, a2)
            return t, a2

        def two_pi_parts():
            v = 2 * math.pi
            out = []
            for _ in range(2):
                e = math.floor(math.log2(v))
                c = math.floor(v / 2.0 ** (e - 9)) * 2.0 ** (e - 9)
                out.append(c)
                v -= c
            return out + [v]

        rope_last = [()]

        def swa():
            w = ("od_w_qkv_2", 0)
            menter = m_enter()
            nxt = stream([(w, i * P) for i in (8, 9, 10, 11, 0, 1, 2, 3, 4, 5, 6, 7)], xs)
            nxt.start()
            rr, rrt = pre_scale()
            tab = rope_tables(rope_last[0])
            t1 = dve(tt(SIN, SIN, rr[:, :], ALU.mult), tab, rrt)
            t2 = dve(tt(COS, COS, rr[:, :], ALU.mult), tab, rrt)
            Q["dve"].append((None, [t1, t2], False))
            z = lambda i: nxt()
            kts, vts = [], []
            for i in range(2):
                kb, kt = z(8 + i)
                kts.append(rope(kb, kt, 1.0, [(M1[0:64, 2 * i, :], 0, 64), (M1[64:128, 2 * i, :], 0, 64),
                                              (M1[0:64, 2 * i + 1, :], 64, 64), (M1[64:128, 2 * i + 1, :], 64, 64)],
                                menter))
            for i in range(2):
                vb, vt = z(10 + i)
                vts.append(value_rows(vb, vt, M1[:, 4 + i, :].rearrange("p (b c) -> p b c", b=NB), (rr, rrt), menter))
            tmp.give(rr, vts[1])
            heads = []
            for i in range(8):
                qb, qt = z(i)
                x_used(qt)
                tq = rope(qb, qt, 0.125, [(M0[:, i, :], 0, P)], menter)
                for h in (2 * i, 2 * i + 1):
                    p0 = 64 * (h % 2)
                    g = h // 4
                    vr = M1[:, 4 + g // 2, :].rearrange("p (b c) -> p b c", b=NB)
                    heads.append((M0[p0:p0 + 64, i, :], M1[p0:p0 + 64, g, :],
                                  lambda b, g=g, vr=vr: vr[:, b, 64 * (g % 2):64 * (g % 2) + 64], i, p0,
                                  (kts[g // 2], vts[g // 2], tq)))
            done = [None]
            attention(heads, lambda b: (max(b - 1, 0), 2 - (b == 0), P if b == 0 else 0), M2m,
                      lambda h: CT[:, C_SINK + 16 + h:C_SINK + 17 + h], to_hidden(0), done)
            m_leave(done[0])
            return ("od_w_o_2", 0)

        def memory(l):
            menter = m_enter()
            box = {}
            mh = HHb[:, 0:4, :].rearrange("p a (b t) -> p (a b) t", b=2)
            ml = HHb[:, 4:8, :].rearrange("p a (b t) -> p (a b) t", b=2)
            KT = M1[:, 0:4, :].rearrange("p a (b t) -> p (a b) t", b=2)
            VR = M1[:, 4:8, :].rearrange("p (m a) t -> p m (a t)", m=2)
            kt, vt, ms = [], [], []

            def prepare(m):
                if m == 0:
                    box["raw"] = []
                    for i in range(4):
                        q, f = tmp.take()
                        src = d["memT"][2 * i * P:2 * (i + 1) * P, :].rearrange("(k p) t -> p k t", p=P)
                        box["raw"].append((q, dma(f"mm{i}", q[:, :].rearrange("p (k t) -> p k t", k=2), src, f)))
                if m == 1:
                    st = box["st"] = Stats(False)
                    for q, t in box["raw"]:
                        st.add(q[:, :], t)
                    s = st.s2
                    st.t2 = dve(tt(s[:, 0:256], s[:, 0:256], s[:, 256:512], ALU.add), st.t2)
                if m == 3:
                    (rb, rt), = box["st"].finish(D, RMS_EPS, 2)
                    for k in range(KD):
                        q, t = box["raw"][k // 2]
                        o = q[:, 256 * (k % 2):256 * (k % 2) + 256]
                        s = dve(stt(o, o, vec("g_mem_2", l * KD + k), rb[:, 0:256], ALU.mult, ALU.mult), rt, t)
                        c = split(mh[:, k, :], ml[:, k, :], o, s, menter)
                        ms.append((mh[:, k, :], ml[:, k, :], c))
                        if k % 2:
                            tmp.give(q, c)
                    psum.give(rb, s)

            w = ("w_xkv_2", l)

            def unit(i):
                m = i % KD
                if i < KD:
                    bank, t = project(w, m * P, ms)
                    kt.append(act(copy(KT[:, m, :], bank[:, 0:256]), t, menter))
                    psum.give(bank, kt[-1])
                    return
                s, ready = next_unit(w, D + m * P)
                bank, free = psum.take()
                for b in range(2):
                    for k, (h, lo, tok) in enumerate(ms):
                        t = op("pe", mm3(bank[:, b * P:(b + 1) * P], h[:, b * P:(b + 1) * P], lo[:, b * P:(b + 1) * P],
                                         wh[s][:, k, :], wl[s][:, k, :], k == 0, k == KD - 1), ready, free, tok)
                spl_free[s] = t
                vt.append(act(copy(VR[:, :, m * P:(m + 1) * P], bank[:, 0:256].rearrange("p (b c) -> p b c", b=2)), t,
                              menter))
                psum.give(bank, vt[-1])
                box["last"] = t

            return prepare, unit, (KT, VR, kt, vt, box)

        def cross(l, KT, VR, kt, vt, box):
            menter = [m_enter(), box["last"]]
            tq = []
            nxt = stream([(("w_xq_2", l), m * P) for m in range(KD)], xs)
            nxt.start()
            rr, rrt = pre_scale()
            for m in range(KD):
                bank, t = nxt()
                tq.append(dve(tt(M0[:, m, :], bank[:, :], rr[:, :], ALU.mult), t, menter, rrt))
                psum.give(bank, tq[-1])
            tmp.give(rr, tq[-1])
            x_used(t)
            st = {}
            pt_free = [y_free[0], y_free[0]]
            pts = {}
            SC = 1.0 / 16

            def score(h, b):
                bank, f = psum.take()
                for i in range(2):
                    t = op("pe", lambda e, i=i: e.matmul(bank[:, 0:256], M0[:, 2 * h + i, b * P:(b + 1) * P],
                                                         KT[:, 2 * h + i, :], start=i == 0, stop=i == 1),
                           f, tq[2 * h + i], kt[2 * h + i])
                s, sf = tmp.take()
                c, cf = sm_ring.take()
                r = dve(lambda e: e.tensor_reduce(c[:, 0:1], bank[:, 0:256], AX, ALU.max), t, cf)
                r = dve(ts(c[:, 1:2], c[:, 0:1], -SC, None, ALU.mult), r)
                x = act(lambda e: e.activation(s[:, 0:256], bank[:, 0:256], ACT.Exp, bias=c[:, 1:2], scale=SC,
                                               accum_out=c[:, 2:3]), r, sf)
                psum.give(bank, x)
                r = dve(lambda e: e.reciprocal(c[:, 3:4], c[:, 2:3]), x)
                r = dve(ts(s[:, 0:256], s[:, 0:256], c[:, 3:4], None, ALU.mult), r)
                sm_ring.give(c, r)
                st[h, b] = (s, r)

            def turn(h, b):
                s, tok = st.pop((h, b))
                bank, f = psum.take()
                for i in range(2):
                    t = op("pe", lambda e, i=i: e.transpose(bank[:, i * P:(i + 1) * P], s[:, i * P:(i + 1) * P], ident),
                           tok, f)
                tmp.give(s, t)
                o = 4 * (h % 2)
                c = act(copy(Y[:, o:o + 2, b * P:(b + 1) * P], bank[:, 0:256].rearrange("p (i q) -> p i q", i=2)), t,
                        pt_free[h % 2])
                psum.give(bank, c)
                pts[h] = c

            def value(h):
                o = 4 * (h % 2)
                for j in range(2):
                    bank, f = psum.take()
                    for i in range(2):
                        t = op("pe", lambda e, i=i, j=j, bank=bank: e.matmul(bank[:, :], VR[:, i, (2 * h + j) * P:(2 * h + j + 1) * P],
                                                             Y[:, o + i, :], start=i == 0, stop=i == 1),
                               f, pts[h], vt[2 * h + j])
                    s = 2 * h + j
                    hi, lo = hid[s]
                    r = split(hi, lo, bank[:, :], t, hid_free[s])
                    hs[s] = (hi, lo, r)
                    psum.give(bank, r)
                pt_free[h % 2] = t
                return t

            jobs = [(h, b) for h in range(4) for b in range(NB)]
            for n in range(len(jobs) + 1):
                if n < len(jobs):
                    score(*jobs[n])
                if n >= 1:
                    turn(*jobs[n - 1])
                if n >= NB and n % NB == 1 and n > NB:
                    value(n // NB - 1)
            t = value(3)
            y_free[0] = t
            m_leave(t)
            out_project(("w_xo_2", l), to_y)

        def first_ffn(l, n, ln):
            ffn((f"ffn{n}_w_gu", l), (f"ffn{n}_w_down", l), FF1 // P, True, add_residual)
            block_norm(l, ln)

        def first_mixer(l):
            mixer1(l)
            block_norm(l, "ln2")

        def second_mixer(l):
            if l == 0:
                rope_last[0] = ("dve", cnt["dve"])
                first_split("g_mix_pre_2", 0)
            w = mixer2() if l == 0 else swa()
            prepare, unit, kv = memory(l)
            out_project(w, to_y, prepare)
            unit(0)
            unit(1)

            def fill(m):
                if m < 7:
                    unit(2 * m + 2)
                    unit(2 * m + 3)

            post_norm("g_mix_post_2", l, ystats[0], ("g_x_pre_2", l), fill)
            second_cross(l, kv)

        def second_cross(l, kv):
            cross(l, *kv)
            post_norm("g_x_post_2", l, ystats[0], ("g_ff_pre_2", l))

        def second_ffn(l):
            ffn(("w_ff1_2", l), ("w_ff2_2", l), FF2 // P, False, to_y)
            post_norm("g_ff_post_2", l, ystats[0], ("g_mix_pre_2", 1) if l == 0 else None)

        steps = []
        for l in range(2):
            steps += [lambda l=l: first_ffn(l, 1, "ln1"), lambda l=l: first_mixer(l), lambda l=l: first_ffn(l, 2, "ln3")]
        for l in range(2):
            steps += [lambda l=l: second_mixer(l), lambda l=l: second_ffn(l)]
        for step in steps:
            step()
        oT = d["outT"].rearrange("(k p) t -> p k t", p=P)
        for m in range(KD):
            last = dma("out", oT[:, m, :], XR[:, m, :], xr_tok[m])
        Q["sp"].append((None, [last], False))

        if units_in is None:
            return units

        def emit(name, eng):
            seen = {}
            for fn, waits, inc in Q[name]:
                need = {}
                for s, v in waits:
                    need[s] = max(need.get(s, 0), v)
                for s, v in need.items():
                    if seen.get(s, 0) < v:
                        eng.wait_ge(sems[s], v)
                        seen[s] = v
                if fn is None:
                    continue
                ins = fn(eng)
                if inc:
                    ins.then_inc(sems[name], 1)

        block = es.enter_context(nc.Block())

        @block.sync
        def _(eng):
            emit("sp", eng)

        @block.scalar
        def _(eng):
            emit("act", eng)

        @block.vector
        def _(eng):
            emit("dve", eng)

        @block.gpsimd
        def _(eng):
            emit("pool", eng)

        @block.tensor
        def _(eng):
            emit("pe", eng)


def constants():
    c = np.zeros((P, C_W), np.float32)
    p = np.arange(P)
    c[:, C_ID:C_ID + P] = np.eye(P)
    c[:, C_ONE:C_ONE + P] = 1.0
    half = 32
    inv = np.power(np.float32(10000.0), -np.arange(half, dtype=np.float32) / np.float32(half)).astype(np.float32)
    ang = (np.arange(T, dtype=np.float32)[None, :] * inv[p % 32][:, None]).astype(np.float32).astype(np.float64)
    sign = np.where((p // 32) % 2 == 0, 1.0, -1.0)[:, None]
    c[:, C_COS:C_COS + T] = np.cos(ang)
    c[:, C_SIN:C_SIN + T] = np.sin(ang) * sign
    r, k = p[:, None], np.arange(P)[None, :]
    c[:, C_M1:C_M1 + P] = np.where(k >= r, 0.0, NEG)
    c[:, C_M1 + 2 * P:C_M1 + 3 * P] = np.where(k <= r, 0.0, NEG)
    c[:, C_M2:C_M2 + P] = np.where(k > r, 0.0, NEG)
    c[:, C_M2 + P:C_M2 + 2 * P] = np.where(k <= r, 0.0, NEG)
    for h in range(4):
        c[h, C_SEL + h * P:C_SEL + (h + 1) * P] = 1.0
    c[:, C_INV] = inv[p % 32]
    c[:, C_EPS] = LN_EPS
    c[:, C_EPS + 1] = RMS_EPS
    return c


_WEIGHTS = ["ffn1_w_gu", "ffn1_w_down", "w_in", "w_out", "ffn2_w_gu", "ffn2_w_down", "ev_w_in_2", "ev_rg_wa_2",
            "ev_rg_wx_2", "ev_w_out_2", "od_w_qkv_2", "od_w_o_2", "w_xq_2", "w_xkv_2", "w_xo_2", "w_ff1_2", "w_ff2_2",
            ]


def kernel(**inputs):
    import concourse.bacc as _bacc
    from concourse.bass_utils import run_bass_kernel_spmd as _run

    a = {n: np.ascontiguousarray(v) for n, v in inputs.items()}
    arrays = {n: a[n] for n in _WEIGHTS}
    arrays["xT"] = np.ascontiguousarray(a["x"][0].T)
    arrays["memT"] = np.ascontiguousarray(a["mem_2"][0].T)
    vecs = np.zeros((V_W, P), np.float32)
    for n, s in VEC_SIZES:
        vecs[V_OFF[n]:V_OFF[n] + s] = a[n].reshape(s, P)
    vecs[V_BI, 0:8] = a["ev_b_if_2"][0]
    arrays["vecs"] = np.ascontiguousarray(vecs.T)
    c = constants()
    c[:, C_SINK:C_SINK + 16] = a["attn_sink"].reshape(1, 16)
    c[:, C_SINK + 16:C_SINK + 32] = a["od_sinks_2"].reshape(1, 16)
    arrays["consts"] = c
    arrays["pos"] = np.ascontiguousarray(np.broadcast_to(a["positions_2"].reshape(1, T), (P, T)))

    def make():
        nc = _bacc.Bacc("TRN2", target_bir_lowering=False, num_devices=1)
        d = {}
        for n, v in arrays.items():
            d[n] = nc.dram_tensor(f"in_{n}", v.shape, mybir.dt.from_np(v.dtype), kind="ExternalInput").ap()
        d["outT"] = nc.dram_tensor("outT", (D, T), F32, kind="ExternalOutput").ap()
        return nc, d

    order = build(*make(), None)
    nc, d = make()
    build(nc, d, order)
    r = _run(nc, [{f"in_{n}": v for n, v in arrays.items()}], core_ids=[0])
    return np.ascontiguousarray(r.results[0]["outT"].T)[None]
```

```python
import math
from contextlib import ExitStack

import numpy as np
import concourse.bass as bass
from concourse import mybir

F32 = mybir.dt.float32
F32R = mybir.dt.float32r
I32 = mybir.dt.int32
ALU = mybir.AluOpType
ACT = mybir.ActivationFunctionType
AX = mybir.AxisListType.X

P = 128
T = 512
D = 1024
KD = 8
NB = 4
ALPHA = float(4.0 ** 0.25)
LN_EPS = 1e-5
RMS_EPS = 1e-6
NEG = -1e30
FF1 = 2816
FF2 = 4096

RAW = 3
SPL = 4
LEAD = 3
NTMP = 11
EVERY1 = 2.8
EVERY2 = 2
EVERY3 = 4
DELAY3 = 4
DELAY1 = 8
DELAY2 = 4

C_ID = 0
C_ONE = 128
C_COS = 256
C_SIN = 768
C_M1 = 1280
C_M2 = 1664
C_SEL = 1920
C_INV = 2432
C_EPS = 2433
C_SINK = 2436
C_W = 2468

VEC_SIZES = [("ln1_g", 16), ("ln1_b", 16), ("ln2_g", 16), ("ln2_b", 16), ("ln3_g", 16), ("ln3_b", 16),
             ("sc_conv_w", 12), ("cc_conv_w", 124), ("cc_conv_b", 4), ("cc_ln_g", 4), ("cc_ln_b", 4),
             ("g_mix_pre_2", 16), ("g_mix_post_2", 16), ("g_x_pre_2", 16), ("g_x_post_2", 16), ("g_mem_2", 16),
             ("g_ff_pre_2", 16), ("g_ff_post_2", 16), ("ev_conv_w_2", 16), ("ev_conv_b_2", 4),
             ("ev_rg_ba_2", 4), ("ev_rg_bx_2", 4), ("ev_rg_lambda_2", 4)]
V_OFF = {}
V_W = 0
for _n, _s in VEC_SIZES:
    V_OFF[_n] = V_W
    V_W += _s
V_BI = V_W
V_W += 2


class Ring:

    def __init__(self, items):
        self.q = [(i, ()) for i in items]

    def take(self):
        return self.q.pop(0)

    def give(self, item, *toks):
        self.q.append((item, toks))


def build(nc, d, units_in):
    units = []
    es = ExitStack()
    with es:
        def sb(name, shape, dt=F32):
            return es.enter_context(nc.sbuf_tensor(name, shape, dt))

        XR = sb("XR", [P, KD, T])
        with nc.sbuf_tensor("XH", [P, KD, T], F32R) as XH:
            pass
        XM = sb("XM", [P, KD, T])
        XL = sb("XL", [P, KD, T], F32R)
        Y = sb("Y", [P, KD, T])
        HHa = sb("HHa", [P, KD, T], F32R)
        HLa = sb("HLa", [P, KD, T], F32R)
        with nc.sbuf_tensor("HHb", [P, KD, T], F32R) as HHb, nc.sbuf_tensor("HLb", [P, KD, T], F32R) as HLb:
            pass
        M0 = sb("M0", [P, KD, T])
        M1 = sb("M1", [P, KD, T])
        raw = [sb(f"raw{i}", [P, KD, P]) for i in range(RAW)]
        wh = [sb(f"wh{i}", [P, KD, P], F32R) for i in range(SPL)]
        wl = [sb(f"wl{i}", [P, KD, P], F32R) for i in range(SPL)]
        tmps = [sb(f"tmp{i}", [P, T]) for i in range(NTMP)]
        CT = sb("CT", [P, C_W])
        VT = sb("VT", [P, V_W])
        sm = sb("sm", [P, 128])
        sts = [sb(f"st{i}", [P, 32]) for i in range(2)]
        banks = [es.enter_context(nc.psum_tensor(f"ps{i}", [P, T], F32)) for i in range(8)]

        sems = {}

        def sem(name):
            if name not in sems:
                sems[name] = es.enter_context(nc.semaphore(name))
            return sems[name]

        for n in ("pe", "act", "dve", "pool", "ld", "ct", "mm", "out", "rga", "rgb", "pos"):
            sem(n)
        for i in range(RAW):
            sem(f"w{i}")

        Q = {e: [] for e in ("pe", "act", "dve", "pool", "sp")}
        cnt = {e: 0 for e in Q}

        def flat(ts):
            for t in ts:
                if not t:
                    continue
                if isinstance(t[0], str):
                    yield t
                else:
                    yield from flat(t)

        def op(e, fn, *after):
            cnt[e] += 1
            Q[e].append((fn, list(flat(after)), True))
            return (e, cnt[e])

        def quiet(e, fn, *after):
            Q[e].append((fn, list(flat(after)), False))

        def dve(fn, *a):
            return op("dve", fn, *a)

        def act(fn, *a):
            return op("act", fn, *a)

        def pool(fn, *a):
            return op("pool", fn, *a)

        dma_n = {}

        def dma(name, out, src, *after):
            dma_n[name] = dma_n.get(name, 0) + 16
            s = sem(name)
            quiet("sp", lambda e: e.dma_start(out, src).then_inc(s, 16), *after)
            return (name, dma_n[name])

        psum = Ring(banks)
        tmp = Ring(tmps)
        st_ring = Ring(sts)

        def copy(out, in_):
            return lambda e: e.activation(out, in_, ACT.Copy)

        def vcopy(out, in_):
            return lambda e: e.tensor_copy(out, in_)

        def func(out, in_, f, **kw):
            return lambda e: e.activation(out, in_, f, **kw)

        def tt(out, a, b, o):
            return lambda e: e.tensor_tensor(out, a, b, o)

        def ts(out, a, s1, s2, o0, o1=None):
            if o1 is None:
                return lambda e: e.tensor_scalar(out, a, s1, None, o0)
            return lambda e: e.tensor_scalar(out, a, s1, s2, o0, o1)

        def stt(out, a, s, b, o0, o1):
            return lambda e: e.scalar_tensor_tensor(out=out, in0=a, scalar=s, in1=b, op0=o0, op1=o1)

        def f32(ap):
            return ap.bitcast(F32)

        raw_free = [()] * RAW
        spl_free = [()] * SPL
        loaded, split_at, ptr = [], [], [0]

        def load_unit(i):
            name, l, k0, nk, c0 = units_in[i]
            s = i % RAW
            src = d[name][l][k0 * P:(k0 + nk) * P, c0:c0 + P].rearrange("(k p) c -> p k c", p=P)
            loaded.append(dma(f"w{s}", raw[s][:, 0:nk, :], src, raw_free[s]))

        def split_unit(i):
            nk = units_in[i][3]
            r, s = i % RAW, i % SPL
            hi = act(copy(wh[s][:, 0:nk, :], raw[r][:, 0:nk, :]), loaded[i], spl_free[s])
            lo = dve(tt(wl[s][:, 0:nk, :], raw[r][:, 0:nk, :], f32(wh[s][:, 0:nk, :]), ALU.subtract), hi)
            raw_free[r] = lo
            split_at.append(lo)

        def next_unit(w, c0, k0=0, nk=KD, base=None):
            i = ptr[0]
            base = i if base is None else base
            ptr[0] += 1
            if units_in is None:
                units.append((*w, k0, nk, c0))
                return i % SPL, ("dve", 1)
            n = len(units_in)
            while len(split_at) < min(n, base + SPL):
                while len(loaded) < min(n, len(split_at) + RAW):
                    load_unit(len(loaded))
                split_unit(len(split_at))
            while len(loaded) < min(n, len(split_at) + RAW):
                load_unit(len(loaded))
            return i % SPL, split_at[i]

        def mm3(out, lh, ll, rh, rl, start, stop):
            def f(e):
                e.matmul(out, lh, rh, start=start, stop=False)
                e.matmul(out, lh, rl, start=False, stop=False)
                return e.matmul(out, ll, rh, start=False, stop=stop)
            return f

        def two(out, lh, ll, rh, start):
            def f(e):
                e.matmul(out, lh, rh, start=start, stop=False)
                e.matmul(out, ll, rh, start=False, stop=False)
            return f

        def one(out, l, r, stop):
            return lambda e: e.matmul(out, l, r, start=False, stop=stop)

        filler = [None, 1, 0]

        def fill_with(gen, every, delay=0):
            filler[:] = [gen, every, -delay]

        def tick(n=1):
            if filler[0]:
                filler[2] += n
                if filler[2] >= filler[1]:
                    filler[2] -= filler[1]
                    next(filler[0], None)

        def drain():
            if filler[0]:
                for _ in filler[0]:
                    pass
            filler[0] = None

        def project_group(cols, xs, k0=0, order=None):
            nk = len(xs)
            base = ptr[0]
            n = next((x[0].shape[-1] for x in xs if x), T)
            us = [next_unit(w, c0, k0, nk, base) + psum.take() for w, c0 in cols]
            out = []
            for n_k, k in enumerate(order or range(nk)):
                if xs[k] is None:
                    drain()
                h, l, tok = xs[k][:3]
                htok = xs[k][-1]
                for s, ready, bank, free in us:
                    o = bank[:, 0:n]
                    f = two(o, wh[s][:, k, :], wl[s][:, k, :], h, n_k == 0)
                    quiet("pe", f, *((ready, free, htok) if n_k == 0 else (htok,)))
                for s, ready, bank, free in us:
                    last = n_k == nk - 1
                    f = one(bank[:, 0:n], wh[s][:, k, :], l, last)
                    if not last:
                        quiet("pe", f, tok)
                    else:
                        done = op("pe", f, tok)
                        spl_free[s] = done
                        out.append((bank, done))
                tick(n / T * len(us))
            return out

        def project(w, c0, xs, k0=0):
            return project_group([(w, c0)], xs, k0)[0]

        def stream(cols, xs):
            todo = list(cols)
            got = []

            def start(order=None):
                lead = todo[:LEAD]
                got.extend(project_group(lead, xs, 0, order))

            def nxt():
                if not got:
                    got.extend(project_group(todo[:1], xs))
                todo.pop(0)
                return got.pop(0)

            nxt.start = start
            return nxt

        def split(hi, lo, src, *after):
            a = act(copy(hi, src), *after)
            return dve(tt(lo, src, f32(hi), ALU.subtract), a)

        xT = d["xT"].rearrange("(k p) t -> p k t", p=P)
        t_x = []
        for k in range(KD):
            if units_in is not None and k in (0, 2, 4):
                load_unit(k // 2)
            t_x.append(dma(f"x{k}", XR[:, k, :], xT[:, k, :]))
        ident = CT[:, C_ID:C_ID + P]
        ones = CT[:, C_ONE:C_ONE + P]
        COS = CT[:, C_COS:C_COS + T]
        SIN = CT[:, C_SIN:C_SIN + T]
        M1m = CT[:, C_M1:C_M1 + 384]
        M2m = CT[:, C_M2:C_M2 + 256]
        CAU = CT[:, C_M1:C_M1 + P]

        def eps(v):
            c = {LN_EPS: C_EPS, RMS_EPS: C_EPS + 1}[v]
            return CT[:, c:c + 1]

        def vec(name, i):
            return VT[:, V_OFF[name] + i:V_OFF[name] + i + 1]

        xr_tok = list(t_x)
        x_free = [()] * KD
        xs = [None] * KD

        def split_x(k, src, *after):
            t = split(XH[:, k, :], XL[:, k, :], src, x_free[k], *after)
            xs[k] = (XH[:, k, :], XL[:, k, :], t)
            return t

        for k in range(KD):
            if units_in is not None and k in (0, 2, 4):
                split_unit(k // 2)
            split_x(k, XR[:, k, :], t_x[k])
        t_ct = [dma("ct", CT[:, :], d["consts"]), dma("ct", VT[:, :], d["vecs"])][-1]

        hid = [(HHa[:, i, :], HLa[:, i, :]) for i in range(KD)] + [(HHb[:, i, :], HLb[:, i, :]) for i in range(KD)]
        hid_free = [()] * 16
        m_last = [()]

        class Stats:

            def __init__(self, mean):
                self.mean, self.n, self.t1, self.t2 = mean, 0, None, None
                self.s2, self.f2 = tmp.take()
                if mean:
                    self.s1, self.f1 = tmp.take()

            def add(self, ap, tok, eng="dve"):
                self.n += 1
                if self.n == 1:
                    self.t2 = act(func(self.s2[:, :], ap, ACT.Square), tok, self.f2)
                    self.first = (ap, tok)
                    self.tail = None
                    return
                q, f = tmp.take()
                a = act(func(q[:, :], ap, ACT.Square), tok, f)
                self.fold(eng)
                self.tail = (ap, tok, q, a)

            def fold(self, eng):
                if self.tail is None:
                    return
                ap, tok, q, a = self.tail
                if self.mean:
                    x = self.first if self.t1 is None else (self.s1[:, :], self.t1)
                    self.t1 = pool(tt(self.s1[:, :], x[0], ap, ALU.add), x[1], tok, self.f1)
                self.t2 = op(eng, tt(self.s2[:, :], self.s2[:, :], q[:, :], ALU.add), a, self.t2)
                tmp.give(q, self.t2)
                self.tail = None

            def finish(self, n, e, blocks=NB):
                steps = self.finish_steps(n, e, blocks)
                while True:
                    try:
                        next(steps)
                    except StopIteration as r:
                        return r.value

            def finish_steps(self, n, e, blocks=NB):
                tb, bf = psum.take()
                ap, tok, q, a = self.tail or (None,) * 4
                one = ones[:, 0:1]
                nt = 1 if q is None else 2

                def sums(at, i, x, tk):
                    for b in range(blocks):
                        o = nt * (at + b) + i
                        t = op("pe", lambda v, b=b, o=o: v.matmul(tb[:, o:o + 1], x[:, b * P:(b + 1) * P], one,
                                                                  start=True, stop=True), tk, bf)
                    return t

                if self.mean:
                    x = (self.s1, self.t1) if self.t1 else self.first
                    t = sums(NB, 0, *x)
                    tmp.give(self.s1, t)
                t = sums(0, 0, self.s2, self.t2)
                tmp.give(self.s2, t)
                if q is not None:
                    if self.mean:
                        sums(NB, 1, ap, tok)
                    t = sums(0, 1, q, a)
                    tmp.give(q, t)
                c, cf = st_ring.take()
                w = blocks
                yield
                g = 2 * NB if self.mean else w
                z = dve(lambda v: v.tensor_reduce(c[:, 24:24 + g], tb[:, 0:nt * g].rearrange("p (g i) -> p g i", i=nt), AX,
                                                  ALU.add), t, cf)
                psum.give(tb, z)
                if self.mean:
                    m = dve(ts(c[:, 8:8 + w], c[:, 28:28 + w], 1.0 / n, None, ALU.mult), z)
                    v = dve(stt(c[:, 12:12 + w], c[:, 8:8 + w], -1.0, c[:, 8:8 + w], ALU.mult, ALU.mult), m)
                    v = dve(stt(c[:, 16:16 + w], c[:, 24:24 + w], 1.0 / n, c[:, 12:12 + w], ALU.mult, ALU.add), v)
                    v = dve(ts(c[:, 16:16 + w], c[:, 16:16 + w], 0.0, None, ALU.max), v)
                    a = act(func(c[:, 0:w], c[:, 16:16 + w], ACT.Sqrt, bias=eps(e)), v)
                else:
                    a = act(func(c[:, 0:w], c[:, 24:24 + w], ACT.Sqrt, bias=eps(e), scale=1.0 / n), z)
                r = dve(lambda v: v.reciprocal(c[:, 4:4 + w], c[:, 0:w]), a)
                parts = [(4, r)]
                if self.mean:
                    parts.append((20, dve(tt(c[:, 20:20 + w], c[:, 8:8 + w], c[:, 4:4 + w], ALU.mult), r)))
                out = []
                yield
                for o, tok in parts:
                    bank, bf = psum.take()
                    for b in range(blocks):
                        t = op("pe", lambda v, b=b, o=o, bank=bank: v.matmul(
                            bank[:, b * P:(b + 1) * P], c[:, o + b:o + b + 1].to_broadcast([P, P]), ident, start=True,
                            stop=True), tok, bf)
                    out.append((bank, t))
                st_ring.give(c, t)
                return out

        def center():
            s, f = tmp.take()
            t = dve(tt(s[:, :], XR[:, 0, :], XR[:, 1, :], ALU.add), xr_tok[0], xr_tok[1], f)
            for m in range(2, KD):
                yield
                t = dve(tt(s[:, :], s[:, :], XR[:, m, :], ALU.add), t, xr_tok[m])
            for _ in range(3):
                yield
            bank, bf = psum.take()
            p = op("pe", lambda e: e.matmul(bank[:, :], ones, s[:, :], start=True, stop=True), t, bf)
            tmp.give(s, p)
            for m in range(KD):
                yield
                xr_tok[m] = dve(stt(XR[:, m, :], bank[:, :], -1.0 / D, XR[:, m, :], ALU.mult, ALU.add), p, xr_tok[m])
            psum.give(bank, xr_tok[KD - 1])

        stats = [None]

        def block_norm(l, which, nxt=None):
            (rb, rt), (mb, mt) = stats[0].finish(D, LN_EPS)
            if nxt:
                stats[0] = Stats(False)
            pend = None
            for m in range(KD + 1):
                if m < KD:
                    q, f = tmp.take()
                    t = dve(tt(q[:, :], XR[:, m, :], rb[:, :], ALU.mult), rt, f, xr_tok[m])
                    t = dve(tt(q[:, :], q[:, :], mb[:, :], ALU.subtract), t, mt)
                    if nxt is None:
                        h = act(func(XH[:, m, :], q[:, :], ACT.Identity, bias=vec(f"{which}_b", l * KD + m),
                                     scale=vec(f"{which}_g", l * KD + m)), t, x_free[m])
                    x = act(func(XR[:, m, :], q[:, :], ACT.Identity, bias=vec(f"{which}_b", l * KD + m),
                                 scale=vec(f"{which}_g", l * KD + m)), t)
                    tmp.give(q, x)
                    if nxt:
                        xr_tok[m] = x
                        h = scaled_split(m, *nxt)
                    else:
                        h = (h, x)
                if pend is not None and nxt:
                    pend[1]()
                elif pend is not None:
                    k, hk = pend
                    xr_tok[k] = dve(tt(XL[:, k, :], XR[:, k, :], f32(XH[:, k, :]), ALU.subtract), hk, x_free[k])
                    xs[k] = (XH[:, k, :], XL[:, k, :], xr_tok[k], hk[0])
                pend = (m, h)
            psum.give(rb, t)
            psum.give(mb, t)

        def scaled_split(m, name, l):
            g = vec(name, l * KD + m)
            h = act(func(XH[:, m, :], XR[:, m, :], ACT.Copy, scale=g), xr_tok[m], x_free[m])

            def lo():
                stats[0].add(XR[:, m, :], xr_tok[m], "pool")
                t = dve(stt(XL[:, m, :], XR[:, m, :], g, f32(XH[:, m, :]), ALU.mult, ALU.subtract), h, x_free[m])
                xs[m] = (XH[:, m, :], XL[:, m, :], t, h)
            return lo

        y_free = [()]

        def post_norm(name, l, ystats, nxt):
            (rb, rt), = ystats.finish(D, RMS_EPS)
            if nxt:
                stats[0] = Stats(False)
            pend = None
            for m in range(KD + 1):
                if m < KD:
                    s = dve(stt(Y[:, m, :], Y[:, m, :], vec(name, l * KD + m), rb[:, :], ALU.mult, ALU.mult), rt, ys[m])
                if pend:
                    pend()
                if m < KD:
                    xr_tok[m] = dve(tt(XR[:, m, :], XR[:, m, :], Y[:, m, :], ALU.add), s, xr_tok[m])
                    pend = scaled_split(m, *nxt) if nxt else None
            psum.give(rb, s)
            y_free[0] = xr_tok[KD - 1]

        def pre_scale():
            (rb, rt), = stats[0].finish(D, RMS_EPS)
            rr, f = tmp.take()
            t = act(copy(rr[:, :], rb[:, :]), rt, f)
            psum.give(rb, t)
            return rr, t

        t_met = [None]
        tables = [None]

        def ffn(w_up, w_down, nf, gated, take, extra=None):
            chunks = [range(c, min(c + KD, nf)) for c in range(0, nf, KD)]
            ready = [None] * nf
            cols = []
            for j in range(nf):
                cols.append((w_up, j * P))
                if gated:
                    cols.append((w_up, nf * P + j * P))
            nxt = stream(cols, xs)
            nxt.start()
            if t_met[0] is None:
                for e in ("pe", "act", "dve", "pool"):
                    Q[e].append((None, [t_ct], False))
                t_met[0] = True
            rr, rt = (None, None) if gated else pre_scale()
            side = center() if gated else None
            rr_used = [None]

            def up(c):
                for j in chunks[c]:
                    s = (c % 2) * KD + j % KD
                    hi, lo = hid[s]
                    h, f2 = tmp.take()
                    q, f1 = tmp.take()
                    if gated:
                        gb, gt = nxt()
                        a = act(func(q[:, :], gb[:, :], ACT.Silu), gt, f1)
                        psum.give(gb, a)
                        ub, ut = nxt()
                        v = dve(stt(h[:, :], q[:, :], 0.5, ub[:, :], ALU.mult, ALU.mult), a, ut, f2)
                        psum.give(ub, v)
                    else:
                        ub, ut = nxt()
                        v = dve(stt(q[:, :], ub[:, :], 0.0, rr[:, :], ALU.max, ALU.mult), ut, f1, rt)
                        rr_used[0] = v
                        psum.give(ub, v)
                        v = act(func(h[:, :], q[:, :], ACT.Square), v, f2)
                    tmp.give(q, v)
                    ready[j] = split(hi, lo, h[:, :], v, hid_free[s])
                    tmp.give(h, ready[j])
                    if tables[0]:
                        next(tables[0], None)
                    if c == 1 and extra:
                        next(extra, None)
                    if gated and c == 0:
                        for _ in range(3):
                            next(side, None)
                for k in range(KD):
                    x_free[k] = ut

            def down(c):
                src = [hid[(c % 2) * KD + j % KD] + (ready[j],) for j in chunks[c]]
                for m in range(KD):
                    bank, t = project(w_down, m * P, src, k0=chunks[c][0])
                    psum.give(bank, take(m, bank, t, c == 0, c == len(chunks) - 1))
                for j in chunks[c]:
                    hid_free[(c % 2) * KD + j % KD] = t

            for c in range(len(chunks)):
                up(c)
                if c:
                    down(c - 1)
            if not gated:
                tmp.give(rr, rr_used[0])
            down(len(chunks) - 1)

        def add_residual(m, bank, t, first, last):
            if last and m > 1:
                stats[0].fold("dve")
            if first:
                xr_tok[m] = dve(stt(XR[:, m, :], XR[:, m, :], ALPHA, bank[:, :], ALU.mult, ALU.add), t, xr_tok[m])
            else:
                xr_tok[m] = dve(tt(XR[:, m, :], XR[:, m, :], bank[:, :], ALU.add), t, xr_tok[m])
            done = xr_tok[m]
            if last:
                if m == 0:
                    stats[0] = Stats(True)
                stats[0].add(XR[:, m, :], xr_tok[m])
            return done

        ys = [None] * KD
        ystats = [None]

        def to_y(m, bank, t, first, last):
            if last and m > 1:
                ystats[0].fold("dve")
            if first:
                ys[m] = dve(vcopy(Y[:, m, :], bank[:, :]), t, y_free[0])
            else:
                ys[m] = dve(tt(Y[:, m, :], Y[:, m, :], bank[:, :], ALU.add), t, ys[m])
            if last:
                if m == 0:
                    ystats[0] = Stats(False)
                ystats[0].add(Y[:, m, :], ys[m])
            return ys[m]

        def x_used(t):
            for k in range(KD):
                x_free[k] = t

        def rope(bank, tok, scale, outs, *free):
            a_, f1 = tmp.take()
            b_, f2 = tmp.take()
            for q in range(4):
                o = 32 * q
                i = 32 * (q ^ 1)
                sw = act(copy(b_[o:o + 32, :], bank[i:i + 32, :]), tok, f2)
            c1 = dve(stt(a_[:, :], bank[:, :], scale, COS, ALU.mult, ALU.mult), sw, f1)
            psum.give(bank, c1)
            c2 = dve(stt(b_[:, :], b_[:, :], scale, SIN, ALU.mult, ALU.mult), sw)
            t = [op("pool" if i > 1 else "dve", tt(ap, a_[p0:p0 + n, :], b_[p0:p0 + n, :], ALU.add), c1, c2, *free)
                 for i, (ap, p0, n) in enumerate(outs)]
            tmp.give(a_, *t)
            tmp.give(b_, *t)
            return t

        def value_rows(bank, tok, out, rr, *free):
            q, f = tmp.take()
            if rr:
                a = dve(tt(q[:, :], bank[:, :], rr[0][:, :], ALU.mult), tok, f, rr[1])
            else:
                a = act(copy(q[:, :], bank[:, :]), tok, f)
            psum.give(bank, a)

            def rest():
                vb, vf = psum.take()
                for b in range(NB):
                    t = op("pe", lambda e, b=b: e.transpose(vb[:, b * P:(b + 1) * P], q[:, b * P:(b + 1) * P], ident),
                           a, vf)
                tmp.give(q, t)
                v = dve(vcopy(out, vb[:, :].rearrange("p (b c) -> p b c", b=NB)), t, *free)
                psum.give(vb, v)
                return v
            return rest

        def lend(aps, *toks):
            for a in aps:
                tmp.give(a, *toks)

        def reclaim(aps):
            ids = [id(a) for a in aps]
            got = [t for a, t in tmp.q if id(a) in ids]
            assert len(got) == len(aps)
            tmp.q = [x for x in tmp.q if id(x[0]) not in ids]
            return got

        sm_ring = Ring([sm[:, 24 * i:24 * i + 24] for i in range(4)])

        def attention(heads, H, blocks, mask, sink, outs, done, on_act=False):
            S, C, N, PT, obank = {}, {}, {}, {}, {}
            NORM, TURN, VALUE = 5, 7, 9

            def score(h, b):
                q, k, v, tile, p0, tok, vtok = heads[h]
                k0, nk, c0 = blocks(b)
                w = nk * P
                if b == 0:
                    C[h] = sm_ring.take()
                c, cf = C[h]
                bank, f = psum.take()
                t = op("pe", lambda e: e.matmul(bank[:, 0:w], q[:, b * P:(b + 1) * P], k[:, k0 * P:k0 * P + w],
                                                start=True, stop=True), f, tok)
                s, sf = tmp.take()
                r = dve(lambda e: e.tensor_tensor_reduce(s[:, 0:w], bank[:, 0:w], mask[:, c0:c0 + w], 1.0, -3e38,
                                                         ALU.add, ALU.max, c[:, b:b + 1]), t, sf, cf)
                psum.give(bank, r)
                S[h, b] = (s, r)

            def exps(h):
                c, cf = C[h]
                m = dve(ts(c[:, 4:8], c[:, 0:4], sink(h), -1.0, ALU.max, ALU.mult), S[h, NB - 1][1])
                z = act(func(c[:, 12:16], c[:, 4:8], ACT.Exp, bias=sink(h)), m)
                for b in range(NB):
                    w = blocks(b)[1] * P
                    s, r = S[h, b]
                    x = act(lambda e, s=s, w=w, b=b: e.activation(s[:, 0:w], s[:, 0:w], ACT.Exp, bias=c[:, 4 + b:5 + b],
                                                                 accum_out=c[:, 8 + b:9 + b]), m)
                S[h] = (z, x)

            def norm(h, b):
                c, cf = C[h]
                if b == 0:
                    t = dve(tt(c[:, 16:20], c[:, 8:12], c[:, 12:16], ALU.add), S[h])
                    S[h] = dve(lambda e: e.reciprocal(c[:, 20:24], c[:, 16:20]), t)
                w = blocks(b)[1] * P
                s, r = S[h, b]
                if on_act:
                    n = act(func(s[:, 0:w], s[:, 0:w], ACT.Copy, scale=c[:, 20 + b:21 + b]), S[h])
                else:
                    n = dve(ts(s[:, 0:w], s[:, 0:w], c[:, 20 + b:21 + b], None, ALU.mult), S[h])
                N[h] = N.get(h, ()) + (n,)
                if b == NB - 1:
                    sm_ring.give(c, *N.pop(h))
                S[h, b] = (s, n)

            def turn(h, b):
                w = blocks(b)[1] * P
                s, n = S.pop((h, b))
                bank, f = psum.take()
                for i in range(w // P):
                    t = op("pe", lambda e, i=i: e.transpose(bank[:, i * P:(i + 1) * P], s[:, i * P:(i + 1) * P], ident),
                           n, f)
                tmp.give(s, t)
                pt, pf = tmp.take()
                cp = act(copy(pt[:, 0:w], bank[:, 0:w]), t, pf)
                psum.give(bank, cp)
                PT[h, b] = (pt, cp)

            def value(h, b):
                q, k, v, tile, p0, tok, vtok = heads[h]
                k0, nk, c0 = blocks(b)
                pt, cp = PT.pop((h, b))
                if tile not in obank:
                    obank[tile] = psum.take()
                bank, f = obank[tile]
                for i in range(nk):
                    t = op("pe", lambda e, i=i: e.matmul(bank[p0:p0 + 64, b * P:(b + 1) * P], v(k0 + i),
                                                         pt[:, i * P:(i + 1) * P], start=i == 0, stop=i == nk - 1),
                           cp, f, vtok[0][vtok[1]])
                tmp.give(pt, t)
                if b == NB - 1 and (h == H - 1 or heads[h + 1][3] != tile):
                    psum.give(bank, outs(tile, bank, t))
                done[0] = t

            for n in range(H * NB + VALUE):
                while n < H * NB and len(heads) <= n // NB:
                    yield
                for lag, f in ((NORM, norm), (VALUE, value), (0, score), (TURN, turn)):
                    if 0 <= n - lag < H * NB:
                        f(*divmod(n - lag, NB))
                if n < H * NB and n % NB == NB - 1:
                    exps(n // NB)
                yield

        def to_hidden(tile0):
            def outs(tile, bank, t):
                s = tile0 + tile
                hi, lo = hid[s]
                r = split(hi, lo, bank[:, :], t, hid_free[s])
                hs[s] = (hi, lo, r)
                return r
            return outs

        hs = [None] * KD

        def out_project(w, take, order=None, finish=None):
            nxt = stream([(w, m * P) for m in range(KD)], hs)
            nxt.start(order)
            drain()
            if finish:
                finish()
            for m in range(KD):
                bank, t = nxt()
                psum.give(bank, take(m, bank, t, True, True))
            for s in range(KD):
                hid_free[s] = t

        def m_enter():
            return [hid_free[s] for s in range(KD, 16)] + list(m_last)

        def m_leave(*toks):
            for s in range(KD, 16):
                hid_free[s] = toks
            m_last[0] = toks

        def conv(acc, src, taps, pad, bias, tok, *free):
            n, f = taps
            order = [pad] + [j for j in range(n) if j != pad]
            t = None
            for j in order:
                s = j - pad
                lo, hi = max(0, -s), min(T, T - s)
                o, i = acc[:, lo:hi], src[:, lo + s:hi + s]
                if t is None:
                    if bias is None:
                        t = dve(ts(o, i, f(j), None, ALU.mult), tok, *free)
                    else:
                        t = dve(ts(o, i, f(j), bias, ALU.mult, ALU.add), tok, *free)
                else:
                    t = dve(stt(o, i, f(j), o, ALU.mult, ALU.add), t)
                yield t

        def run_all(*gens):
            last = [None] * len(gens)
            live = list(range(len(gens)))
            while live:
                for g in list(live):
                    try:
                        last[g] = next(gens[g])
                    except StopIteration:
                        live.remove(g)
            return last

        def mixer1(l):
            hs[:] = [None] * KD
            w = ("w_in", l)
            menter = m_enter()
            yf = y_free[0]
            nxt = stream([(w, i * P) for i in (10, 11, 6, 7, 14, 12, 8, 15, 13, 9, 2, 4, 0, 3, 5, 1)], xs)
            nxt.start()
            z = lambda i: nxt()
            extra = [Y[:, i, :] for i in range(4, 8)] + [M1[:, i, :] for i in range(4, 8)]
            lend(extra[:4], yf)
            lend(extra[4:], menter)
            heads = []
            vr = M0[:, 6, :].rearrange("p (b c) -> p b c", b=NB)
            kb, kt = z(10)
            kd_t = rope(kb, kt, 1.0, [(M0[0:64, 4, :], 0, 64), (M0[64:128, 4, :], 0, 64),
                                      (M0[0:64, 5, :], 64, 64), (M0[64:128, 5, :], 64, 64)], menter)
            vb, vt = z(11)
            v_rest = value_rows(vb, vt, vr, None, menter)
            v_t = []

            def query(i):
                qb, qt = z(6 + i)
                q_t = rope(qb, qt, 0.125, [(M0[:, i, :], 0, P)], menter)
                for h in (2 * i, 2 * i + 1):
                    p0 = 64 * (h % 2)
                    g = h // 4
                    heads.append((M0[p0:p0 + 64, i, :], M0[p0:p0 + 64, 4 + g, :],
                                  lambda b, g=g: vr[:, b, 64 * g:64 * g + 64], i, p0, (kd_t, q_t), (v_t, 0)))

            gens, last = [], [None, None]

            def gate(i):
                gb, gt = z(14 + i)
                q, f = tmp.take()
                a = act(func(q[:, :], gb[:, :], ACT.Sigmoid), gt, f)
                psum.give(gb, a)
                ab, at = z(12 + i)
                u = dve(tt(Y[:, i, :], q[:, :], ab[:, :], ALU.mult), a, at, yf)
                psum.give(ab, u)
                tmp.give(q, u)
                gens.append(conv(Y[:, 2 + i, :], Y[:, i, :], (31, lambda j, i=i: vec("cc_conv_w", (l * 31 + j) * 2 + i)), 15,
                                 vec("cc_conv_b", l * 2 + i), u, yf))

            def long_conv():
                while len(gens) < 1:
                    yield
                n = [0, 0]
                while n != [31, 31]:
                    for _ in range(2):
                        for i in range(len(gens)):
                            if n[i] < 31:
                                last[i] = next(gens[i])
                                n[i] += 1
                    yield
                st = Stats(True)
                for i in range(2):
                    st.add(Y[:, 2 + i, :], last[i])
                yield
                (rb, rt), (mb, mt) = yield from st.finish_steps(2 * P, LN_EPS)
                yield
                for m in range(2):
                    ap = Y[:, 2 + m, :]
                    t = dve(tt(ap, ap, rb[:, :], ALU.mult), rt, last[m])
                    t = dve(tt(ap, ap, mb[:, :], ALU.subtract), t, mt)
                    q, f = tmp.take()
                    a = act(func(q[:, :], ap, ACT.Silu, bias=vec("cc_ln_b", l * 2 + m), scale=vec("cc_ln_g", l * 2 + m)), t, f)
                    r = split(*hid[6 + m], q[:, :], a, hid_free[6 + m])
                    hs[6 + m] = hid[6 + m] + (r,)
                    tmp.give(q, r)
                    y_free[0] = r
                    yield
                psum.give(rb, t)
                psum.give(mb, t)

            def short(i):
                cb, ct = z(2 + i)
                q, f = tmp.take()
                a = act(copy(q[:, :], cb[:, :]), ct, f)
                psum.give(cb, a)
                hb, ht = z(4 + i)
                p = dve(tt(M1[:, i, :], q[:, :], hb[:, :], ALU.mult), a, ht, menter)
                psum.give(hb, p)
                tmp.give(q, p)
                c, = run_all(conv(M1[:, 2 + i, :], M1[:, i, :],
                                  (3, lambda j, i=i: vec("sc_conv_w", (l * 3 + j) * 2 + i)), 1, None, p))
                bb, bt = z(i)
                x_used(bt)
                q, f = tmp.take()
                y = dve(tt(q[:, :], M1[:, 2 + i, :], bb[:, :], ALU.mult), c, bt, f)
                psum.give(bb, y)
                r = split(*hid[i], q[:, :], y, hid_free[i])
                hs[i] = hid[i] + (r,)
                tmp.give(q, r)
                return r

            done = [None]

            def both():
                live = [attention(heads, 8, lambda b: (max(b - 1, 0), 3 - (b == 0) - (b == 3), P if b == 0 else 0), M1m,
                                  lambda h: CT[:, C_SINK + l * 8 + h:C_SINK + l * 8 + h + 1], to_hidden(2), done, True),
                        long_conv(), center()]
                while live:
                    for g in list(live):
                        try:
                            next(g)
                        except StopIteration:
                            live.remove(g)
                    yield

            query(0)
            fill_with(both(), EVERY1, DELAY1)
            query(1)
            v_t.append(v_rest())
            gate(0)
            query(2)
            gate(1)
            query(3)
            short(0)
            r = short(1)

            def finish():
                toks = reclaim(extra)
                y_free[0] = [y_free[0], toks]
                mask_last[0] = ("dve", cnt["dve"])
                m_leave(done[0], r, *toks)

            out_project(("w_out", l), add_residual, [0, 1, 6, 7, 2, 3, 4, 5], finish)

        def log1p(e_, out, n, w, tok):
            zt, f1 = tmp.take()
            z2, f2 = tmp.take()
            z, zz = zt[0:n, 0:w], z2[0:n, 0:w]
            t = dve(ts(z, e_, 2.0, None, ALU.add), tok, f1)
            t = dve(lambda v: v.reciprocal(z, z), t)
            t = dve(tt(z, z, e_, ALU.mult), t)
            t = dve(tt(zz, z, z, ALU.mult), t, f2)
            t = dve(ts(out, zz, 2.0 / 17, 2.0 / 15, ALU.mult, ALU.add), t)
            for k in (13, 11, 9, 7, 5, 3, 1):
                t = dve(tt(out, out, zz, ALU.mult), t)
                t = dve(ts(out, out, 2.0 / k, None, ALU.add), t)
            t = dve(tt(out, out, z, ALU.mult), t)
            tmp.give(zt, t)
            tmp.give(z2, t)
            return t

        def mixer2():
            hs[:] = [None] * KD
            w = ("ev_w_in_2", 0)
            menter = m_enter()
            yf = y_free[0]
            cols = [2048]
            for h in range(4):
                cols += [2056 + h * P, 2568 + h * P, h * P, 512 + h * P, 1024 + h * P, 1536 + h * P]
            nxt = stream([(w, c) for c in cols], xs)
            nxt.start()
            rr, rrt = pre_scale()
            z = lambda c0: nxt()
            gb, gt = z(2048)
            G, f = tmp.take()
            t = dve(tt(G[0:8, :], gb[0:8, :], rr[0:8, :], ALU.mult), gt, f, rrt)
            psum.give(gb, t)
            t = dve(ts(G[0:8, :], G[0:8, :], VT[0:8, V_BI:V_BI + 1], None, ALU.add), t)
            W_, wf = tmp.take()
            cb, cf = psum.take()
            gates = {"t": t}

            def gate_columns():
                for b in range(NB):
                    t = op("pe", lambda e, b=b: e.transpose(cb[:, 8 * b:8 * b + 8], G[0:8, b * P:(b + 1) * P],
                                                            CT[0:8, C_ID:C_ID + 8]), gates["t"], cf)
                t = dve(vcopy(W_[:, 0:32], cb[:, 0:32]), t, wf)
                f_ = W_[:, 0:32].rearrange("p (b g) -> p b g", g=8)[:, :, 4:8]
                v = lambda i: W_[:, 32 + 16 * i:48 + 16 * i]
                v3 = lambda i: v(i).rearrange("p (b g) -> p b g", g=4)
                t = dve(stt(v3(0), f_, -1.0, f_, ALU.mult, ALU.max), t)
                t = act(func(v(0), v(0), ACT.Exp, scale=-1.0), t)
                t = log1p(v(0), v(1), P, 16, t)
                gates["lf"] = dve(stt(v3(2), f_, 0.0, v3(1), ALU.min, ALU.subtract), t)

            FP, f1 = tmp.take()
            E_, f2 = tmp.take()
            L_, f3 = tmp.take()
            acol = sm[:, 96:112]
            ecol = W_[:, 128:144]

            def gate_rows():
                lf = W_[:, 64:80]
                for b in range(NB):
                    t = op("pe", lambda e, b=b: e.transpose(cb[0:4, b * P:(b + 1) * P], lf[:, 4 * b:4 * b + 4], ident),
                           gates["lf"])
                o1 = dve(lambda e: e.memset(E_[0:4, :], 1.0), f2)
                t = dve(lambda e: e.tensor_tensor_scan(FP[0:4, :], E_[0:4, :], cb[0:4, :], 0.0, ALU.mult, ALU.add),
                        o1, t, f1)
                psum.give(cb, t)
                ta = dve(tt(G[0:4, :], G[0:4, :], FP[0:4, :], ALU.subtract), t)
                gates["M"] = tm = dve(lambda e: e.tensor_tensor_scan(E_[0:4, :], G[0:4, :], G[0:4, :], 0.0, ALU.max,
                                                                     ALU.max), ta)
                t = dve(tt(L_[0:4, :], FP[0:4, :], E_[0:4, :], ALU.add), tm, f3)
                tmp.give(FP, t)
                gates["a"] = ta
                gates["e"] = act(func(L_[0:4, :], L_[0:4, :], ACT.Exp, scale=-1.0), t)

            def gate_cols():
                ab, af = psum.take()
                for o, src, tok in ((0, G, gates["a"]), (16, L_, gates["e"])):
                    for b in range(NB):
                        t = op("pe", lambda e, b=b, o=o, src=src: e.transpose(
                            ab[:, o + 4 * b:o + 4 * b + 4], src[0:4, b * P:(b + 1) * P], CT[0:4, C_ID:C_ID + 4]), tok, af)
                tmp.give(G, t)
                tmp.give(L_, t)
                t = dve(vcopy(acol, ab[:, 0:16]), t)
                gates["col"] = dve(vcopy(ecol, ab[:, 16:32]), t)
                psum.give(ab, gates["col"])

            rw, rf = tmp.take()
            rwa = dma("rga", rw[:, :].rearrange("p (n c) -> p n c", n=4), d["ev_rg_wa_2"][0].rearrange("n p c -> p n c"), rf)
            rx, rf = tmp.take()
            rwx = dma("rgb", rx[:, :].rearrange("p (n c) -> p n c", n=4), d["ev_rg_wx_2"][0].rearrange("n p c -> p n c"), rf)
            lam = VT[:, V_OFF["ev_rg_lambda_2"]:V_OFF["ev_rg_lambda_2"] + 4]
            s1, f = tmp.take()
            t = dve(stt(s1[:, 0:4], lam, -1.0, lam, ALU.mult, ALU.max), f)
            t = act(func(s1[:, 0:4], s1[:, 0:4], ACT.Exp, scale=-1.0), t)
            t = log1p(s1[:, 0:4], s1[:, 8:12], P, 4, t)
            t = dve(ts(s1[:, 16:20], lam, -1.0, 0.0, ALU.mult, ALU.max), t)
            t = dve(tt(s1[:, 8:12], s1[:, 8:12], s1[:, 16:20], ALU.add), t)
            tcs = dve(ts(sm[:, 112:116], s1[:, 8:12], 8.0, None, ALU.mult), t)
            tmp.give(s1, tcs)

            qkvo = []

            def lru(n):
                xb_, xt = z(2056 + n * P)
                x_t = dve(tt(Y[:, n, :], xb_[:, :], rr[:, :], ALU.mult), xt, yf, rrt)
                psum.give(xb_, x_t)
                xc, f = tmp.take()
                t, = run_all(conv(xc[:, :], Y[:, n, :], (4, lambda j: vec("ev_conv_w_2", j * 4 + n)), 3,
                                  vec("ev_conv_b_2", n), x_t, f))
                yb_, yt = z(2056 + 512 + n * P)
                g = dve(tt(Y[:, 4 + n, :], yb_[:, :], rr[:, :], ALU.mult), yt, yf, rrt)
                psum.give(yb_, g)
                lru_state[n] = (xc, t, g)
                return yt

            lru_state = {}

            def lru_rest(n):
                xc, t, g = lru_state[n]
                b1, f1 = psum.take()
                b2, f2 = psum.take()
                p1 = op("pe", lambda e: e.matmul(b1[:, :], rw[:, n * P:(n + 1) * P], xc[:, :], start=True, stop=True), t, f1, rwa)
                p2 = op("pe", lambda e: e.matmul(b2[:, :], rx[:, n * P:(n + 1) * P], xc[:, :], start=True, stop=True), t, f2, rwx)
                r_, f1 = tmp.take()
                i_, f2 = tmp.take()
                a1 = act(func(r_[:, :], b1[:, :], ACT.Sigmoid, bias=vec("ev_rg_ba_2", n)), p1, f1)
                a2 = act(func(i_[:, :], b2[:, :], ACT.Sigmoid, bias=vec("ev_rg_bx_2", n)), p2, f2)
                psum.give(b1, a1)
                psum.give(b2, a2)
                yield
                ix = dve(tt(i_[:, :], i_[:, :], xc[:, :], ALU.mult), a2)
                tmp.give(xc, ix)
                yy = dve(ts(r_[:, :], r_[:, :], sm[:, 112 + n:113 + n], None, ALU.mult), a1, tcs)
                yield
                th, f3 = tmp.take()
                at = act(func(th[:, :], r_[:, :], ACT.Tanh), yy, f3)
                ae = act(func(r_[:, :], r_[:, :], ACT.Exp, scale=-1.0), yy, at)
                yield
                dd, f4 = tmp.take()
                t = dve(ts(dd[:, :], th[:, :], 1.0, None, ALU.add), at, f4)
                t = dve(lambda e: e.reciprocal(dd[:, :], dd[:, :]), t)
                yield
                t = dve(stt(dd[:, :], dd[:, :], 2.0, th[:, :], ALU.mult, ALU.mult), t)
                tmp.give(th, t)
                t = act(func(dd[:, :], dd[:, :], ACT.Sqrt), t)
                yield
                t = dve(tt(i_[:, :], i_[:, :], dd[:, :], ALU.mult), t, ix)
                tmp.give(dd, t)
                t = dve(lambda e: e.tensor_tensor_scan(Y[:, n, :], r_[:, :], i_[:, :], 0.0, ALU.mult, ALU.add), t, ae)
                tmp.give(i_, t)
                tmp.give(r_, t)
                yield
                g = act(func(Y[:, 4 + n, :], Y[:, 4 + n, :], ACT.Gelu_apprx_tanh), g)
                q, f = tmp.take()
                t = dve(tt(q[:, :], Y[:, n, :], Y[:, 4 + n, :], ALU.mult), t, g, f)
                r = split(*hid[4 + n], q[:, :], t, hid_free[4 + n])
                hs[4 + n] = hid[4 + n] + (r,)
                tmp.give(q, r)
                y_free[0] = t
                lru_state[n] = (None, p2, g)

            third = [m[:, i, :] for m in (M0, M1) for i in (3, 7)]
            lend(third, menter)
            for h in range(4):
                if h == 3:
                    menter = [menter, reclaim(third)]
                lru(h)
                rest = lru_rest(h)
                if h == 0:
                    gate_columns()
                qb, qt = z(h * P)
                tq = dve(tt(M0[:, h, :], qb[:, :], rr[:, :], ALU.mult), qt, menter, rrt)
                psum.give(qb, tq)
                if h == 0:
                    gate_rows()
                next(rest)
                next(rest)
                kb, kt = z(512 + h * P)
                tk = dve(tt(M0[:, 4 + h, :], kb[:, :], rr[:, :], ALU.mult), kt, menter, rrt)
                psum.give(kb, tk)
                next(rest)
                next(rest)
                vb, vt = z(1024 + h * P)
                v_rest = value_rows(vb, vt, M1[:, h, :].rearrange("p (b c) -> p b c", b=NB), (rr, rrt), menter)
                if h == 0:
                    gate_cols()
                for _ in rest:
                    pass
                ob, ot = z(1536 + h * P)
                to = dve(tt(M1[:, 4 + h, :], ob[:, :], rr[:, :], ALU.mult), ot, menter, rrt)
                psum.give(ob, to)
                to = act(func(M1[:, 4 + h, :], M1[:, 4 + h, :], ACT.Sigmoid), to)
                tv = v_rest()
                qkvo.append((tq, tk, tv, to))
            x_used(ot)
            tmp.give(rr, to)
            tmp.give(rw, lru_state[3][1])
            tmp.give(rx, lru_state[3][1])
            mem = Memory(0, XM[:, 4:8, :], x_free)

            extra = [Y[:, i, :] for i in (0, 1, 4, 5)]
            lend(extra, y_free[0])
            SCL = float(128) ** -0.5
            tM, tcol = gates["M"], gates["col"]
            mbs, exs, ndb = {}, {}, {}

            def weights_of(h, s):
                tq, tk, tv, to = qkvo[h]
                if s == 0:
                    mb, mf = psum.take()
                    mbs[h] = (mb, op("pe", lambda e: e.matmul(mb[:, :], CT[0:4, C_SEL + h * P:C_SEL + (h + 1) * P],
                                                              E_[0:4, :], start=True, stop=True), tM, mf), None)
                mb, tm, g2 = mbs[h]
                t0 = s * P
                w_ = T - t0
                sbk, sf = psum.take()
                tsc = op("pe", lambda e: e.matmul(sbk[:, 0:w_], M0[:, 4 + h, t0:t0 + P], M0[:, h, t0:T], start=True,
                                                  stop=True), tq, tk, sf)
                ex, xf = tmp.take()
                ac = acol[:, 4 * s + h:4 * s + h + 1]
                g0 = dve(stt(ex[:, 0:P], mb[:, t0:t0 + P], -1.0, CAU, ALU.mult, ALU.add), tm, xf, g2)
                g1 = act(func(ex[:, 0:P], ex[:, 0:P], ACT.Exp, bias=ac), g0, tcol)
                g2 = g1
                if w_ > P:
                    g2 = act(func(ex[:, P:w_], mb[:, t0 + P:T], ACT.Exp, bias=ac, scale=-1.0), g0, tcol)
                v = dve(stt(ex[:, 0:w_], sbk[:, 0:w_], SCL, ex[:, 0:w_], ALU.mult, ALU.mult), g1, g2, tsc)
                psum.give(sbk, v)
                mbs[h] = (mb, tm, g2)
                if s == NB - 1:
                    psum.give(mb, g2)
                exs[h, s] = (ex, v)

            def products(h, s):
                tq, tk, tv, to = qkvo[h]
                if s == 0:
                    ndb[h] = psum.take() + psum.take()
                nb_, nf, db_, df = ndb[h]
                t0 = s * P
                ex, v = exs.pop((h, s))
                op("pe", lambda e: e.matmul(nb_[:, t0:T], M1[:, h, t0:t0 + P], ex[:, 0:T - t0], start=s == 0,
                                            stop=s == NB - 1), v, tv, nf)
                for b in range(s, NB):
                    td = op("pe", lambda e, b=b: e.matmul(db_[:, b:b + 1], ex[:, (b - s) * P:(b - s + 1) * P],
                                                          ones[:, 0:1], start=s == 0 and b == 0, stop=s == b,
                                                          skip_group_check=True), v, df)
                tmp.give(ex, td)
                return td

            def finish(h, td):
                to = qkvo[h][3]
                nb_, nf, db_, df = ndb[h]
                c, cf = st_ring.take()
                v = dve(vcopy(c[:, 0:4], db_[:, 0:4]), td, cf)
                psum.give(db_, v)
                v = dve(stt(c[:, 4:8], c[:, 0:4], -1.0, c[:, 0:4], ALU.mult, ALU.max), v)
                v = dve(tt(c[:, 8:12], c[:, 4:8], ecol.rearrange("p (b h) -> p b h", h=4)[:, :, h], ALU.max), v, tcol)
                v = dve(lambda e: e.reciprocal(c[:, 12:16], c[:, 8:12]), v)

                def rest():
                    rb, rf = psum.take()
                    for b in range(NB):
                        p = op("pe", lambda e, b=b: e.matmul(rb[:, b * P:(b + 1) * P],
                                                             c[:, 12 + b:13 + b].to_broadcast([P, P]), ident,
                                                             start=True, stop=True), v, rf)
                    st_ring.give(c, p)
                    dn, f = tmp.take()
                    u = dve(tt(dn[:, :], M1[:, 4 + h, :], rb[:, :], ALU.mult), p, to, f)
                    psum.give(rb, u)
                    u = dve(tt(dn[:, :], dn[:, :], nb_[:, :], ALU.mult), u, td)
                    r = split(*hid[h], dn[:, :], u, hid_free[h])
                    psum.give(nb_, r)
                    hs[h] = hid[h] + (r,)
                    tmp.give(dn, r)
                    return r
                return rest

            def memory_parts():
                yield from mem.normed()
                yield from mem.parts()

            prep = memory_parts()
            MEM2 = {n: (n - 5,) if n < 17 else (2 * n - 22, 2 * n - 21) for n in range(5, 19)}
            jobs = [(h, s) for h in range(4) for s in range(NB)]
            late = []
            SKEW = 3
            for n in range(len(jobs) + SKEW):
                if n < len(jobs):
                    weights_of(*jobs[n])
                if late:
                    r = late.pop()()
                for _ in range(4):
                    next(prep, None)
                for i in MEM2.get(n, ()):
                    mem.unit(i)
                if n >= SKEW:
                    h, s = jobs[n - SKEW]
                    td = products(h, s)
                    if s == NB - 1:
                        late.append(finish(h, td))
            r = late.pop()()
            tmp.give(E_, mbs[3][1])
            tmp.give(W_, r)
            def finish():
                mem.turn()
                m_leave(td, r)
                y_free[0] = [y_free[0], reclaim(extra)]

            return ("ev_w_out_2", 0), mem, [4, 5, 6, 7, 0, 1, 2, 3], finish

        def rope_tables(after, res):
            pi_, f = tmp.take()
            tp = dma("pos", pi_[:, :].bitcast(I32), d["pos"], f)
            an, f1 = tmp.take()
            k_, f2 = tmp.take()
            t = dve(vcopy(an[:, :], pi_[:, :].bitcast(I32)), tp, f1)
            t = dve(ts(an[:, :], an[:, :], CT[:, C_INV:C_INV + 1], None, ALU.mult), t, f2)
            c1, c2, c3 = two_pi_parts()
            big = 12582912.0
            for m in (4096.0, 1.0):
                t = dve(ts(k_[:, :], an[:, :], 1.0 / (2 * math.pi * m), big, ALU.mult, ALU.add), t)
                yield
                t = dve(ts(k_[:, :], k_[:, :], big, None, ALU.subtract), t)
                yield
                for c in (c1, c2, c3):
                    t = dve(stt(an[:, :], k_[:, :], -c * m, an[:, :], ALU.mult, ALU.add), t)
                    yield
            lim = 3.1415925
            t = dve(ts(an[:, :], an[:, :], lim, -lim, ALU.min, ALU.max), t)
            yield
            t1 = dve(stt(k_[:, :], an[:, :], -1.0, an[:, :], ALU.mult, ALU.max), t)
            yield
            t1 = dve(ts(k_[:, :], k_[:, :], -1.0, 0.5 * math.pi, ALU.mult, ALU.add), t1)
            yield
            a1 = act(func(SIN, an[:, :], ACT.Sin), t, after)
            a2 = act(func(COS, k_[:, :], ACT.Sin), t1, after)
            for q in (0, 2):
                t = dve(ts(SIN[32 * q:32 * q + 32, :], SIN[32 * q:32 * q + 32, :], -1.0, None, ALU.mult), a1)
                yield
            tmp.give(pi_, t1)
            tmp.give(an, a1)
            tmp.give(k_, a2)
            res.extend([t, a2])

        def two_pi_parts():
            v = 2 * math.pi
            out = []
            for _ in range(2):
                e = math.floor(math.log2(v))
                c = math.floor(v / 2.0 ** (e - 9)) * 2.0 ** (e - 9)
                out.append(c)
                v -= c
            return out + [v]

        rope_last = [()]
        table_toks = []

        def swa():
            hs[:] = [None] * KD
            w = ("od_w_qkv_2", 0)
            menter = m_enter()
            yf = y_free[0]
            nxt = stream([(w, i * P) for i in (8, 10, 0, 9, 1, 2, 11, 3, 4, 5, 6, 7)], xs)
            nxt.start()
            rr, rrt = pre_scale()
            for _ in tables[0]:
                pass
            tab = table_toks
            t1 = dve(tt(SIN, SIN, rr[:, :], ALU.mult), tab, rrt)
            t2 = dve(tt(COS, COS, rr[:, :], ALU.mult), tab, rrt)
            Q["dve"].append((None, [t1, t2], False))
            extra = [Y[:, i, :] for i in range(4, 8)] + [M1[:, i, :] for i in (6, 7)]
            lend(extra[:4], yf)
            lend(extra[4:], menter)
            mem = Memory(1, Y[:, 0:4, :], yf)
            z = lambda i: nxt()
            kts, vts, heads = [], [], []

            def key(i):
                kb, kt = z(8 + i)
                kts.append(rope(kb, kt, 1.0, [(M1[0:64, 2 * i, :], 0, 64), (M1[64:128, 2 * i, :], 0, 64),
                                              (M1[0:64, 2 * i + 1, :], 64, 64), (M1[64:128, 2 * i + 1, :], 64, 64)],
                                menter))

            def val(i):
                vb, vt = z(10 + i)
                return value_rows(vb, vt, M1[:, 4 + i, :].rearrange("p (b c) -> p b c", b=NB), (rr, rrt), menter)

            def query(i):
                qb, qt = z(i)
                x_used(qt)
                tq = rope(qb, qt, 0.125, [(M0[:, i, :], 0, P)], menter)
                for h in (2 * i, 2 * i + 1):
                    p0 = 64 * (h % 2)
                    g = h // 4
                    vr = M1[:, 4 + g // 2, :].rearrange("p (b c) -> p b c", b=NB)
                    heads.append((M0[p0:p0 + 64, i, :], M1[p0:p0 + 64, g, :],
                                  lambda b, g=g, vr=vr: vr[:, b, 64 * (g % 2):64 * (g % 2) + 64], i, p0,
                                  (kts[g // 2], tq), (vts, g // 2)))

            done = [None]
            key(0)
            v_rest = val(0)
            query(0)
            fill_with(attention(heads, 16, lambda b: (max(b - 1, 0), 2 - (b == 0), P if b == 0 else 0), M2m,
                                lambda h: CT[:, C_SINK + 16 + h:C_SINK + 17 + h], to_hidden(0), done), EVERY2, DELAY2)
            key(1)
            vts.append(v_rest())
            query(1)
            query(2)
            v_rest = val(1)
            query(3)
            vts.append(v_rest())
            tmp.give(rr, vts[1])
            for i in range(4, 8):
                query(i)
                if i == 4:
                    for _ in mem.normed():
                        pass
            for _ in mem.parts():
                next(filler[0], None)
            for i in range(16):
                mem.unit(i)

            def finish():
                mem.turn()
                toks = reclaim(extra)
                y_free[0] = [y_free[0], toks, mem.raw_done]
                m_leave(done[0], *toks)

            return ("od_w_o_2", 0), mem, None, finish

        MR = CT[:, C_M1 + P:C_M1 + 3 * P]
        mr_tok = [None]
        mask_last = [()]

        def memory_rms():
            raw = Y[:, 0:4, :]
            t = dma("mm", raw.rearrange("p a (b t) -> p (a b) t", b=2),
                    d["memT"].rearrange("(k p) t -> p k t", p=P), y_free[0])
            st = Stats(False)
            for i in range(4):
                st.add(raw[:, i, :], t)
                yield
            y_free[0] = st.tail[3]
            st.fold("dve")
            st.tail = None
            st.t2 = dve(tt(st.s2[:, 0:256], st.s2[:, 0:256], st.s2[:, 256:512], ALU.add), st.t2)
            yield
            (rb, rt), = yield from st.finish_steps(D, RMS_EPS, 2)
            mr_tok[0] = dve(vcopy(MR, rb[:, 0:256]), rt, mask_last[0])
            psum.give(rb, mr_tok[0])

        class Memory:

            def __init__(self, l, raw, *free):
                self.l, self.w = l, ("w_xkv_2", l)
                self.raw = raw
                flat_raw = raw.rearrange("p a (b t) -> p (a b) t", b=2)
                self.k = lambda k: flat_raw[:, k, :]
                self.t = dma("mm", flat_raw, d["memT"].rearrange("(k p) t -> p k t", p=P), *free)
                self.ms, self.kt, self.vt, self.pend = [], [], [], None
                self.mh = XL[:, 0:4, :].rearrange("p a (b t) -> p (a b) t", b=2)
                self.ml = XL[:, 4:8, :].rearrange("p a (b t) -> p (a b) t", b=2)

            def normed(self):
                s = []
                for k in range(KD):
                    o = self.k(k)
                    s.append(dve(stt(o, o, vec("g_mem_2", self.l * KD + k), MR, ALU.mult, ALU.mult), mr_tok[0], self.t))
                    yield
                self.s = s

            def parts(self):
                pend = None
                for k in range(KD + 1):
                    if k < KD:
                        h = act(copy(self.mh[:, k, :], self.k(k)), self.s[k], x_free)
                    if pend is not None:
                        j, hj = pend
                        c = dve(tt(self.ml[:, j, :], self.k(j), f32(self.mh[:, j, :]), ALU.subtract), hj)
                        self.ms.append((self.mh[:, j, :], self.ml[:, j, :], c))
                    pend = (k, h)
                    yield
                self.raw_done = c

            def unit(self, i):
                m = i % KD
                if i < KD:
                    bank, t = project(self.w, m * P, self.ms)
                    out = XM[:, m // 2, 256 * (m % 2):256 * (m % 2) + 256]
                    self.kt.append(act(copy(out, bank[:, 0:256]), t, x_free))
                    psum.give(bank, self.kt[-1])
                    return
                bank, t = project(self.w, D + m * P, self.ms)
                q, f = tmp.take()
                c = act(copy(q[:, 0:256], bank[:, 0:256]), t, f)
                psum.give(bank, c)
                self.last = t
                self.turn()
                self.pend = (m, q, c)

            def turn(self):
                if self.pend is None:
                    return
                m, q, c = self.pend
                self.pend = None
                bank, free = psum.take()
                for b in range(2):
                    t = op("pe", lambda e, b=b: e.transpose(bank[:, b * P:(b + 1) * P], q[:, b * P:(b + 1) * P], ident),
                           c, free)
                tmp.give(q, t)
                out = XM[:, 4:8, :].rearrange("p (m a) t -> p m (a t)", m=2)[:, :, m * P:(m + 1) * P]
                self.vt.append(act(copy(out, bank[:, 0:256].rearrange("p (b c) -> p b c", b=2)), t, x_free,
                                   self.raw_done))
                psum.give(bank, self.vt[-1])

            def move(self):
                self.turn()
                menter = m_enter()
                self.moved = []
                for a in range(KD):
                    toks = self.kt[2 * a:2 * a + 2] if a < 4 else self.vt
                    self.moved.append(pool(vcopy(M1[:, a, :], XM[:, a, :]), toks, menter))
                x_used([self.last, self.moved[-1]])

        def cross(l, mem):
            KT = M1[:, 0:4, :].rearrange("p a (b t) -> p (a b) t", b=2)
            VR = M1[:, 4:8, :].rearrange("p (m a) t -> p m (a t)", m=2)
            kt = [mem.moved[m // 2] for m in range(KD)]
            vt = [mem.moved[KD - 1]] * KD
            hs[:] = [None] * KD
            menter = m_enter()
            tq = []
            nxt = stream([(("w_xq_2", l), m * P) for m in range(KD)], xs)
            nxt.start()
            rr, rrt = pre_scale()
            extra = [Y[:, i, :] for i in (2, 3, 6, 7)]
            lend(extra, y_free[0])
            S, C = {}, {}
            pt_free = [y_free[0], y_free[0]]
            pts = {}
            SC = 1.0 / 16

            def score(h, b):
                if b == 0:
                    C[h] = sm_ring.take()
                c, cf = C[h]
                bank, f = psum.take()
                for i in range(2):
                    t = op("pe", lambda e, i=i: e.matmul(bank[:, 0:256], M0[:, 2 * h + i, b * P:(b + 1) * P],
                                                         KT[:, 2 * h + i, :], start=i == 0, stop=i == 1),
                           f, tq[2 * h + i], kt[2 * h + i])
                s, sf = tmp.take()
                r = dve(lambda e: e.tensor_reduce(c[:, b:b + 1], bank[:, 0:256], AX, ALU.max), t, cf)
                r = dve(ts(c[:, 4 + b:5 + b], c[:, b:b + 1], -SC, None, ALU.mult), r)
                x = act(lambda e: e.activation(s[:, 0:256], bank[:, 0:256], ACT.Exp, bias=c[:, 4 + b:5 + b], scale=SC,
                                               accum_out=c[:, 8 + b:9 + b]), r, sf)
                psum.give(bank, x)
                S[h, b] = (s, x)

            def norm(h, b):
                c, cf = C[h]
                if b == 0:
                    S[h] = dve(lambda e: e.reciprocal(c[:, 12:16], c[:, 8:12]), S[h, NB - 1][1])
                s, x = S[h, b]
                n = dve(ts(s[:, 0:256], s[:, 0:256], c[:, 12 + b:13 + b], None, ALU.mult), S[h])
                if b == NB - 1:
                    sm_ring.give(c, n)
                S[h, b] = (s, n)

            def turn(h, b):
                s, n = S.pop((h, b))
                bank, f = psum.take()
                for i in range(2):
                    t = op("pe", lambda e, i=i: e.transpose(bank[:, i * P:(i + 1) * P], s[:, i * P:(i + 1) * P], ident),
                           n, f)
                tmp.give(s, t)
                o = 4 * (h % 2)
                cp = act(copy(Y[:, o:o + 2, b * P:(b + 1) * P], bank[:, 0:256].rearrange("p (i q) -> p i q", i=2)), t,
                         pt_free[h % 2])
                psum.give(bank, cp)
                pts[h] = cp

            def value(h):
                o = 4 * (h % 2)
                for j in range(2):
                    bank, f = psum.take()
                    for i in range(2):
                        t = op("pe", lambda e, i=i, j=j, bank=bank: e.matmul(
                            bank[:, :], VR[:, i, (2 * h + j) * P:(2 * h + j + 1) * P], Y[:, o + i, :], start=i == 0,
                            stop=i == 1), f, pts[h], vt[2 * h + j])
                    s = 2 * h + j
                    hi, lo = hid[s]
                    r = split(hi, lo, bank[:, :], t, hid_free[s])
                    hs[s] = (hi, lo, r)
                    psum.give(bank, r)
                pt_free[h % 2] = t
                return t

            last = [None]

            def steps():
                for n in range(4 * NB + 7):
                    while n < 4 * NB and len(tq) < 2 * (n // NB) + 2:
                        yield
                    if 0 <= n - 5 < 4 * NB:
                        norm(*divmod(n - 5, NB))
                    if n < 4 * NB:
                        score(*divmod(n, NB))
                    if 0 <= n - 6 < 4 * NB:
                        turn(*divmod(n - 6, NB))
                    if n >= 10 and (n - 10) % NB == 0:
                        yield
                        last[0] = value((n - 10) // NB)
                    yield

            for m in range(KD):
                bank, t = nxt()
                tq.append(dve(tt(M0[:, m, :], bank[:, :], rr[:, :], ALU.mult), t, menter, rrt))
                psum.give(bank, tq[-1])
                if m == 1:
                    fill_with(steps(), EVERY3, DELAY3)
            tmp.give(rr, tq[-1])
            x_used(t)

            def finish():
                t = last[0]
                y_free[0] = [t, reclaim(extra)]
                m_leave(t)

            out_project(("w_xo_2", l), to_y, None, finish)

        def first_ffn(l, n, ln):
            ffn((f"ffn{n}_w_gu", l), (f"ffn{n}_w_down", l), FF1 // P, True, add_residual,
                memory_rms() if (l, n) == (1, 2) else None)
            block_norm(l, ln, ("g_mix_pre_2", 0) if (l, n) == (1, 2) else None)

        def first_mixer(l):
            mixer1(l)
            block_norm(l, "ln2")

        def second_mixer(l):
            if l == 0:
                rope_last[0] = ("dve", cnt["dve"])
            w, mem, order, finish = mixer2() if l == 0 else swa()

            def leave():
                finish()
                mem.move()

            out_project(w, to_y, order, leave)
            post_norm("g_mix_post_2", l, ystats[0], ("g_x_pre_2", l))
            cross(l, mem)
            post_norm("g_x_post_2", l, ystats[0], ("g_ff_pre_2", l))

        def second_ffn(l):
            if l == 0:
                tables[0] = rope_tables(rope_last[0], table_toks)
            ffn(("w_ff1_2", l), ("w_ff2_2", l), FF2 // P, False, to_y)
            post_norm("g_ff_post_2", l, ystats[0], ("g_mix_pre_2", 1) if l == 0 else None)

        steps = []
        for l in range(2):
            steps += [lambda l=l: first_ffn(l, 1, "ln1"), lambda l=l: first_mixer(l), lambda l=l: first_ffn(l, 2, "ln3")]
        for l in range(2):
            steps += [lambda l=l: second_mixer(l), lambda l=l: second_ffn(l)]
        for step in steps:
            step()
        oT = d["outT"].rearrange("(k p) t -> p k t", p=P)
        for m in range(KD):
            last = dma("out", oT[:, m, :], XR[:, m, :], xr_tok[m])
        Q["sp"].append((None, [last], False))

        if units_in is None:
            return units

        def emit(name, eng):
            seen = {}
            for fn, waits, inc in Q[name]:
                need = {}
                for s, v in waits:
                    need[s] = max(need.get(s, 0), v)
                for s, v in need.items():
                    if seen.get(s, 0) < v:
                        eng.wait_ge(sems[s], v)
                        seen[s] = v
                if fn is None:
                    continue
                ins = fn(eng)
                if inc:
                    ins.then_inc(sems[name], 1)

        block = es.enter_context(nc.Block())

        @block.sync
        def _(eng):
            emit("sp", eng)

        @block.scalar
        def _(eng):
            emit("act", eng)

        @block.vector
        def _(eng):
            emit("dve", eng)

        @block.gpsimd
        def _(eng):
            emit("pool", eng)

        @block.tensor
        def _(eng):
            emit("pe", eng)


def constants():
    c = np.zeros((P, C_W), np.float32)
    p = np.arange(P)
    c[:, C_ID:C_ID + P] = np.eye(P)
    c[:, C_ONE:C_ONE + P] = 1.0
    half = 32
    inv = np.power(np.float32(10000.0), -np.arange(half, dtype=np.float32) / np.float32(half)).astype(np.float32)
    ang = (np.arange(T, dtype=np.float32)[None, :] * inv[p % 32][:, None]).astype(np.float32).astype(np.float64)
    sign = np.where((p // 32) % 2 == 0, -1.0, 1.0)[:, None]
    c[:, C_COS:C_COS + T] = np.cos(ang)
    c[:, C_SIN:C_SIN + T] = np.sin(ang) * sign
    r, k = p[:, None], np.arange(P)[None, :]
    c[:, C_M1:C_M1 + P] = np.where(k >= r, 0.0, NEG)
    c[:, C_M1 + 2 * P:C_M1 + 3 * P] = np.where(k <= r, 0.0, NEG)
    c[:, C_M2:C_M2 + P] = np.where(k > r, 0.0, NEG)
    c[:, C_M2 + P:C_M2 + 2 * P] = np.where(k <= r, 0.0, NEG)
    for h in range(4):
        c[h, C_SEL + h * P:C_SEL + (h + 1) * P] = 1.0
    c[:, C_INV] = inv[p % 32]
    c[:, C_EPS] = LN_EPS
    c[:, C_EPS + 1] = RMS_EPS
    return c


_WEIGHTS = ["ffn1_w_gu", "ffn1_w_down", "w_in", "w_out", "ffn2_w_gu", "ffn2_w_down", "ev_w_in_2", "ev_rg_wa_2",
            "ev_rg_wx_2", "ev_w_out_2", "od_w_qkv_2", "od_w_o_2", "w_xq_2", "w_xkv_2", "w_xo_2", "w_ff1_2", "w_ff2_2",
            ]


def kernel(**inputs):
    import concourse.bacc as _bacc
    from concourse.bass_utils import run_bass_kernel_spmd as _run

    a = {n: np.ascontiguousarray(v) for n, v in inputs.items()}
    arrays = {n: a[n] for n in _WEIGHTS}
    arrays["xT"] = np.ascontiguousarray(a["x"][0].T)
    arrays["memT"] = np.ascontiguousarray(a["mem_2"][0].T)
    vecs = np.zeros((V_W, P), np.float32)
    for n, s in VEC_SIZES:
        vecs[V_OFF[n]:V_OFF[n] + s] = a[n].reshape(s, P)
    vecs[V_BI, 0:8] = a["ev_b_if_2"][0]
    arrays["vecs"] = np.ascontiguousarray(vecs.T)
    c = constants()
    c[:, C_SINK:C_SINK + 16] = a["attn_sink"].reshape(1, 16)
    c[:, C_SINK + 16:C_SINK + 32] = a["od_sinks_2"].reshape(1, 16)
    arrays["consts"] = c
    arrays["pos"] = np.ascontiguousarray(np.broadcast_to(a["positions_2"].reshape(1, T), (P, T)))

    def make():
        nc = _bacc.Bacc("TRN2", target_bir_lowering=False, num_devices=1)
        d = {}
        for n, v in arrays.items():
            d[n] = nc.dram_tensor(f"in_{n}", v.shape, mybir.dt.from_np(v.dtype), kind="ExternalInput").ap()
        d["outT"] = nc.dram_tensor("outT", (D, T), F32, kind="ExternalOutput").ap()
        return nc, d

    order = build(*make(), None)
    nc, d = make()
    build(nc, d, order)
    r = _run(nc, [{f"in_{n}": v for n, v in arrays.items()}], core_ids=[0])
    return np.ascontiguousarray(r.results[0]["outT"].T)[None]
```
